# Optimizing a Trainium2 kernel written in Bass

```python
import jax, jax.numpy as jnp
from jax import lax
import numpy as np
import jax
import jax.numpy as jnp

D_MODEL = 1024
BATCH = 1
SEQ = 256
DEPTH = 2

D_FF = 2816
FFN_RESID = 0.5
EPS = 1e-6
GM_WIDTH = 512
GM_GROUPS = 4
GM_GROUP_DIM = GM_WIDTH // GM_GROUPS
GM_CHUNK = 128
MLA_HEADS = 8
MLA_Q_RANK = 384
MLA_KV_RANK = 256
MLA_NOPE = 64
MLA_ROPE = 32
MLA_QK_DIM = MLA_NOPE + MLA_ROPE
MLA_V = 64
MLA_WIDTH = MLA_HEADS * MLA_V
ROPE_THETA = 10000.0
Q_BLOCK = 128
SSD_HEADS = 8
SSD_HEAD_DIM = 64
SSD_INNER = SSD_HEADS * SSD_HEAD_DIM
SSD_GROUPS = 2
SSD_STATE = 128
SSD_CONV = 4
SSD_CHUNK = 128
SSD_CONV_DIM = SSD_INNER + 2 * SSD_GROUPS * SSD_STATE
N_BRANCH = 3
BRANCH_WIDTH = 512
IN_WIDTHS = (2 * GM_WIDTH, MLA_Q_RANK, MLA_KV_RANK, MLA_ROPE, SSD_INNER, SSD_CONV_DIM, SSD_HEADS, N_BRANCH * D_MODEL)
IN_COLS = sum(IN_WIDTHS)
IN_OFFSETS = tuple(int(v) for v in np.cumsum(IN_WIDTHS)[:-1])


def rms_norm(x, gain):
    xf = x.astype(jnp.float32)
    y = xf * lax.rsqrt(jnp.mean(xf * xf, axis=-1, keepdims=True) + EPS)
    return (y * gain.astype(jnp.float32)).astype(x.dtype)

def swiglu_ffn(h, w_in, w_out):
    gate, up = jnp.split(h @ w_in, 2, axis=-1)
    return (jax.nn.silu(gate) * up) @ w_out

def apply_rope(x, cos, sin):
    x1, x2 = jnp.split(x, 2, axis=-1)
    return jnp.concatenate([x1 * cos - x2 * sin, x2 * cos + x1 * sin], axis=-1)

def gmlp_mixer(uv, v_gain, w_s, b_s):
    bsz, s, _ = uv.shape
    u, v = jnp.split(jax.nn.gelu(uv, approximate=False), 2, axis=-1)
    v = rms_norm(v, v_gain).reshape(bsz, s // GM_CHUNK, GM_CHUNK, GM_GROUPS, GM_GROUP_DIM)
    causal = jnp.tril(jnp.ones((GM_CHUNK, GM_CHUNK), dtype=bool))
    w = jnp.where(causal[None], w_s, 0.0).astype(v.dtype)
    sp = jnp.einsum('gts,bcsgd->bctgd', w, v) + b_s.T[:, :, None].astype(v.dtype)
    return u * sp.reshape(bsz, s, GM_WIDTH)

def blocked_causal_attention(q, k, v):
    bsz, s, nh, dqk = q.shape
    dv = v.shape[-1]
    nb = s // Q_BLOCK
    scale = dqk ** -0.5
    qb = q.reshape(bsz, nb, Q_BLOCK, nh, dqk).transpose(1, 0, 3, 2, 4)
    kt = k.transpose(0, 2, 1, 3)
    vt = v.transpose(0, 2, 1, 3)
    kpos = jnp.arange(s)

    def one_block(args):
        qi, i = args
        sc = jnp.einsum('bhqd,bhkd->bhqk', qi, kt, preferred_element_type=jnp.float32) * scale
        qpos = i * Q_BLOCK + jnp.arange(Q_BLOCK)
        sc = jnp.where(kpos[None, :] <= qpos[:, None], sc, -jnp.inf)
        p = jax.nn.softmax(sc, axis=-1).astype(vt.dtype)
        return jnp.einsum('bhqk,bhkd->bhqd', p, vt)

    out = lax.map(one_block, (qb, jnp.arange(nb)))
    return out.transpose(1, 0, 3, 2, 4).reshape(bsz, s, nh * dv)

def mla_mixer(c_q, c_kv, k_rope, cos, sin, q_norm, kv_norm, w_uq, w_ukv, q_gain, k_gain):
    bsz, s, _ = c_q.shape
    q = (rms_norm(c_q, q_norm) @ w_uq).reshape(bsz, s, MLA_HEADS, MLA_QK_DIM)
    kv = (rms_norm(c_kv, kv_norm) @ w_ukv).reshape(bsz, s, MLA_HEADS, MLA_NOPE + MLA_V)
    k_nope, v = jnp.split(kv, [MLA_NOPE], axis=-1)
    k_pe = jnp.broadcast_to(k_rope[:, :, None, :], (bsz, s, MLA_HEADS, MLA_ROPE))
    k = jnp.concatenate([k_nope, k_pe], axis=-1)
    q = rms_norm(q, q_gain)
    k = rms_norm(k, k_gain)
    q = jnp.concatenate([q[..., :MLA_NOPE], apply_rope(q[..., MLA_NOPE:], cos, sin)], axis=-1)
    k = jnp.concatenate([k[..., :MLA_NOPE], apply_rope(k[..., MLA_NOPE:], cos, sin)], axis=-1)
    return blocked_causal_attention(q, k, v)

def segsum(a):
    t = a.shape[-1]
    idx = jnp.arange(t)
    ax = jnp.where(idx[:, None] > idx[None, :], a[..., :, None], 0.0)
    ss = jnp.cumsum(ax, axis=-2)
    return jnp.where(idx[:, None] >= idx[None, :], ss, -jnp.inf)

def ssd_scan(xs, dt, a_log, b_in, c_in):
    bsz, s, nh, hp = xs.shape
    ng, ns = b_in.shape[2], b_in.shape[3]
    nr = nh // ng
    nc = s // SSD_CHUNK
    a = -jnp.exp(a_log.astype(jnp.float32))
    da = (dt * a).reshape(bsz, nc, SSD_CHUNK, ng, nr).transpose(0, 3, 4, 1, 2)
    xdt = (xs * dt[..., None].astype(xs.dtype)).reshape(bsz, nc, SSD_CHUNK, ng, nr, hp)
    bc = b_in.reshape(bsz, nc, SSD_CHUNK, ng, ns)
    cc = c_in.reshape(bsz, nc, SSD_CHUNK, ng, ns)
    cs = jnp.cumsum(da, axis=-1)
    dt_ = xs.dtype
    lmat = jnp.exp(segsum(da)).astype(dt_)
    cb = jnp.einsum('bclgn,bcsgn->bgcls', cc, bc)
    y_diag = jnp.einsum('bgrcls,bcsgrp->bclgrp', cb[:, :, None] * lmat, xdt)
    decay_states = jnp.exp(cs[..., -1:] - cs).astype(dt_)
    states = jnp.einsum('bclgn,bgrcl,bclgrp->bcgrpn', bc, decay_states, xdt)
    chunk_tot = jnp.pad(cs[..., -1], ((0, 0), (0, 0), (0, 0), (1, 0)))
    decay_chunk = jnp.exp(segsum(chunk_tot)).astype(dt_)
    states0 = jnp.concatenate([jnp.zeros_like(states[:, :1]), states], axis=1)
    new_states = jnp.einsum('bgrzc,bcgrpn->bzgrpn', decay_chunk, states0)
    states_in = new_states[:, :-1]
    y_off = jnp.einsum('bclgn,bcgrpn,bgrcl->bclgrp', cc, states_in, jnp.exp(cs).astype(dt_))
    return (y_diag + y_off).reshape(bsz, s, nh, hp)

def ssd_mixer(z, xbc, dt_raw, conv_w, conv_b, dt_bias, a_log, d_skip, norm_gain):
    bsz, s, _ = xbc.shape
    xbc = lax.conv_general_dilated(xbc, conv_w[:, None, :].astype(xbc.dtype), (1,), [(SSD_CONV - 1, 0)],
                                   dimension_numbers=('NWC', 'WIO', 'NWC'), feature_group_count=SSD_CONV_DIM)
    xbc = jax.nn.silu(xbc + conv_b.astype(xbc.dtype))
    xs, b_in, c_in = jnp.split(xbc, [SSD_INNER, SSD_INNER + SSD_GROUPS * SSD_STATE], axis=-1)
    xs = xs.reshape(bsz, s, SSD_HEADS, SSD_HEAD_DIM)
    b_in = b_in.reshape(bsz, s, SSD_GROUPS, SSD_STATE)
    c_in = c_in.reshape(bsz, s, SSD_GROUPS, SSD_STATE)
    dt = jax.nn.softplus(dt_raw.astype(jnp.float32) + dt_bias.astype(jnp.float32))
    y = ssd_scan(xs, dt, a_log, b_in, c_in) + xs * d_skip[:, None].astype(xs.dtype)
    y = y.reshape(bsz, s, SSD_INNER) * jax.nn.silu(z)
    y = rms_norm(y.reshape(bsz, s, SSD_GROUPS, SSD_INNER // SSD_GROUPS), norm_gain.reshape(SSD_GROUPS, -1))
    return y.reshape(bsz, s, SSD_INNER)

def first_inputs(seed: int = 0) -> dict:
    key = jax.random.key(seed)
    ks = jax.random.split(key, 32)
    f32 = jnp.float32

    def nrm(k, shape, scale):
        return jax.random.normal(k, shape, f32) * scale

    def gain(k, shape):
        return 1.0 + 0.05 * jax.random.normal(k, shape, f32)

    L = DEPTH
    x = jax.random.normal(ks[0], (BATCH, SEQ, D_MODEL), f32)
    offsets = jax.random.randint(ks[1], (BATCH, 1), 0, SEQ, dtype=jnp.int32)
    positions = offsets + jnp.arange(SEQ, dtype=jnp.int32)[None, :]
    dt0 = jnp.exp(jax.random.uniform(ks[2], (L, SSD_HEADS), f32, np.log(1e-3), np.log(1e-1)))
    return {
        'x': x,
        'positions': positions,
        'ffn1_norm': gain(ks[3], (L, D_MODEL)),
        'ffn1_w_in': nrm(ks[4], (L, D_MODEL, 2 * D_FF), D_MODEL ** -0.5),
        'ffn1_w_out': nrm(ks[5], (L, D_FF, D_MODEL), D_FF ** -0.5),
        'mix_norm': gain(ks[6], (L, D_MODEL)),
        'w_in': nrm(ks[7], (L, D_MODEL, IN_COLS), D_MODEL ** -0.5),
        'gm_v_norm': gain(ks[8], (L, GM_WIDTH)),
        'gm_w_s': nrm(ks[9], (L, GM_GROUPS, GM_CHUNK, GM_CHUNK), 0.5 * GM_CHUNK ** -0.5),
        'gm_b_s': 1.0 + 0.1 * jax.random.normal(ks[10], (L, GM_GROUPS, GM_CHUNK), f32),
        'mla_q_norm': gain(ks[11], (L, MLA_Q_RANK)),
        'mla_kv_norm': gain(ks[12], (L, MLA_KV_RANK)),
        'mla_w_uq': nrm(ks[13], (L, MLA_Q_RANK, MLA_HEADS * MLA_QK_DIM), MLA_Q_RANK ** -0.5),
        'mla_w_ukv': nrm(ks[14], (L, MLA_KV_RANK, MLA_HEADS * (MLA_NOPE + MLA_V)), MLA_KV_RANK ** -0.5),
        'mla_q_gain': gain(ks[15], (L, MLA_QK_DIM)),
        'mla_k_gain': gain(ks[16], (L, MLA_QK_DIM)),
        'ssd_conv_w': nrm(ks[17], (L, SSD_CONV, SSD_CONV_DIM), SSD_CONV ** -0.5),
        'ssd_conv_b': nrm(ks[18], (L, SSD_CONV_DIM), 0.02),
        'ssd_dt_bias': dt0 + jnp.log(-jnp.expm1(-dt0)),
        'ssd_a_log': jnp.log(jax.random.uniform(ks[19], (L, SSD_HEADS), f32, 1.0, 16.0)),
        'ssd_d': 1.0 + 0.1 * jax.random.normal(ks[20], (L, SSD_HEADS), f32),
        'ssd_norm': gain(ks[21], (L, SSD_INNER)),
        'w_branch': nrm(ks[22], (L, N_BRANCH, BRANCH_WIDTH, D_MODEL), BRANCH_WIDTH ** -0.5),
        'w_out': nrm(ks[23], (L, D_MODEL, D_MODEL), D_MODEL ** -0.5),
        'ffn2_norm': gain(ks[24], (L, D_MODEL)),
        'ffn2_w_in': nrm(ks[25], (L, D_MODEL, 2 * D_FF), D_MODEL ** -0.5),
        'ffn2_w_out': nrm(ks[26], (L, D_FF, D_MODEL), D_FF ** -0.5),
    }

def first_block(x, positions, ffn1_norm, ffn1_w_in, ffn1_w_out, mix_norm, w_in, gm_v_norm, gm_w_s, gm_b_s,
              mla_q_norm, mla_kv_norm, mla_w_uq, mla_w_ukv, mla_q_gain, mla_k_gain,
              ssd_conv_w, ssd_conv_b, ssd_dt_bias, ssd_a_log, ssd_d, ssd_norm,
              w_branch, w_out, ffn2_norm, ffn2_w_in, ffn2_w_out):
    bsz, s, _ = x.shape
    inv_freq = 1.0 / (ROPE_THETA ** (jnp.arange(0, MLA_ROPE, 2, dtype=jnp.float32) / MLA_ROPE))
    ang = positions.astype(jnp.float32)[..., None] * inv_freq
    cos = jnp.cos(ang)[:, :, None, :].astype(x.dtype)
    sin = jnp.sin(ang)[:, :, None, :].astype(x.dtype)
    for l in range(DEPTH):
        x = x + FFN_RESID * swiglu_ffn(rms_norm(x, ffn1_norm[l]), ffn1_w_in[l], ffn1_w_out[l])
        h = rms_norm(x, mix_norm[l])
        uv, c_q, c_kv, k_rope, z, xbc, dt_raw, gates = jnp.split(h @ w_in[l], IN_OFFSETS, axis=-1)
        y_a = gmlp_mixer(uv, gm_v_norm[l], gm_w_s[l], gm_b_s[l])
        y_b = mla_mixer(c_q, c_kv, k_rope, cos, sin, mla_q_norm[l], mla_kv_norm[l], mla_w_uq[l], mla_w_ukv[l],
                        mla_q_gain[l], mla_k_gain[l])
        y_c = ssd_mixer(z, xbc, dt_raw, ssd_conv_w[l], ssd_conv_b[l], ssd_dt_bias[l], ssd_a_log[l], ssd_d[l],
                        ssd_norm[l])
        g = jax.nn.sigmoid(gates).reshape(bsz, s, N_BRANCH, D_MODEL)
        merged = (g[:, :, 0] * (y_a @ w_branch[l, 0])
                  + g[:, :, 1] * (y_b @ w_branch[l, 1])
                  + g[:, :, 2] * (y_c @ w_branch[l, 2]))
        x = x + merged @ w_out[l]
        x = x + FFN_RESID * swiglu_ffn(rms_norm(x, ffn2_norm[l]), ffn2_w_in[l], ffn2_w_out[l])
    return x


GRID_W = 64
CTX_LEN = 256
N_MIXERS = 4
MIX_RET, MIX_NAT, MIX_POOL, MIX_SWA = 0, 1, 2, 3
N_RET = len(range(MIX_RET, DEPTH, N_MIXERS))
N_NAT = len(range(MIX_NAT, DEPTH, N_MIXERS))
N_POOL = len(range(MIX_POOL, DEPTH, N_MIXERS))
N_SWA = len(range(MIX_SWA, DEPTH, N_MIXERS))
NEG_INF = -1e30
ROPE_BASE = 10000.0
FFN_HIDDEN = 2816
RET_HEADS = 4
RET_QK_DIM = D_MODEL // RET_HEADS
RET_V_DIM = 2 * RET_QK_DIM
RET_CHUNK = 128
NAT_HEADS = 16
NAT_HEAD_DIM = D_MODEL // NAT_HEADS
NAT_KH = 8
NAT_KW = 16
POOL_WINDOWS = (2, 4, 8, 16)
POOL_GROUPS = len(POOL_WINDOWS)
POOL_GROUP_DIM = D_MODEL // POOL_GROUPS
SWA_Q_HEADS = 16
SWA_KV_HEADS = 4
SWA_HEAD_DIM = D_MODEL // SWA_Q_HEADS
SWA_WINDOW = 128
SWA_BLOCK = 128


def rms_norm_2(x, g):
    xf = x.astype(jnp.float32)
    y = xf * lax.rsqrt(jnp.mean(xf * xf, axis=-1, keepdims=True) + EPS)
    return (y * g.astype(jnp.float32)).astype(x.dtype)

def ada_in(h, g, m, j):
    xn = rms_norm_2(h, g)
    return (xn * (1.0 + m[:, j, 1][:, None]) + m[:, j, 0][:, None]).astype(h.dtype)

def gated_residual(h, m, j, y, w):
    return h + (w * m[:, j, 2][:, None] * y).astype(h.dtype)

def swiglu(x, w_in, w_out):
    a, b = jnp.split(x @ w_in, 2, axis=-1)
    return (jax.nn.silu(a) * b) @ w_out

def rope_angles(positions, dim):
    seg = dim // len(positions)
    inv = ROPE_BASE ** (-jnp.arange(0, seg, 2, dtype=jnp.float32) / seg)
    return jnp.concatenate([jnp.tile(p.astype(jnp.float32)[:, None] * inv, (1, 2)) for p in positions], axis=-1)

def apply_rope_2(x, ang, n_axes):
    xf = x.astype(jnp.float32)
    segs = jnp.split(xf, 2 * n_axes, axis=-1)
    rot = jnp.concatenate([s for a in range(n_axes) for s in (-segs[2 * a + 1], segs[2 * a])], axis=-1)
    return (xf * jnp.cos(ang)[None, :, None] + rot * jnp.sin(ang)[None, :, None]).astype(x.dtype)

def retention_scan(q, k, v, log_gamma, s0, include_diag):
    B, T, H, _ = q.shape
    dv = v.shape[-1]
    C = RET_CHUNK
    N = T // C
    idx = jnp.arange(C, dtype=jnp.float32)
    diff = idx[:, None] - idx[None, :]
    keep = (diff >= 0) if include_diag else (diff > 0)
    intra = jnp.where(keep[None], jnp.exp(jnp.maximum(diff, 0.0)[None] * log_gamma[:, None, None]), 0.0)
    q_dec = jnp.exp((idx + 1.0)[None] * log_gamma[:, None])
    k_dec = jnp.exp((C - 1.0 - idx)[None] * log_gamma[:, None])
    c_dec = jnp.exp(C * log_gamma)[:, None, None]

    def chunks(a):
        return a.reshape(B, N, C, H, a.shape[-1]).transpose(1, 0, 3, 2, 4)

    def step(s, qkv):
        qn, kn, vn = qkv
        att = jnp.einsum('bhid,bhjd->bhij', qn, kn) * intra
        o = jnp.einsum('bhij,bhjv->bhiv', att, vn) + jnp.einsum('bhid,bhdv->bhiv', qn * q_dec[..., None], s)
        s = s * c_dec + jnp.einsum('bhjd,bhjv->bhdv', kn * k_dec[..., None], vn)
        return s, o

    s_fin, o = lax.scan(step, s0, (chunks(q), chunks(k), chunks(v)))
    return o.transpose(1, 0, 3, 2, 4).reshape(B, T, H, dv), s_fin

def retention_bidir(q, k, v, lg_f, lg_b, s0_f, s0_b):
    o_f, s_f = retention_scan(q, k, v, lg_f, s0_f, True)
    rev = lambda a: jnp.flip(a, axis=1)
    o_b, s_b = retention_scan(rev(q), rev(k), rev(v), lg_b, s0_b, False)
    return o_f + rev(o_b), s_f, s_b

def retention_mixer(xl, xc, w_in, w_out, gn_g, decay_f, decay_b, ctx_out):
    H, DK, DV = RET_HEADS, RET_QK_DIM, RET_V_DIM
    lg_f = jax.nn.log_sigmoid(decay_f.astype(jnp.float32))
    lg_b = jax.nn.log_sigmoid(decay_b.astype(jnp.float32))

    def project(x, ang):
        B, T, _ = x.shape
        q, k, v, g = jnp.split(x @ w_in, [H * DK, 2 * H * DK, 2 * H * DK + H * DV], axis=-1)
        q = q.reshape(B, T, H, DK)
        k = k.reshape(B, T, H, DK) * DK ** -0.5
        v = v.reshape(B, T, H, DV)
        if ang is not None:
            q = apply_rope_2(q, ang, 1)
            k = apply_rope_2(k, ang, 1)
        return q.astype(jnp.float32), k.astype(jnp.float32), v.astype(jnp.float32), g

    def read_out(o, g):
        mu = jnp.mean(o, axis=-1, keepdims=True)
        var = jnp.mean(jnp.square(o - mu), axis=-1, keepdims=True)
        on = (o - mu) * lax.rsqrt(var + EPS) * gn_g.astype(jnp.float32).reshape(H, DV)
        B, T = o.shape[:2]
        return (jax.nn.silu(g) * on.reshape(B, T, H * DV).astype(g.dtype)) @ w_out

    qc, kc, vc, gc = project(xc, None)
    Bc, L = xc.shape[:2]
    if ctx_out:
        zeros = jnp.zeros((Bc, H, DK, DV), jnp.float32)
        oc, s_f, s_b = retention_bidir(qc, kc, vc, lg_f, lg_b, zeros, zeros)
        yc = read_out(oc, gc)
    else:
        pos = jnp.arange(L, dtype=jnp.float32)[:, None]
        s_f = jnp.einsum('bthd,bthv->bhdv', kc * jnp.exp((L - 1.0 - pos) * lg_f)[None, :, :, None], vc)
        s_b = jnp.einsum('bthd,bthv->bhdv', kc * jnp.exp(pos * lg_b)[None, :, :, None], vc)
        yc = None
    T = xl.shape[1]
    ang = rope_angles([jnp.arange(T)], DK)
    ql, kl, vl, gl = project(xl, ang)
    ol, _, _ = retention_bidir(ql, kl, vl, lg_f, lg_b, s_f, s_b)
    return read_out(ol, gl), yc

def nat_mixer(xl, xc, w_qkv, w_o, rpb, ctx_out):
    H, DH = NAT_HEADS, NAT_HEAD_DIM

    def project(x):
        B, T, _ = x.shape
        q, k, v = jnp.split(x @ w_qkv, 3, axis=-1)
        return (q * DH ** -0.5).reshape(B, T, H, DH), k.reshape(B, T, H, DH), v.reshape(B, T, H, DH)

    qc, kc, vc = project(xc)
    ql, kl, vl = project(xl)
    B, T, _ = xl.shape
    rows = T // GRID_W
    kh = min(NAT_KH, rows)
    nk = kh * NAT_KW
    qg = ql.reshape(B, rows, GRID_W, H, DH)
    kg = kl.reshape(B, rows, GRID_W, H, DH)
    vg = vl.reshape(B, rows, GRID_W, H, DH)
    cols = jnp.arange(GRID_W)
    col_idx = jnp.clip(cols - NAT_KW // 2, 0, GRID_W - NAT_KW)[:, None] + jnp.arange(NAT_KW)
    col_bias_idx = col_idx - cols[:, None] + NAT_KW - 1

    def row_block(r):
        r0 = jnp.clip(r - kh // 2, 0, rows - kh)
        kw = lax.dynamic_slice_in_dim(kg, r0, kh, axis=1)[:, :, col_idx]
        vw = lax.dynamic_slice_in_dim(vg, r0, kh, axis=1)[:, :, col_idx]
        qr = lax.dynamic_index_in_dim(qg, r, axis=1, keepdims=False)
        row_bias_idx = r0 + jnp.arange(kh) - r + NAT_KH - 1
        bias = rpb[:, row_bias_idx][:, :, col_bias_idx].transpose(0, 2, 1, 3)
        s_nb = jnp.einsum('bchd,bacnhd->bhcan', qr, kw).astype(jnp.float32) + bias.astype(jnp.float32)
        s_cx = jnp.einsum('bchd,bjhd->bhcj', qr, kc).astype(jnp.float32)
        p = jax.nn.softmax(jnp.concatenate([s_nb.reshape(B, H, GRID_W, nk), s_cx], axis=-1), axis=-1).astype(vl.dtype)
        p_nb = p[..., :nk].reshape(B, H, GRID_W, kh, NAT_KW)
        return jnp.einsum('bhcan,bacnhd->bchd', p_nb, vw) + jnp.einsum('bhcj,bjhd->bchd', p[..., nk:], vc)

    o = lax.map(row_block, jnp.arange(rows))
    yl = o.transpose(1, 0, 2, 3, 4).reshape(B, T, H * DH) @ w_o
    yc = None
    if ctx_out:
        p = jax.nn.softmax(jnp.einsum('bihd,bjhd->bhij', qc, kc).astype(jnp.float32), axis=-1).astype(vc.dtype)
        oc = jnp.einsum('bhij,bjhd->bihd', p, vc)
        yc = oc.reshape(oc.shape[0], oc.shape[1], H * DH) @ w_o
    return yl, yc

def pool_mixer(x, w_grp, scale):
    B, T, D = x.shape
    G, Dg = POOL_GROUPS, POOL_GROUP_DIM
    xf = x.astype(jnp.float32).reshape(B, T, G, Dg)
    csum = jnp.concatenate([jnp.zeros((B, 1, G, Dg), jnp.float32), jnp.cumsum(xf, axis=1)], axis=1)
    half = jnp.asarray([w // 2 for w in POOL_WINDOWS])
    t = jnp.arange(T)[:, None]
    lo = jnp.clip(t - half, 0, T)
    hi = jnp.clip(t + half, 0, T)
    grp = jnp.arange(G)[None, :]
    mean = (csum[:, hi, grp] - csum[:, lo, grp]) / (hi - lo).astype(jnp.float32)[None, :, :, None]
    pooled = (mean - xf).astype(x.dtype)
    return jnp.einsum('btgc,gcd->btgd', pooled, w_grp).reshape(B, T, D) * scale

def swa_mixer(xl, xc, w_qkv, w_o, sink, ctx_out):
    HQ, HKV, DH = SWA_Q_HEADS, SWA_KV_HEADS, SWA_HEAD_DIM
    G = HQ // HKV

    def project(x, ang):
        B, T, _ = x.shape
        q, k, v = jnp.split(x @ w_qkv, [HQ * DH, (HQ + HKV) * DH], axis=-1)
        q = q.reshape(B, T, HQ, DH)
        k = k.reshape(B, T, HKV, DH)
        v = v.reshape(B, T, HKV, DH)
        if ang is not None:
            q = apply_rope_2(q, ang, 2)
            k = apply_rope_2(k, ang, 2)
        return (q * DH ** -0.5).reshape(B, T, HKV, G, DH), k, v

    B, T, _ = xl.shape
    t = jnp.arange(T)
    ang = rope_angles([t // GRID_W, t % GRID_W], DH)
    ql, kl, vl = project(xl, ang)
    qc, kc, vc = project(xc, None)
    sink_l = sink.astype(jnp.float32).reshape(HKV, G)
    nb = T // SWA_BLOCK
    nw = SWA_WINDOW // SWA_BLOCK
    nk = (2 * nw + 1) * SWA_BLOCK

    def band(a):
        ap = jnp.pad(a, ((0, 0), (SWA_WINDOW, SWA_WINDOW), (0, 0), (0, 0))).reshape(B, nb + 2 * nw, SWA_BLOCK, HKV, DH)
        return jnp.concatenate([ap[:, o:o + nb] for o in range(2 * nw + 1)], axis=2)

    kb, vb = band(kl), band(vl)
    qb = ql.reshape(B, nb, SWA_BLOCK, HKV, G, DH)
    qpos = (jnp.arange(nb)[:, None] * SWA_BLOCK + jnp.arange(SWA_BLOCK))[:, :, None]
    kpos = (jnp.arange(nb)[:, None] * SWA_BLOCK - SWA_WINDOW + jnp.arange(nk))[:, None, :]
    allowed = (jnp.abs(qpos - kpos) <= SWA_WINDOW) & (kpos >= 0) & (kpos < T)
    s_loc = jnp.where(allowed, jnp.einsum('bnikgd,bnjkd->bkgnij', qb, kb).astype(jnp.float32), NEG_INF)
    s_cx = jnp.einsum('bnikgd,bjkd->bkgnij', qb, kc).astype(jnp.float32)
    s_sk = jnp.broadcast_to(sink_l[None, :, :, None, None, None], s_loc.shape[:-1] + (1,))
    p = jax.nn.softmax(jnp.concatenate([s_loc, s_cx, s_sk], axis=-1), axis=-1)[..., :-1].astype(vl.dtype)
    o = jnp.einsum('bkgnij,bnjkd->bnikgd', p[..., :nk], vb) + jnp.einsum('bkgnij,bjkd->bnikgd', p[..., nk:], vc)
    yl = o.reshape(B, T, HQ * DH) @ w_o
    yc = None
    if ctx_out:
        s = jnp.einsum('bikgd,bjkd->bkgij', qc, kc).astype(jnp.float32)
        sk = jnp.broadcast_to(sink_l[None, :, :, None, None], s.shape[:-1] + (1,))
        pc = jax.nn.softmax(jnp.concatenate([s, sk], axis=-1), axis=-1)[..., :-1].astype(vc.dtype)
        oc = jnp.einsum('bkgij,bjkd->bikgd', pc, vc)
        yc = oc.reshape(oc.shape[0], oc.shape[1], HQ * DH) @ w_o
    return yl, yc

def second_inputs(seed: int = 0) -> dict:
    key = jax.random.key(seed)
    ks = jax.random.split(key, 24)
    D, F = D_MODEL, FFN_HIDDEN
    nrm = lambda k, shape, s: jax.random.normal(k, shape, jnp.float32) * s
    ret_in = 2 * RET_HEADS * RET_QK_DIM + 2 * RET_HEADS * RET_V_DIM
    ret_v = RET_HEADS * RET_V_DIM
    decay_logit = jnp.log(2.0 ** (5.0 + jnp.arange(RET_HEADS, dtype=jnp.float32)) - 1.0)
    nat_w = NAT_HEADS * NAT_HEAD_DIM
    swa_in = (SWA_Q_HEADS + 2 * SWA_KV_HEADS) * SWA_HEAD_DIM
    swa_o = SWA_Q_HEADS * SWA_HEAD_DIM
    return {
        'x': nrm(ks[0], (BATCH, SEQ, D), 1.0),
        'c': nrm(ks[1], (BATCH, D), 1.0),
        'ctx': nrm(ks[2], (BATCH, CTX_LEN, D), 1.0),
        'c_ctx': nrm(ks[3], (D,), 1.0),
        'w_mod': nrm(ks[4], (DEPTH, D, 9 * D), 0.5 * D ** -0.5),
        'b_mod': nrm(ks[5], (DEPTH, 9 * D), 0.01),
        'norm_g': 1.0 + nrm(ks[6], (DEPTH, 3, D), 0.02),
        'ffn_w_in': nrm(ks[7], (DEPTH, 2, D, 2 * F), D ** -0.5),
        'ffn_w_out': nrm(ks[8], (DEPTH, 2, F, D), F ** -0.5),
        'ret_w_in': nrm(ks[9], (N_RET, D, ret_in), D ** -0.5),
        'ret_w_out': nrm(ks[10], (N_RET, ret_v, D), ret_v ** -0.5),
        'ret_gn_g': 1.0 + nrm(ks[11], (N_RET, ret_v), 0.02),
        'ret_decay_f': decay_logit + nrm(ks[12], (N_RET, RET_HEADS), 0.05),
        'ret_decay_b': decay_logit + nrm(ks[13], (N_RET, RET_HEADS), 0.05),
        'nat_w_qkv': nrm(ks[14], (N_NAT, D, 3 * nat_w), D ** -0.5),
        'nat_w_o': nrm(ks[15], (N_NAT, nat_w, D), nat_w ** -0.5),
        'nat_rpb': nrm(ks[16], (N_NAT, NAT_HEADS, 2 * NAT_KH - 1, 2 * NAT_KW - 1), 0.1),
        'pool_w': nrm(ks[17], (N_POOL, POOL_GROUPS, POOL_GROUP_DIM, POOL_GROUP_DIM), POOL_GROUP_DIM ** -0.5),
        'pool_scale': 1.0 + nrm(ks[18], (N_POOL, D), 0.02),
        'swa_w_qkv': nrm(ks[19], (N_SWA, D, swa_in), D ** -0.5),
        'swa_w_o': nrm(ks[20], (N_SWA, swa_o, D), swa_o ** -0.5),
        'swa_sink': nrm(ks[21], (N_SWA, SWA_Q_HEADS), 0.5),
        'final_norm_g': 1.0 + nrm(ks[22], (D,), 0.02),
    }

def second_block(x, c, ctx, c_ctx, w_mod, b_mod, norm_g, ffn_w_in, ffn_w_out,
              ret_w_in, ret_w_out, ret_gn_g, ret_decay_f, ret_decay_b,
              nat_w_qkv, nat_w_o, nat_rpb, pool_w, pool_scale,
              swa_w_qkv, swa_w_o, swa_sink, final_norm_g):
    D = x.shape[-1]
    h, hc = x, ctx
    s_c = jax.nn.silu(c)
    s_cc = jax.nn.silu(c_ctx)[None]
    for i in range(DEPTH):
        kind, occ = i % N_MIXERS, i // N_MIXERS
        last = i == DEPTH - 1
        ctx_live = (not last) or kind != MIX_POOL
        ml = (s_c @ w_mod[i] + b_mod[i]).reshape(-1, 3, 3, D)
        h = gated_residual(h, ml, 0, swiglu(ada_in(h, norm_g[i, 0], ml, 0), ffn_w_in[i, 0], ffn_w_out[i, 0]), 0.5)
        xl = ada_in(h, norm_g[i, 1], ml, 1)
        xc = None
        if ctx_live:
            mc = (s_cc @ w_mod[i] + b_mod[i]).reshape(-1, 3, 3, D)
            hc = gated_residual(hc, mc, 0, swiglu(ada_in(hc, norm_g[i, 0], mc, 0), ffn_w_in[i, 0], ffn_w_out[i, 0]), 0.5)
            xc = ada_in(hc, norm_g[i, 1], mc, 1)
        if kind == MIX_RET:
            yl, yc = retention_mixer(xl, xc, ret_w_in[occ], ret_w_out[occ], ret_gn_g[occ],
                                     ret_decay_f[occ], ret_decay_b[occ], not last)
        elif kind == MIX_NAT:
            yl, yc = nat_mixer(xl, xc, nat_w_qkv[occ], nat_w_o[occ], nat_rpb[occ], not last)
        elif kind == MIX_POOL:
            yl = pool_mixer(xl, pool_w[occ], pool_scale[occ])
            yc = None if last else pool_mixer(xc, pool_w[occ], pool_scale[occ])
        else:
            yl, yc = swa_mixer(xl, xc, swa_w_qkv[occ], swa_w_o[occ], swa_sink[occ], not last)
        h = gated_residual(h, ml, 1, yl, 1.0)
        if not last:
            hc = gated_residual(hc, mc, 1, yc, 1.0)
            hc = gated_residual(hc, mc, 2, swiglu(ada_in(hc, norm_g[i, 2], mc, 2), ffn_w_in[i, 1], ffn_w_out[i, 1]), 0.5)
        h = gated_residual(h, ml, 2, swiglu(ada_in(h, norm_g[i, 2], ml, 2), ffn_w_in[i, 1], ffn_w_out[i, 1]), 0.5)
    return rms_norm_2(h, final_norm_g)


def setup_inputs(seed=0):
    out = dict(first_inputs(seed))
    for name, value in second_inputs(seed + 1).items():
        if name != "x":
            out[name + "_2"] = value
    return out


def reference(
    x, positions, ffn1_norm, ffn1_w_in, ffn1_w_out, mix_norm, w_in, gm_v_norm, gm_w_s, gm_b_s,
    mla_q_norm, mla_kv_norm, mla_w_uq, mla_w_ukv, mla_q_gain, mla_k_gain, ssd_conv_w,
    ssd_conv_b, ssd_dt_bias, ssd_a_log, ssd_d, ssd_norm, w_branch, w_out, ffn2_norm, ffn2_w_in,
    ffn2_w_out, c_2, ctx_2, c_ctx_2, w_mod_2, b_mod_2, norm_g_2, ffn_w_in_2, ffn_w_out_2,
    ret_w_in_2, ret_w_out_2, ret_gn_g_2, ret_decay_f_2, ret_decay_b_2, nat_w_qkv_2, nat_w_o_2,
    nat_rpb_2, pool_w_2, pool_scale_2, swa_w_qkv_2, swa_w_o_2, swa_sink_2, final_norm_g_2,
):
    x = first_block(
        x, positions, ffn1_norm, ffn1_w_in, ffn1_w_out, mix_norm, w_in, gm_v_norm, gm_w_s,
        gm_b_s, mla_q_norm, mla_kv_norm, mla_w_uq, mla_w_ukv, mla_q_gain, mla_k_gain,
        ssd_conv_w, ssd_conv_b, ssd_dt_bias, ssd_a_log, ssd_d, ssd_norm, w_branch, w_out,
        ffn2_norm, ffn2_w_in, ffn2_w_out,
    )
    return second_block(
        x, c_2, ctx_2, c_ctx_2, w_mod_2, b_mod_2, norm_g_2, ffn_w_in_2, ffn_w_out_2, ret_w_in_2,
        ret_w_out_2, ret_gn_g_2, ret_decay_f_2, ret_decay_b_2, nat_w_qkv_2, nat_w_o_2,
        nat_rpb_2, pool_w_2, pool_scale_2, swa_w_qkv_2, swa_w_o_2, swa_sink_2, final_norm_g_2,
    )


_drawn_inputs = setup_inputs


def setup_inputs(seed=0):
    import zlib

    import numpy as np

    out = dict(_drawn_inputs(seed))
    spreads = {}
    factors = {'gm_v_norm': 7.884,
     'mla_q_norm': 8.0,
     'mla_kv_norm': 6.185,
     'mla_q_gain': 8.0,
     'mla_k_gain': 8.0,
     'ssd_conv_b': 3.112,
     'b_mod_2': 6.347,
     'norm_g_2': 8.0,
     'ret_gn_g_2': 8.0,
     'nat_rpb_2': 64.0,
     'final_norm_g_2': 8.63}
    for name, (base, spread) in spreads.items():
        noise = np.random.default_rng([zlib.crc32(name.encode()), seed]).standard_normal(out[name].shape)
        drawn = base * np.exp(spread * noise) if base else spread * noise
        out[name] = jnp.asarray(drawn.astype(out[name].dtype))
    for name, factor in factors.items():
        out[name] = (out[name] * factor).astype(out[name].dtype)
    return out
```

```python
from contextlib import ExitStack

import concourse.bass as bass
from concourse import mybir

F32 = mybir.dt.float32
F32R = mybir.dt.float32r
I32 = mybir.dt.int32
ALU = mybir.AluOpType
ACT = mybir.ActivationFunctionType
AX = mybir.AxisListType.X

P = 128
D = 1024
KD = D // P
SEQ = 256
DEPTH = 2
DFF = 2816
KF = DFF // P
GROUPS = DFF // 256
EPS = 1e-6
HEADS = 8
QK = 96
ROPE0 = 64
NEG = -1e30
UV, CQ, CKV, ZC, XBC, DT, GATES = 0, 1024, 1408, 1696, 2208, 3232, 3240
BANKS = 8
NRAW = 3
NSPLIT = 2
SLAB = 2048
MODS_PER_FFN = 18
C_IDENT, C_U, C_CAUSAL, C_ONES, C_NAT, C_FREQ, C_FLIP, C_END = (
    0, 128, 256, 384, 512, 576, 592, 720)
R_COS, R_SIN, R_DIST, R_END = 0, 256, 512, 1024
TWO_PI = 6.283185307179586
TP1, TP2 = 6.28125, 0.0019350051879882812
TP3 = TWO_PI - TP1 - TP2


KINDS = {
    "pe": {"projected": "xbc dtp zp uvp cqp ckvp gp bp qp kvp wop rqp rkp rvp rgp rwp nqp nkp nvp nwp",
           "turned": "turn ty xst bt wst qkt cols", "scores": "sc nsp rap", "probs_turned": "ptp nptp",
           "attended": "op nop rop", "scan_sums": "csb csp cbp spp", "scan_out": "yd stp yo"},
    "act": {"projection_kept": "xr z uv cq ckv xs btok q kv rqc rkc rv rg Y0 nq nk nv gate_rows",
            "columns_hi": "xh yh qkT pT", "parameters": "sincos lge alog scc_half scc",
            "probs": "pr npr", "scan": "cv dte expE expc st wexp", "squares": "ssa xn"},
    "dve": {"parameters": "cols_copied angles lgx lg ctx_ready modc", "columns_lo": "xT yT npT",
            "scan_in": "dtr dtn conv daU csc dec wlog rope", "scan_weights": "diff_half cbm MT xdd ra",
            "scan_rows": "yd_in yo_in yc gvn cqn ckn ya qkr rn ry",
            "merged": "merged mtmp", "attention_max": "nmax nnm", "attended": "yb_head ny_head",
            "residual": "Xd Xw Xr Xn sgg nt Y", "mean_square": "ms", "gate_diagonals": "diag aff wT"},
    "pool": {"rstd": "rstd", "padding": "xr0 nbias"},
}
KIND = {(engine, stage): kind for engine, kinds in KINDS.items()
        for kind, stages in kinds.items() for stage in stages.split()}


class Ledger:

    def __init__(self, nc, ctx, known):
        self.nc, self.ctx, self.known = nc, ctx, known
        self.events, self.count, self.sems = {}, {}, {}
        self.bank_of, self.freed, self.units, self.order, self.params = {}, {}, 0, [], 16

    def sem(self, name):
        if name not in self.sems:
            self.sems[name] = self.ctx.enter_context(self.nc.semaphore(name))
        return self.sems[name]

    def value(self, event):
        name, n = self.known.events[event] if self.known else ("first_writing", 1)
        return self.sem(name), n

    def reader_of(self, unit):
        name, n = self.known.freed[unit] if self.known else ("first_writing", 1)
        return self.sem(name), n

    def all_params(self):
        return self.known.params if self.known else 16


class Signals:

    def __init__(self, ledger, name):
        self.l, self.name = ledger, name

    def inc(self, stage, *key, also=(), frees=None):
        name = f"{self.name}_{KIND.get((self.name, stage), stage)}"
        n = self.l.count[name] = self.l.count.get(name, 0) + 1
        for event in ((stage, *key), *also):
            self.l.events[event] = (name, n)
        if frees is not None:
            self.l.freed[frees] = (name, n)
        return self.l.sem(name), 1

    def at(self, *event):
        return self.l.value(event)


class Slabs:

    def __init__(self):
        self.items, self.index, self.nsplit = [], {}, 0

    def add(self, key, src, kt, n, split=True):
        self.index[key] = len(self.items)
        self.items.append((key, src, kt, n, self.nsplit if split else None))
        self.nsplit += split


def plan(w):
    s = Slabs()

    def rows(m, k0, kt, c0, n):
        return m[k0 * P:(k0 + kt) * P, c0:c0 + n].rearrange("(k p) n -> p k n", p=P)

    mods = [0]

    def mod():
        i = mods[0]
        mods[0] += 1
        l, g = divmod(i, 36)
        s.add(("mod", i), rows(w["w_mod_2"][l], 0, KD, 256 * g, 256), KD, 256, split=False)

    def ffn(name, w_up, w_down, with_mods):
        for g in range(GROUPS):
            s.add((name, "gate", g), rows(w_up, 0, KD, 256 * g, 256), KD, 256)
            s.add((name, "up", g), rows(w_up, 0, KD, DFF + 256 * g, 256), KD, 256)
            if with_mods:
                mod()
        i = 0
        for n in range(2):
            for d in range(6):
                kt = min(4, KF - 4 * d)
                s.add((name, "down", n, d), rows(w_down, 4 * d, kt, 512 * n, 512), kt, 512)
                if with_mods and i < MODS_PER_FFN - GROUPS:
                    mod()
                i += 1

    def wide(name, m, c0, n):
        for half in range(2):
            s.add((name, half), rows(m, 4 * half, 4, c0, n), 4, n)

    for l in range(DEPTH):
        m = w["w_in"][l]
        ffn(("f1", l), w["ffn1_w_in"][l], w["ffn1_w_out"][l], True)
        for i in range(4):
            s.add(("xbc", l, i), rows(m, 0, KD, XBC + 256 * i, 256), KD, 256)
        s.add(("dt", l), rows(m, 0, KD, DT, 8), KD, 8)
        wide(("z", l), m, ZC, 512)
        for n in range(2):
            wide(("uv", l, n), m, UV + 512 * n, 512)
        wide(("cq", l), m, CQ, 384)
        wide(("ckv", l), m, CKV, 288)
        for br in (2, 0):
            for n in range(2):
                wide(("g", l, br, n), m, GATES + D * br + 512 * n, 512)
            for n in range(2):
                s.add(("b", l, br, n), rows(w["w_branch"][l, br], 0, 4, 512 * n, 512), 4, 512)
        for n in range(2):
            s.add(("q", l, n), rows(w["mla_w_uq"][l], 0, 3, 384 * n, 384), 3, 384)
        s.add(("kv", l), rows(w["mla_w_ukv"][l], 0, 2, 0, 1024), 2, 1024)
        for n in range(2):
            wide(("g", l, 1, n), m, GATES + D + 512 * n, 512)
        for n in range(2):
            s.add(("b", l, 1, n), rows(w["w_branch"][l, 1], 0, 4, 512 * n, 512), 4, 512)
        for n in range(2):
            wide(("wo", l, n), w["w_out"][l], 512 * n, 512)
        ffn(("f2", l), w["ffn2_w_in"][l], w["ffn2_w_out"][l], True)
    ffn(("g1", 0), w["ffn_w_in_2"][0, 0], w["ffn_w_out_2"][0, 0], False)
    for h in range(4):
        m = w["ret_w_in_2"][0]
        for i, part in enumerate("qk"):
            s.add(("r" + part, h), rows(m, 0, KD, 1024 * i + 256 * h, 256), KD, 256)
        for i, part in enumerate("vg"):
            wide(("r" + part, h), m, 2048 * (i + 1) + 512 * h, 512)
        for n in range(2):
            s.add(("rw", h, n), rows(w["ret_w_out_2"][0], 4 * h, 4, 512 * n, 512), 4, 512)
    ffn(("g2", 0), w["ffn_w_in_2"][0, 1], w["ffn_w_out_2"][0, 1], False)
    ffn(("g1", 1), w["ffn_w_in_2"][1, 0], w["ffn_w_out_2"][1, 0], False)
    m = w["nat_w_qkv_2"][0]
    for i, part in enumerate("qk"):
        for j in range(4):
            s.add(("n" + part, j), rows(m, 0, KD, 1024 * i + 256 * j, 256), KD, 256)
    for n in range(2):
        wide(("nv", n), m, 2048 + 512 * n, 512)
    for n in range(2):
        wide(("nw", n), w["nat_w_o_2"][0], 512 * n, 512)
    ffn(("g2", 1), w["ffn_w_in_2"][1, 1], w["ffn_w_out_2"][1, 1], False)
    return s


def build(nc, w, consts, out, known):
    slabs = plan(w)
    with ExitStack() as ctx:
        L = Ledger(nc, ctx, known)
        base = [nc.sbuf_base + 64 & ~63]

        def place(name, shape, dt=F32, off=None):
            size = 4
            for x in shape[1:]:
                size *= x
            size = (size + 63) // 64 * 64
            if off is None:
                off = base[0]
                base[0] += size
            return nc.alloc_sbuf_tensor_at(name, list(shape), dt, offset=off)

        raw = [place(f"raw{i}", [P, SLAB]) for i in range(NRAW)]
        whi = [place(f"whi{i}", [P, SLAB], F32R) for i in range(NSPLIT)]
        wlo = [place(f"wlo{i}", [P, SLAB], F32R) for i in range(NSPLIT)]
        cst = place("cst", [P, C_END])
        X = place("X", [P, 4, D])
        cols = place("cols", [P, 4, P])
        modc = place("modc", [P, DEPTH, 72, 2])
        scc = place("scc", [P, KD, 2])
        small = place("small", [P, 256])
        cs16 = place("cs16", [P, 2, 2, 16])
        aff = place("aff", [P, KD, 2])
        dtb = place("dtb", [P, 3, DEPTH, 8])
        qkg = place("qkg", [P, DEPTH, 2, QK])
        vgain = place("vgain", [P, 512])
        lgs = place("lgs", [P, 8, 8])
        bsum = place("bsum", [P, 16])
        R0 = base[0]
        KB = 1024
        xT = {512: (place("xTh", [P, KD, 512], F32R), place("xTl", [P, KD, 512], F32R)),
              256: (place("xTh256", [P, KD, 256], F32R, off=R0), place("xTl256", [P, KD, 256], F32R, off=R0 + 8 * KB))}
        A0 = base[0]
        B0 = A0 - 16 * KB

        def arena(name, shape, off, dt=F32):
            t = nc.alloc_sbuf_tensor_at(name, list(shape), dt, offset=A0 + off)
            return t

        xn = arena("xn", [P, 4, D], 0)
        junk_a = arena("junk_a", [P, D], 16 * KB)
        junk_v = arena("junk_v", [P, D], 20 * KB)
        rowt = arena("rowt", [P, 4, P], 24 * KB)
        hh = arena("hh", [P, KF * 512], 0, F32R)
        hl = arena("hl", [P, KF * 512], 44 * KB, F32R)
        sg = arena("sg", [P, 2, 512], 88 * KB)
        gb = nc.alloc_sbuf_tensor_at("gb", [P, 2, D], F32, offset=A0 - 16 * KB)
        dg = nc.alloc_sbuf_tensor_at("dg", [P, KD, P], F32, offset=A0 - 8 * KB)
        def barena(name, shape, off, dt=F32):
            return nc.alloc_sbuf_tensor_at(name, list(shape), dt, offset=B0 + off)

        xr = barena("xr", [P, 8, 259], 0)
        cv = barena("cv", [P, 8, 256], 9 * KB)
        xs = barena("xs", [P, 2, 512], 17 * KB)
        E_ = barena("E", [P, 8, P], 21 * KB)
        xdt = barena("xdt", [P, 512], 25 * KB)
        xdd = barena("xdd", [P, 512], 27 * KB)
        st = barena("st", [P, 512], 29 * KB)
        btok = barena("btok", [P, 2, P], 31 * KB)
        cbm = barena("cbm", [P, 2, P], 32 * KB)
        gu = barena("gu", [P, 2, 512], 33 * KB)
        gv = barena("gv", [P, 2, 512], 37 * KB)
        z = barena("z", [P, 2, 512], 41 * KB)
        cq = barena("cq", [P, 2, 384], 45 * KB)
        ckv = barena("ckv", [P, 2, 288], 48 * KB)
        wT = barena("wT", [P, 4, P], 51 * KB)
        ws = barena("ws", [P, 4, P], 53 * KB)
        merged = barena("merged", [P, 2, D], 55 * KB)
        gates = barena("gates", [P, 2, D], 63 * KB)
        ytT = [(barena(f"yth{i}", [P, 4, 256], 71 * KB + 8 * i * KB, F32R),
                barena(f"ytl{i}", [P, 4, 256], 75 * KB + 8 * i * KB, F32R)) for i in range(2)]
        tmp = barena("tmp", [P, 2, 512], 87 * KB)
        qkT = barena("qkT", [P, HEADS, 512], 0)
        kv = barena("kv", [P, 2, D], 17 * KB)
        sq = barena("sq", [P, 16, QK], 25 * KB)
        cqTh = barena("cqTh", [P, 3, 256], 33 * KB, F32R)
        cqTl = barena("cqTl", [P, 3, 256], 36 * KB, F32R)
        ckTh = barena("ckTh", [P, 2, 256], 39 * KB, F32R)
        ckTl = barena("ckTl", [P, 2, 256], 41 * KB, F32R)
        qk = barena("qk", [P, 2, 16, QK], 91 * KB)
        yb = barena("yb", [P, 2, 512], 91 * KB)
        pr = barena("pr", [P, 2, 384], 103 * KB)
        pT = barena("pT", [P, 384], 89 * KB)
        rq = arena("rq", [P, 2, 512], 0)
        rk = arena("rk", [P, 2, 512], 4 * KB)
        rv = arena("rv", [P, 4, 512], 8 * KB)
        rg = arena("rg", [P, 4, 512], 16 * KB)
        ra = arena("ra", [P, 3, 512], 24 * KB)
        WX = arena("WX", [P, 2, 2, 256], 30 * KB)
        wtmp = arena("wtmp", [P, 2, 2, 256], 34 * KB)
        rYh = arena("rYh", [P, 4, 512], 38 * KB, F32R)
        rYl = arena("rYl", [P, 4, 512], 46 * KB, F32R)
        Y = arena("Y", [P, 4, D], 54 * KB)
        rt = arena("rt", [P, 2, 512], 70 * KB)
        gbm = arena("gbm", [P, 2, D], 74 * KB)
        dgm = arena("dgm", [P, KD, P], 82 * KB)
        rcst = arena("rcst", [P, R_END], 86 * KB)
        nq = arena("nq", [P, 8, 256], 0)
        nk = arena("nk", [P, 8, 512], 8 * KB)
        nv = arena("nv", [P, 4, D], 24 * KB)
        nbias = [arena(f"nbias{i}", [P, 2, 4, 256], (40 + 8 * i) * KB) for i in range(2)]
        npr = arena("npr", [P, 2, 512], 56 * KB)
        npT = arena("npT", [P, 2, 512], 60 * KB)
        ny = arena("ny", [P, 2, D], 64 * KB)
        nt = arena("nt", [P, 512], 72 * KB)
        fg = arena("fg", [P, D], 70 * KB)
        fo = arena("fo", [P, 2, D], 74 * KB)

        ident = cst[:, C_IDENT:C_IDENT + P]
        upper = cst[:, C_U:C_U + P]
        ones = cst[:, C_ONES:C_ONES + P]
        bank = [ctx.enter_context(nc.psum_tensor(f"bank{i}", [P, 512], F32)) for i in range(BANKS)]
        landed = [ctx.enter_context(nc.semaphore(f"raw{i}_landed")) for i in range(NRAW)]
        block = ctx.enter_context(nc.Block())

        def unit(*key):
            return bank[L.known.bank_of[key]] if L.known else bank[0]

        def col(table, row, n=1):
            return cols[:, table, row:row + n]

        NORM1, NORMX, NORM2, NORMG, QN, KVN, SSN = 0, 16, 32, 48, 96, 102, 106
        CVB, CVW, GN, BS = 0, 16, 80, 96
        BM, CC = 0, 72

        def row_loads():
            f = lambda name, pat: w[name].rearrange(pat, p=P)
            yield rowt[NORM1:NORM1 + 16, 0, :], f("ffn1_norm", "l (k p) -> (l k) p")
            yield rowt[NORMX:NORMX + 16, 0, :], f("mix_norm", "l (k p) -> (l k) p")
            yield rowt[NORM2:NORM2 + 16, 0, :], f("ffn2_norm", "l (k p) -> (l k) p")
            yield rowt[NORMG:NORMG + 48, 0, :], f("norm_g_2", "l j (k p) -> (l j k) p")
            yield rowt[QN:QN + 6, 0, :], f("mla_q_norm", "l (k p) -> (l k) p")
            yield rowt[KVN:KVN + 4, 0, :], f("mla_kv_norm", "l (k p) -> (l k) p")
            yield rowt[SSN:SSN + 8, 0, :], f("ssd_norm", "l (k p) -> (l k) p")
            yield rowt[CVB:CVB + 16, 1, :], f("ssd_conv_b", "l (k p) -> (l k) p")
            yield rowt[CVW:CVW + 64, 1, :], f("ssd_conv_w", "l j (k p) -> (l j k) p")
            yield rowt[GN:GN + 16, 1, :], f("ret_gn_g_2", "l (k p) -> (l k) p")
            yield rowt[BS:BS + 8, 1, :], w["gm_b_s"].rearrange("l g t -> (l g) t")
            for l in range(DEPTH):
                yield rowt[BM:BM + 72, 2 + l, :], w["b_mod_2"][l].rearrange("(k p) -> k p", p=P)
            yield rowt[CC:CC + 8, 2, :], f("c_2", "l (k p) -> (l k) p")
            yield rowt[CC + 8:CC + 16, 2, :], w["c_ctx_2"].rearrange("(k p) -> k p", p=P)

        ROWS = (114, 104, 88, 72)

        def wide_row(a, n):
            return bass.AP(a.tensor, a.offset, [[0, P], [1, n]])

        def stripe(t, n, l):
            return t[:, l, n * 512:(n + 1) * 512]

        def view(tile, key):
            _, _, kt, n, _ = slabs.items[slabs.index[key]]
            return tile[:, 0:kt * n].rearrange("p (k n) -> p k n", n=n)

        def halves(key):
            i = slabs.items[slabs.index[key]][4] % NSPLIT
            return view(whi[i], key), view(wlo[i], key)

        def arrival(key):
            s = slabs.index[key]
            return landed[s % NRAW], 16 * (s // NRAW + 1)

        @block.sync
        def _(sp):
            e = Signals(L, "sp")
            n_first = [0]

            def first(dst, src):
                sp.dma_start(dst, src).then_inc(L.sem("params_landed"), 16)
                n_first[0] += 16

            def slab_range(a, b):
                for s in range(a, b):
                    key, src, kt, n, split = slabs.items[s]
                    if s >= NRAW:
                        old = slabs.items[s - NRAW][0]
                        if slabs.items[s - NRAW][4] is None:
                            sp.wait_ge(*e.at("mod_used", old))
                        else:
                            sp.wait_ge(*e.at("hi", old))
                            sp.wait_ge(*e.at("lo", old))
                    sp.dma_start(view(raw[s % NRAW], key), src).then_inc(landed[s % NRAW], 16)

            sp.dma_start(X[:, 0:2, :], w["x"][0].rearrange("(t p) n -> p t n", p=P))\
              .then_inc(L.sem("x_landed"), 16)
            slab_range(0, NRAW)
            first(cst[:, :], consts["cst"])
            for dst, src in row_loads():
                first(dst, src)
            for l in range(DEPTH):
                for i, name in enumerate(("ssd_dt_bias", "ssd_a_log", "ssd_d")):
                    first(dtb[:, i, l, :], wide_row(w[name][l], 8))
                for i, name in enumerate(("mla_q_gain", "mla_k_gain")):
                    first(qkg[:, l, i, :], wide_row(w[name][l], QK))
            first(lgs[:, 0, 0:4], wide_row(w["ret_decay_f_2"][0], 4))
            first(lgs[:, 0, 4:8], wide_row(w["ret_decay_b_2"][0], 4))
            with nc.allow_non_contiguous_dma(reason="256 positions, one to a partition and tile"):
                first(bsum[:, 0:2].bitcast(I32), w["positions"][0].rearrange("(t p) -> p t", p=P))
            first(X[:, 2:4, :], w["ctx_2"][0].rearrange("(t p) n -> p t n", p=P))
            L.params = n_first[0]
            slab_range(NRAW, len(slabs.items))
            sp.wait_ge(*e.at("out_row", 1))
            sp.dma_start(out[0].rearrange("(t p) n -> p t n", p=P), fo[:, :, :])\
              .then_inc(L.sem("out_written"), 16)
            sp.wait_ge(L.sem("out_written"), 16)

        def tiles_of(T):
            return range(T // P)

        @block.tensor
        def _(pe):
            e = Signals(L, "pe")

            def new(*key):
                u = L.units
                L.units += 1
                L.bank_of[key] = u % BANKS
                L.order.append(key)
                if u >= BANKS:
                    pe.wait_ge(*L.reader_of(L.order[u - BANKS]))
                return bank[u % BANKS]

            def mm3(ps, lh, ll, rh, rl, start, stop):
                pe.matmul(ps, lh, rh, start=start, stop=False, skip_group_check=True)
                pe.matmul(ps, lh, rl, start=False, stop=False, skip_group_check=True)
                return pe.matmul(ps, ll, rh, start=False, stop=stop, skip_group_check=True)

            mods = [0]

            def mod():
                i = mods[0]
                mods[0] += 1
                pe.wait_ge(*e.at("scc"))
                pe.wait_ge(*arrival(("mod", i)))
                ps = new("modp", i)
                wv = view(raw[slabs.index[("mod", i)] % NRAW], ("mod", i))
                for mc in range(2):
                    for k in range(KD):
                        m = pe.matmul(ps[:, 2 * mc:2 * mc + 2], wv[:, k, mc * P:(mc + 1) * P], scc[:, k, :],
                                      start=k == 0, stop=k == KD - 1)
                m.then_inc(*e.inc("modp", i, also=[("mod_used", ("mod", i))]))

            def split_ready(key):
                pe.wait_ge(*e.at("hi", key))
                pe.wait_ge(*e.at("lo", key))
                return halves(key)

            def feature_major(key, T, units, xh, xl):
                wh, wl = split_ready(key)
                u = 0
                for mc in range(2):
                    if T == 512 or mc == 0:
                        ps = new(*units[u])
                        last_of_unit = T == 512
                    o = 0 if T == 512 else mc * 256
                    for k in range(KD):
                        m = mm3(ps[:, o:o + T], wh[:, k, mc * P:(mc + 1) * P], wl[:, k, mc * P:(mc + 1) * P],
                                xh[:, k, 0:T], xl[:, k, 0:T], k == 0, k == KD - 1)
                    if T == 512 or mc == 1:
                        also = [("used", key)] if mc == 1 else []
                        m.then_inc(*e.inc(*units[u], also=also))
                        u += 1

            def token_major(keys, name, tiles, n, xh, xl, c0=0, k0=0):
                ps = {t: new(*name, t) for t in tiles}
                kk = k0
                total = k0 + sum(slabs.items[slabs.index[k]][2] for k in keys)
                for key in keys:
                    wh, wl = split_ready(key)
                    kt = wh.shape[1]
                    for t in tiles:
                        for k in range(kt):
                            m = mm3(ps[t][:, 0:n], xh[:, kk + k, t * P:(t + 1) * P],
                                    xl[:, kk + k, t * P:(t + 1) * P],
                                    wh[:, k, c0:c0 + n], wl[:, k, c0:c0 + n],
                                    kk + k == k0, kk + k == total - 1)
                        if kk + kt == total:
                            also = [("used", key)] if t == tiles[-1] else []
                            m.then_inc(*e.inc(*name, t, also=also))
                    if kk + kt != total:
                        m.then_inc(*e.inc("used", key))
                    kk += kt

            def turn_in(name, T, ready):
                for k in range(KD):
                    ps = new("turn", name, k)
                    for t in tiles_of(T):
                        if k == 0:
                            pe.wait_ge(*e.at(*ready, t))
                        m = pe.transpose(ps[:, t * P:(t + 1) * P], xn[:, t, k * P:(k + 1) * P], ident)
                    m.then_inc(*e.inc("turn", name, k))

            def turn_y(name, src, chunks, T, ready, c0=0):
                per = 512 // T
                for u in range((chunks + per - 1) // per):
                    ps = new("ty", name, u)
                    for j in range(per):
                        if u * per + j >= chunks:
                            break
                        c = u * per + j
                        for t in tiles_of(T):
                            pe.wait_ge(*e.at(*ready, t))
                            m = pe.transpose(ps[:, j * T + t * P:j * T + (t + 1) * P],
                                             src[:, t, c * P:(c + 1) * P], ident)
                    m.then_inc(*e.inc("ty", name, u))

            def broadcast_gate(name, dgt, whos):
                for who in whos:
                    pe.wait_ge(*e.at("diag", name, who))
                    for n in range(2):
                        ps = new("gbp", name, who, n)
                        m = pe.matmul(ps[:, :], ones, dgt[:, 4 * n:4 * n + 4, :], start=True, stop=True)
                        m.then_inc(*e.inc("gbp", name, who, n))

            def ffn(name, T, with_mods, gate_whos):
                turn_in(name, T, ("xn", name))
                for g in range(GROUPS):
                    if g == 0:
                        pe.wait_ge(*e.at("xT", name, KD - 1))
                    for part in ("gate", "up"):
                        feature_major((name, part, g), T, [(part, name, g, i) for i in range(T // 256)], *xT[T])
                    if with_mods:
                        mod()
                if gate_whos:
                    broadcast_gate(name, dg, gate_whos)
                pe.wait_ge(*e.at("hidden", name, GROUPS - 1, T // 256 - 1))
                hv = (hh[:, 0:KF * T].rearrange("p (k t) -> p k t", t=T),
                      hl[:, 0:KF * T].rearrange("p (k t) -> p k t", t=T))
                i = 0
                for n in range(2):
                    tiles = tiles_of(T)
                    ps = {t: new("down", name, n, t) for t in tiles}
                    for d in range(6):
                        key = (name, "down", n, d)
                        wh, wl = split_ready(key)
                        kt = wh.shape[1]
                        for t in tiles:
                            for k in range(kt):
                                kk = 4 * d + k
                                m = mm3(ps[t][:, :], hv[0][:, kk, t * P:(t + 1) * P],
                                        hv[1][:, kk, t * P:(t + 1) * P], wh[:, k, :], wl[:, k, :],
                                        kk == 0, kk == KF - 1)
                            if d == 5:
                                m.then_inc(*e.inc("down", name, n, t, also=[("used", key)] if t == tiles[-1] else []))
                        if d < 5:
                            m.then_inc(*e.inc("used", key))
                        if with_mods and i < MODS_PER_FFN - GROUPS:
                            mod()
                        i += 1

            pe.wait_ge(L.sem("params_landed"), L.all_params())
            for i in range(4):
                ps = new("cols", i)
                m = pe.transpose(ps[:, 0:ROWS[i]], rowt[0:ROWS[i], i, :], ident[0:ROWS[i], 0:ROWS[i]])
                m.then_inc(*e.inc("cols", i))

            def mixers(l):
                nm = ("mx", l)
                turn_in(nm, 256, ("xn", nm))
                pe.wait_ge(*e.at("xT", nm, KD - 1))
                for i in range(4):
                    feature_major(("xbc", l, i), 256, [("xbc", l, i)], *xT[256])
                token_major([("dt", l)], ("dtp", l), range(2), 8, *xT[256])
                token_major([(("z", l), 0), (("z", l), 1)], ("zp", l), range(2), 512, *xT[256])
                for n in range(2):
                    token_major([(("uv", l, n), 0), (("uv", l, n), 1)], ("uvp", l, n), range(2), 512, *xT[256])
                token_major([(("cq", l), 0), (("cq", l), 1)], ("cqp", l), range(2), 384, *xT[256])
                token_major([(("ckv", l), 0), (("ckv", l), 1)], ("ckvp", l), range(2), 288, *xT[256])
                for t in range(2):
                    pe.wait_ge(*e.at("cv", l))
                    ps = new("xst", l, t)
                    for c in range(4):
                        m = pe.transpose(ps[:, c * P:(c + 1) * P], cv[:, c, t * P:(t + 1) * P], ident)
                    m.then_inc(*e.inc("xst", l, t))
                ps = new("bt", l)
                for g in range(2):
                    m = pe.transpose(ps[:, g * P:(g + 1) * P], cv[:, 4 + g, 0:P], ident)
                m.then_inc(*e.inc("bt", l))
                pe.wait_ge(*e.at("ws", l))
                ps = new("wst", l)
                for g in range(4):
                    m = pe.transpose(ps[:, g * P:(g + 1) * P], ws[:, g, :], ident)
                m.then_inc(*e.inc("wst", l))
                for t in range(2):
                    pe.wait_ge(*e.at("gvn", l, t))
                    if t == 0:
                        pe.wait_ge(*e.at("wT", l))
                    ps = new("spp", l, t)
                    for g in range(4):
                        m = pe.matmul(ps[:, g * P:(g + 1) * P], wT[:, g, :], gv[:, t, g * P:(g + 1) * P],
                                      start=True, stop=True)
                    m.then_inc(*e.inc("spp", l, t))
                for n in range(2):
                    token_major([(("g", l, 2, n), 0), (("g", l, 2, n), 1)], ("gp", l, 2, n), range(2), 512, *xT[256])
                for c in range(2):
                    pe.wait_ge(*e.at("daU", l, c))
                    for h2 in range(2):
                        ps = new("csb", l, c, h2)
                        m = pe.matmul(ps[:, :], ones, E_[:, 4 * h2:4 * h2 + 4, :], start=True, stop=True)
                        m.then_inc(*e.inc("csb", l, c, h2))
                    ps = new("csp", l, c)
                    m = pe.matmul(ps[:, 0:8], upper, small[:, 32 + 8 * c:40 + 8 * c], start=True, stop=True)
                    m = pe.matmul(ps[:, 8:16], ones, small[:, 32 + 8 * c:40 + 8 * c], start=True, stop=True)
                    m.then_inc(*e.inc("csp", l, c))
                    ps = new("cbp", l, c)
                    for g in range(2):
                        m = pe.matmul(ps[:, g * P:(g + 1) * P], cv[:, 4 + g, c * P:(c + 1) * P],
                                      cv[:, 6 + g, c * P:(c + 1) * P], start=True, stop=True)
                    m.then_inc(*e.inc("cbp", l, c))
                    pe.wait_ge(*e.at("MT", l, c))
                    ps = new("yd", l, c)
                    for h in range(8):
                        m = pe.matmul(ps[:, h * 64:(h + 1) * 64], E_[:, h, :], xdt[:, h * 64:(h + 1) * 64],
                                      start=True, stop=True)
                    m.then_inc(*e.inc("yd", l, c))
                    if c == 0:
                        pe.wait_ge(*e.at("btok", l))
                        pe.wait_ge(*e.at("xdd", l))
                        ps = new("stp", l)
                        for g in range(2):
                            m = pe.matmul(ps[:, g * 256:(g + 1) * 256], btok[:, g, :],
                                          xdd[:, g * 256:(g + 1) * 256], start=True, stop=True)
                        m.then_inc(*e.inc("stp", l))
                    else:
                        pe.wait_ge(*e.at("st", l))
                        ps = new("yo", l)
                        for g in range(2):
                            m = pe.matmul(ps[:, g * 256:(g + 1) * 256], cv[:, 6 + g, P:2 * P],
                                          st[:, g * 256:(g + 1) * 256], start=True, stop=True)
                        m.then_inc(*e.inc("yo", l))
                turn_y(("c", l), z, 4, 256, ("yc", l))
                pe.wait_ge(*e.at("yT", ("c", l), 3))
                for n in range(2):
                    token_major([("b", l, 2, n)], ("bp", l, 2, n), range(2), 512, *ytT[0])
                for n in range(2):
                    token_major([(("g", l, 0, n), 0), (("g", l, 0, n), 1)], ("gp", l, 0, n), range(2), 512, *xT[256])
                turn_y(("a", l), gu, 4, 256, ("ya", l))
                pe.wait_ge(*e.at("yT", ("a", l), 1))
                for n in range(2):
                    token_major([("b", l, 0, n)], ("bp", l, 0, n), range(2), 512, *ytT[1])
                turn_y(("cq", l), cq, 3, 256, ("cqn", l))
                turn_y(("ck", l), ckv, 2, 256, ("ckn", l))
                pe.wait_ge(*e.at("yT", ("cq", l), 2))
                for n in range(2):
                    token_major([("q", l, n)], ("qp", l, n), range(2), 384, cqTh, cqTl)
                pe.wait_ge(*e.at("yT", ("ck", l), 1))
                wh, wl = split_ready(("kv", l))
                for n in range(2):
                    for t in range(2):
                        ps = new("kvp", l, n, t)
                        for k in range(2):
                            m = mm3(ps[:, :], ckTh[:, k, t * P:(t + 1) * P], ckTl[:, k, t * P:(t + 1) * P],
                                    wh[:, k, n * 512:(n + 1) * 512], wl[:, k, n * 512:(n + 1) * 512],
                                    k == 0, k == 1)
                        m.then_inc(*e.inc("kvp", l, n, t, also=[("used", ("kv", l))] if n + t == 2 else []))
                for n in range(2):
                    token_major([(("g", l, 1, n), 0), (("g", l, 1, n), 1)], ("gp", l, 1, n), range(2), 512, *xT[256])
                for t in range(2):
                    pe.wait_ge(*e.at("qkr", l, t))
                for h in range(HEADS):
                    ps = new("qkt", l, h)
                    for i in range(2):
                        for t in range(2):
                            m = pe.transpose(ps[0:QK, 256 * i + t * P:256 * i + (t + 1) * P],
                                             qk[:, t, 8 * i + h, :], ident)
                    m.then_inc(*e.inc("qkt", l, h))
                for i in range(HEADS + 2):
                    if i < HEADS:
                        h = i
                        pe.wait_ge(*e.at("qkT", l, h))
                        ps = new("sc", l, h)
                        m = pe.matmul(ps[:, 0:P], qkT[0:QK, h, 0:P], qkT[0:QK, h, 256:384], start=True, stop=True)
                        m = pe.matmul(ps[:, 256:512], qkT[0:QK, h, P:256], qkT[0:QK, h, 256:512],
                                      start=True, stop=True)
                        m.then_inc(*e.inc("sc", l, h))
                    if 1 <= i <= HEADS:
                        h = i - 1
                        pe.wait_ge(*e.at("pr", l, h))
                        ps = new("ptp", l, h)
                        for j in range(3):
                            m = pe.transpose(ps[:, j * P:(j + 1) * P], pr[:, h % 2, j * P:(j + 1) * P], ident)
                        m.then_inc(*e.inc("ptp", l, h))
                    if i >= 2:
                        h = i - 2
                        pe.wait_ge(*e.at("pT", l, h))
                        ps = new("op", l, h)
                        v0, v1 = (kv[:, t, h * P + 64:(h + 1) * P] for t in range(2))
                        m = pe.matmul(ps[:, 0:64], pT[:, 0:P], v0, start=True, stop=True)
                        m = pe.matmul(ps[:, 64:128], pT[:, P:2 * P], v0, start=True, stop=False)
                        m = pe.matmul(ps[:, 64:128], pT[:, 2 * P:3 * P], v1, start=False, stop=True)
                        m.then_inc(*e.inc("op", l, h))
                turn_y(("b", l), yb, 4, 256, ("yb", l))
                pe.wait_ge(*e.at("yT", ("b", l), 1))
                for n in range(2):
                    token_major([("b", l, 1, n)], ("bp", l, 1, n), range(2), 512, *ytT[0])
                turn_y(("m", l), merged, 8, 256, ("mg", l))
                pe.wait_ge(*e.at("yT", ("m", l), 3))
                for n in range(2):
                    token_major([(("wo", l, n), 0), (("wo", l, n), 1)], ("wop", l, n), range(2), 512, *xT[256])

            for l in range(DEPTH):
                ffn(("f1", l), 256, True, ())
                mixers(l)
                ffn(("f2", l), 256, True, ())

            ffn(("g1", 0), 512, False, (0, 1))
            turn_in(("r",), 512, ("xn", ("r",)))
            pe.wait_ge(*e.at("xT", ("r",), KD - 1))
            broadcast_gate(("r",), dgm, (0, 1))
            for h in range(4):
                for part in "qk":
                    feature_major(("r" + part, h), 512, [("r" + part + "p", h, i) for i in range(2)], *xT[512])
                for part in "vg":
                    token_major([(("r" + part, h), 0), (("r" + part, h), 1)], ("r" + part + "p", h),
                                range(4), 512, *xT[512])
                pe.wait_ge(*e.at("rqk", h))
                ps = new("rap", h, 0)
                for jt in range(2):
                    for k in range(2):
                        m = pe.matmul(ps[:, 256 * jt:256 * jt + 256], rk[:, k, jt * P:(jt + 1) * P],
                                      rq[:, k, 0:256], start=k == 0, stop=k == 1, skip_group_check=True)
                m.then_inc(*e.inc("rap", h, 0))
                for jt in range(2):
                    ps = new("rap", h, 1 + jt)
                    for k in range(2):
                        m = pe.matmul(ps[:, :], rk[:, k, 256 + jt * P:256 + (jt + 1) * P], rq[:, k, :],
                                      start=k == 0, stop=k == 1)
                    m.then_inc(*e.inc("rap", h, 1 + jt))
                pe.wait_ge(*e.at("ra", h, 2))
                pe.wait_ge(*e.at("rv", h, 3))
                for t in range(4):
                    ps = new("rop", h, t)
                    if t < 2:
                        pairs = [(ra[:, 0, 256 * jt + t * P:256 * jt + (t + 1) * P], jt) for jt in range(2)]
                        pairs += [(ra[:, 1 + jt, t * P:(t + 1) * P], 2 + jt) for jt in range(2)]
                    else:
                        pairs = [(ra[:, 1 + jt, t * P:(t + 1) * P], 2 + jt) for jt in range(2)]
                    for i, (a, j) in enumerate(pairs):
                        m = pe.matmul(ps[:, :], a, rv[:, j, :], start=i == 0, stop=i == len(pairs) - 1)
                    m.then_inc(*e.inc("rop", h, t))
                turn_y(("r", h), rg, 4, 512, ("ry", h))
                pe.wait_ge(*e.at("yT", ("r", h), 3))
                for n in range(2):
                    token_major([("rw", h, n)], ("rwp", h, n), range(4), 512, rYh, rYl)
            ffn(("g2", 0), 512, False, (0, 1))
            ffn(("g1", 1), 512, False, (0, 1))
            turn_in(("n",), 512, ("xn", ("n",)))
            pe.wait_ge(*e.at("xT", ("n",), KD - 1))
            for j in range(4):
                feature_major(("nq", j), 256, [("nqp", j)], *xT[512])
            for j in range(4):
                feature_major(("nk", j), 512, [("nkp", j, i) for i in range(2)], *xT[512])
            for n in range(2):
                token_major([(("nv", n), 0), (("nv", n), 1)], ("nvp", n), range(4), 512, *xT[512])
            pe.wait_ge(*e.at("nq", 3))
            pe.wait_ge(*e.at("nk", 3, 1))
            pe.wait_ge(*e.at("nv", 1, 3))
            items = [(h, t) for h in range(16) for t in range(2)]
            for i in range(len(items) + 2):
                if i < len(items):
                    h, t = items[i]
                    p0 = 64 * (h % 2)
                    ps = new("nsp", h, t)
                    pe.matmul(ps[:, :], nq[p0:p0 + 64, h // 2, t * P:(t + 1) * P],
                              nk[p0:p0 + 64, h // 2, :], start=True, stop=False, skip_group_check=True)
                    pe.wait_ge(*e.at("nbias", h // 4))
                    m = pe.matmul(ps[:, 0:256], cst[:, C_FLIP:C_FLIP + P], nbias[h // 4 % 2][:, t, h % 4, :],
                                  start=False, stop=True, skip_group_check=True)
                    m.then_inc(*e.inc("nsp", h, t, also=[("nbias_used", h // 4)]))
                if 1 <= i <= len(items):
                    h, t = items[i - 1]
                    pe.wait_ge(*e.at("npr", h, t))
                    ps = new("nptp", h, t)
                    for j in range(4):
                        m = pe.transpose(ps[:, j * P:(j + 1) * P], npr[:, t, j * P:(j + 1) * P], ident)
                    m.then_inc(*e.inc("nptp", h, t))
                if i >= 2:
                    h, t = items[i - 2]
                    pe.wait_ge(*e.at("npT", h, t))
                    ps = new("nop", h, t)
                    for j in range(4):
                        m = pe.matmul(ps[:, 0:64], npT[:, t, j * P:(j + 1) * P], nv[:, j, h * 64:(h + 1) * 64],
                                      start=j == 0, stop=j == 3)
                    m.then_inc(*e.inc("nop", h, t))
            broadcast_gate(("n",), dgm, (0,))
            turn_y(("n",), ny, 8, 256, ("ny",))
            pe.wait_ge(*e.at("yT", ("n",), 3))
            for n in range(2):
                token_major([(("nw", n), 0), (("nw", n), 1)], ("nwp", n), range(2), 512, *xT[256])
            ffn(("g2", 1), 256, False, (0,))

        L.split_keys = [k for k, _, _, _, i in slabs.items if i is not None]
        idx = slabs.index

        def ahead(until, key):
            until(idx[key] + 1)

        @block.scalar
        def _(act):
            e = Signals(L, "act")
            split = [0]

            def until(s):
                while split[0] <= min(s, len(slabs.items) - 1):
                    key, _, kt, n, i = slabs.items[split[0]]
                    split[0] += 1
                    if i is None:
                        continue
                    act.wait_ge(*arrival(key))
                    if i >= NSPLIT:
                        act.wait_ge(*e.at("used", L.split_keys[i - NSPLIT]))
                    m = kt * n
                    nc.scalar.activation(whi[i % NSPLIT][:, 0:m], raw[idx[key] % NRAW][:, 0:m], ACT.Copy).then_inc(*e.inc("hi", key))

            A = nc.scalar.activation

            def norm(name, T):
                for t in tiles_of(T):
                    if t % 2:
                        act.wait_ge(*e.at("X", name, t))
                        if t > 1:
                            act.wait_ge(*e.at("ssa", name, t - 2))
                        A(junk_a[:, :], X[:, t, :], ACT.Square, accum_out=small[:, t:t + 1]).then_inc(*e.inc("ssa", name, t))
                for t in tiles_of(T):
                    if t % 2:
                        act.wait_ge(*e.at("rstd", name))
                        A(xn[:, t, :], X[:, t, :], ACT.Copy, scale=small[:, 8 + t:9 + t]).then_inc(*e.inc("xn", name, t))

            def turned(name, T, gain, bias):
                xTh = xT[T][0]
                for k in range(KD):
                    act.wait_ge(*e.at("turn", name, k))
                    act.wait_ge(*e.at("aff", name))
                    A(xTh[:, k, 0:256], unit("turn", name, k)[:, 0:256], ACT.Identity,
                             scale=gain(k, 0), bias=bias(k, 0) if bias else 0.0).then_inc(*e.inc("xh", name, k, 0))
                    if T == 512:
                        A(xTh[:, k, 256:512], unit("turn", name, k)[:, 256:512], ACT.Identity,
                                 scale=gain(k, 1), bias=bias(k, 1)).then_inc(*e.inc("xh", name, k, 1))

            def turned_y(name, chunks, T, dst, gain=None):
                per = 512 // T
                for u in range((chunks + per - 1) // per):
                    act.wait_ge(*e.at("ty", name, u))
                    if gain is None:
                        m = A(dst[:, u * per:(u + 1) * per, 0:T], unit("ty", name, u)[:, :]
                              .rearrange("p (j t) -> p j t", t=T), ACT.Copy)
                        m.then_inc(*e.inc("yh", name, u))
                    else:
                        for j in range(min(per, chunks - u * per)):
                            c = u * per + j
                            m = A(dst[:, c, 0:T], unit("ty", name, u)[:, j * T:(j + 1) * T], ACT.Copy, scale=gain(c))
                            m.then_inc(*e.inc("yh", name, c))

            def ffn(name, T, gate_whos):
                for g in range(GROUPS):
                    for i in range(T // 256):
                        ahead(until, (name, "gate", g))
                        act.wait_ge(*e.at("gate", name, g, i))
                        b = (g * (T // 256) + i) % 2
                        if (g * (T // 256) + i) >= 2:
                            g2, i2 = divmod(g * (T // 256) + i - 2, T // 256)
                            act.wait_ge(*e.at("hidden", name, g2, i2))
                        A(sg[:, b, :], unit("gate", name, g, i)[:, :], ACT.Silu).then_inc(*e.inc("sg", name, g, i, frees=("gate", name, g, i)))
                    ahead(until, (name, "up", g))
                    for i in range(T // 256):
                        b = (g * (T // 256) + i) % 2
                        o = (g * (T // 256) + i) * 512
                        act.wait_ge(*e.at("ht", name, g, i))
                        A(hh[:, o:o + 512], sg[:, b, :], ACT.Copy).then_inc(*e.inc("hhi", name, g, i))
                for who in gate_whos:
                    for n in range(2):
                        act.wait_ge(*e.at("gbp", name, who, n))
                        A(gb[:, who, n * 512:(n + 1) * 512], unit("gbp", name, who, n)[:, :], ACT.Copy,
                                 scale=0.5).then_inc(*e.inc("gb", name, who, n, frees=("gbp", name, who, n)))
                for n in range(2):
                    for d in range(6):
                        ahead(until, (name, "down", n, d))

            until(0)
            act.wait_ge(L.sem("params_landed"), L.all_params())
            act.wait_ge(*e.at("angles"))
            A(cs16[:, :, :, :], cs16[:, :, :, :], ACT.Sin).then_inc(*e.inc("sincos"))
            act.wait_ge(*e.at("lgx"))
            A(lgs[:, 1, :], lgs[:, 1, :], ACT.Exp).then_inc(*e.inc("lge"))
            A(dtb[:, 1, :, :], dtb[:, 1, :, :], ACT.Exp).then_inc(*e.inc("alog"))
            act.wait_ge(*e.at("cols_copied", 2))
            A(scc[:, :, 0], cols[:, 2, CC:CC + 8], ACT.Silu).then_inc(*e.inc("scc_half", 0))
            A(scc[:, :, 1], cols[:, 2, CC + 8:CC + 16], ACT.Silu).then_inc(*e.inc("scc"))

            gain1 = lambda row: (lambda k, who: col(0, row + k))
            gain2 = lambda k, who: aff[:, k, who:who + 1]

            def bias2(l, j):
                return lambda k, who: modc[:, l, (j * 3) * 8 + k, who:who + 1]

            def mixers(l):
                nm = ("mx", l)
                norm(nm, 256)
                turned(nm, 256, gain1(NORMX + 8 * l), None)
                for i in range(4):
                    ahead(until, ("xbc", l, i))
                    act.wait_ge(*e.at("xbc", l, i))
                    if i == 0:
                        act.wait_ge(*e.at("xr0", l))
                    A(xr[:, 2 * i:2 * i + 2, 3:259], unit("xbc", l, i)[:, :].rearrange("p (m t) -> p m t", m=2),
                             ACT.Copy).then_inc(*e.inc("xr", l, i, frees=("xbc", l, i)))
                ahead(until, ("dt", l))
                ahead(until, (("z", l), 0))
                ahead(until, (("z", l), 1))
                for t in range(2):
                    act.wait_ge(*e.at("zp", l, t))
                    A(z[:, t, :], unit("zp", l, t)[:, :], ACT.Silu).then_inc(*e.inc("z", l, t, frees=("zp", l, t)))
                act.wait_ge(*e.at("dtn", l))
                A(small[:, 64:80], small[:, 64:80], ACT.Exp).then_inc(*e.inc("dte", l))
                for ch in range(8):
                    act.wait_ge(*e.at("conv", l))
                    m = A(cv[:, ch, :], cv[:, ch, :], ACT.Silu, bias=col(1, CVB + 8 * l + ch))
                m.then_inc(*e.inc("cv", l))
                for n in range(2):
                    for half in range(2):
                        ahead(until, (("uv", l, n), half))
                    for t in range(2):
                        act.wait_ge(*e.at("uvp", l, n, t))
                        dst = gv if n else gu
                        A(dst[:, t, :], unit("uvp", l, n, t)[:, :], ACT.Gelu).then_inc(*e.inc("uv", l, n, t, frees=("uvp", l, n, t)))
                for half in range(2):
                    ahead(until, (("cq", l), half))
                for t in range(2):
                    act.wait_ge(*e.at("cqp", l, t))
                    A(cq[:, t, :], unit("cqp", l, t)[:, 0:384], ACT.Copy).then_inc(*e.inc("cq", l, t, frees=("cqp", l, t)))
                for half in range(2):
                    ahead(until, (("ckv", l), half))
                for t in range(2):
                    act.wait_ge(*e.at("ckvp", l, t))
                    A(ckv[:, t, :], unit("ckvp", l, t)[:, 0:288], ACT.Copy).then_inc(*e.inc("ckv", l, t, frees=("ckvp", l, t)))
                for t in range(2):
                    act.wait_ge(*e.at("xst", l, t))
                    A(xs[:, t, :], unit("xst", l, t)[:, :], ACT.Copy).then_inc(*e.inc("xs", l, t, frees=("xst", l, t)))
                act.wait_ge(*e.at("bt", l))
                A(btok[:, :, :], unit("bt", l)[:, 0:256].rearrange("p (g n) -> p g n", g=2), ACT.Copy).then_inc(*e.inc("btok", l, frees=("bt", l)))

                def gate(br):
                    for n in range(2):
                        for half in range(2):
                            ahead(until, (("g", l, br, n), half))
                        for t in range(2):
                            act.wait_ge(*e.at("gp", l, br, n, t))
                            if br != 2:
                                act.wait_ge(*e.at("merged", l, {0: 2, 1: 0}[br], n, t))
                            A(stripe(gates, n, t), unit("gp", l, br, n, t)[:, :], ACT.Sigmoid).then_inc(*e.inc("gate_rows", l, br, n, t, frees=("gp", l, br, n, t)))

                def branch(br):
                    for n in range(2):
                        ahead(until, ("b", l, br, n))

                gate(2)
                for c in range(2):
                    act.wait_ge(*e.at("diff", l, c))
                    A(E_[:, :, :], E_[:, :, :], ACT.Exp).then_inc(*e.inc("expE", l, c))
                    act.wait_ge(*e.at("dec", l, c))
                    A(small[:, 96:112], small[:, 96:112], ACT.Exp).then_inc(*e.inc("expc", l, c))
                    if c == 0:
                        act.wait_ge(*e.at("stp", l))
                        A(st[:, :], unit("stp", l)[:, :], ACT.Copy).then_inc(*e.inc("st", l, frees=("stp", l)))
                turned_y(("c", l), 4, 256, ytT[0][0], lambda c: col(0, SSN + 4 * l + c))
                branch(2)
                gate(0)
                turned_y(("a", l), 4, 256, ytT[1][0])
                branch(0)
                turned_y(("cq", l), 3, 256, cqTh, lambda c: col(0, QN + 3 * l + c))
                turned_y(("ck", l), 2, 256, ckTh, lambda c: col(0, KVN + 2 * l + c))
                for n in range(2):
                    ahead(until, ("q", l, n))
                    for t in range(2):
                        act.wait_ge(*e.at("qp", l, n, t))
                        A(qk[:, t, 4 * n:4 * n + 4, :],
                                 unit("qp", l, n, t)[:, 0:384].rearrange("p (h d) -> p h d", d=QK), ACT.Copy).then_inc(*e.inc("q", l, n, t, frees=("qp", l, n, t)))
                ahead(until, ("kv", l))
                for n in range(2):
                    for t in range(2):
                        act.wait_ge(*e.at("kvp", l, n, t))
                        A(stripe(kv, n, t), unit("kvp", l, n, t)[:, :], ACT.Copy).then_inc(*e.inc("kv", l, n, t, frees=("kvp", l, n, t)))
                gate(1)
                for h in range(HEADS):
                    act.wait_ge(*e.at("qkt", l, h))
                    A(qkT[0:QK, h, :], unit("qkt", l, h)[0:QK, :], ACT.Copy).then_inc(*e.inc("qkT", l, h, frees=("qkt", l, h)))
                for i in range(HEADS + 1):
                    if i < HEADS:
                        h = i
                        act.wait_ge(*e.at("nmax", l, h))
                        if h >= 2:
                            act.wait_ge(*e.at("ptp", l, h - 2))
                        o = 112 + 8 * (h % 2)
                        A(pr[:, h % 2, 0:P], unit("sc", l, h)[:, 0:P], ACT.Exp, scale=QK ** -0.5,
                          bias=small[:, o + 2:o + 3], accum_out=small[:, o + 4:o + 5])
                        m = A(pr[:, h % 2, P:384], unit("sc", l, h)[:, 256:512], ACT.Exp, scale=QK ** -0.5,
                              bias=small[:, o + 3:o + 4], accum_out=small[:, o + 5:o + 6])
                        m.then_inc(*e.inc("pr", l, h, frees=("sc", l, h)))
                    if i >= 1:
                        h = i - 1
                        act.wait_ge(*e.at("ptp", l, h))
                        if h >= 1:
                            act.wait_ge(*e.at("op", l, h - 1))
                        A(pT[:, :], unit("ptp", l, h)[:, 0:384], ACT.Copy).then_inc(*e.inc("pT", l, h, frees=("ptp", l, h)))
                turned_y(("b", l), 4, 256, ytT[0][0])
                branch(1)
                turned_y(("m", l), 8, 256, xT[256][0])
                for n in range(2):
                    for half in range(2):
                        ahead(until, (("wo", l, n), half))

            for l in range(DEPTH):
                norm(("f1", l), 256)
                turned(("f1", l), 256, gain1(NORM1 + 8 * l), None)
                ffn(("f1", l), 256, ())
                mixers(l)
                norm(("f2", l), 256)
                turned(("f2", l), 256, gain1(NORM2 + 8 * l), None)
                ffn(("f2", l), 256, ())

            def block_two_ffn(name, l, j, T, whos):
                norm((name, l), T)
                turned((name, l), T, gain2, bias2(l, j))
                ffn((name, l), T, whos)

            block_two_ffn("g1", 0, 0, 512, (0, 1))
            norm(("r",), 512)
            turned(("r",), 512, gain2, bias2(0, 1))
            for who in range(2):
                for n in range(2):
                    act.wait_ge(*e.at("gbp", ("r",), who, n))
                    A(gbm[:, who, n * 512:(n + 1) * 512], unit("gbp", ("r",), who, n)[:, :], ACT.Copy).then_inc(*e.inc("gb", ("r",), who, n, frees=("gbp", ("r",), who, n)))
            for h in range(4):
                for part, dst in (("q", rq), ("k", rk)):
                    ahead(until, ("r" + part, h))
                    for i in range(2):
                        act.wait_ge(*e.at("r" + part + "p", h, i))
                        if h:
                            act.wait_ge(*e.at("rap", h - 1, 2))
                        A(dst[:, i, 256:512], unit("r" + part + "p", h, i)[:, 256:512], ACT.Copy).then_inc(*e.inc("r" + part + "c", h, i))
                for half in range(2):
                    ahead(until, (("rv", h), half))
                for t in range(4):
                    act.wait_ge(*e.at("rvp", h, t))
                    if h:
                        act.wait_ge(*e.at("rop", h - 1, 3))
                    A(rv[:, t, :], unit("rvp", h, t)[:, :], ACT.Copy).then_inc(*e.inc("rv", h, t, frees=("rvp", h, t)))
                for half in range(2):
                    ahead(until, (("rg", h), half))
                for t in range(4):
                    act.wait_ge(*e.at("rgp", h, t))
                    if h:
                        act.wait_ge(*e.at("ty", ("r", h - 1), 3))
                    A(rg[:, t, :], unit("rgp", h, t)[:, :], ACT.Silu).then_inc(*e.inc("rg", h, t, frees=("rgp", h, t)))
                dist = rcst[:, R_DIST:R_DIST + 512].rearrange("p (j i) -> p j i", j=2)
                act.wait_ge(*e.at("lg"))
                if h:
                    act.wait_ge(*e.at("ra", h - 1, 2))
                act.wait_ge(*e.at("wlog", h))
                A(WX[:, :, 1, :], WX[:, :, 1, :], ACT.Exp)
                A(WX[:, :, 0, :], dist, ACT.Exp, scale=lgs[:, 2, h:h + 1], bias=lgs[:, 3, h:h + 1])
                m = A(wtmp[:, :, 0, :], dist, ACT.Exp, scale=lgs[:, 4, 4 + h:5 + h], bias=lgs[:, 3, 4 + h:5 + h])
                m.then_inc(*e.inc("wexp", h))
                turned_y(("r", h), 4, 512, rYh, lambda c, h=h: col(1, GN + 4 * h + c))
                for n in range(2):
                    ahead(until, ("rw", h, n))
                    if h == 0:
                        for t in range(4):
                            act.wait_ge(*e.at("rwp", 0, n, t))
                            A(stripe(Y, n, t), unit("rwp", 0, n, t)[:, :], ACT.Copy).then_inc(*e.inc("Y0", n, t, frees=("rwp", 0, n, t)))
            block_two_ffn("g2", 0, 2, 512, (0, 1))
            block_two_ffn("g1", 1, 0, 512, (0, 1))
            norm(("n",), 512)
            turned(("n",), 512, gain2, bias2(1, 1))
            for j in range(4):
                ahead(until, ("nq", j))
                act.wait_ge(*e.at("nqp", j))
                A(nq[:, 2 * j:2 * j + 2, :], unit("nqp", j)[:, :].rearrange("p (m t) -> p m t", m=2), ACT.Copy,
                         scale=0.125).then_inc(*e.inc("nq", j, frees=("nqp", j)))
            for j in range(4):
                ahead(until, ("nk", j))
                for i in range(2):
                    act.wait_ge(*e.at("nkp", j, i))
                    A(nk[:, 2 * j + i, :], unit("nkp", j, i)[:, :], ACT.Copy).then_inc(*e.inc("nk", j, i, frees=("nkp", j, i)))
            for n in range(2):
                for half in range(2):
                    ahead(until, (("nv", n), half))
                for t in range(4):
                    act.wait_ge(*e.at("nvp", n, t))
                    A(stripe(nv, n, t), unit("nvp", n, t)[:, :], ACT.Copy).then_inc(*e.inc("nv", n, t, frees=("nvp", n, t)))
            items = [(h, t) for h in range(16) for t in range(2)]
            for i, (h, t) in enumerate(items):
                act.wait_ge(*e.at("nnm", h, t))
                if h:
                    act.wait_ge(*e.at("nptp", h - 1, t))
                o = 128 + 4 * (i % 4)
                m = A(npr[:, t, :], unit("nsp", h, t)[:, :], ACT.Exp, bias=small[:, o + 1:o + 2],
                      accum_out=small[:, o + 2:o + 3])
                m.then_inc(*e.inc("npr", h, t, frees=("nsp", h, t)))
            for n in range(2):
                act.wait_ge(*e.at("gbp", ("n",), 0, n))
                A(gbm[:, 0, n * 512:(n + 1) * 512], unit("gbp", ("n",), 0, n)[:, :], ACT.Copy).then_inc(*e.inc("gb", ("n",), 0, n, frees=("gbp", ("n",), 0, n)))
            turned_y(("n",), 8, 256, xT[256][0])
            for n in range(2):
                for half in range(2):
                    ahead(until, (("nw", n), half))
            block_two_ffn("g2", 1, 2, 256, (0,))
            norm(("last",), 256)

        @block.vector
        def _(dve):
            e = Signals(L, "dve")
            chained = [0]

            def link(ins):
                chained[0] += 1
                ins.then_inc(L.sem("dve_chain"), 1)
                dve.wait_ge(L.sem("dve_chain"), chained[0])

            split = [0]

            def until(s):
                while split[0] <= min(s, len(slabs.items) - 1):
                    key, _, kt, n, i = slabs.items[split[0]]
                    split[0] += 1
                    if i is None:
                        continue
                    dve.wait_ge(*e.at("hi", key))
                    m = kt * n
                    nc.vector.tensor_tensor(wlo[i % NSPLIT][:, 0:m], raw[idx[key] % NRAW][:, 0:m],
                                                   whi[i % NSPLIT][:, 0:m].bitcast(F32), ALU.subtract).then_inc(*e.inc("lo", key))

            V = nc.vector
            TT, TS, STT = V.tensor_tensor, V.tensor_scalar, V.scalar_tensor_tensor
            mods = [0]

            def sumsq(dst, a, junk):
                return V.tensor_tensor_reduce(junk, a, a, 1.0, 0.0, ALU.mult, ALU.add, dst)

            def rstd(name, src, n, width):
                TS(src, src, 1.0 / width, EPS, ALU.mult, ALU.add).then_inc(*e.inc("ms", name))
                dve.wait_ge(*e.at("rstd", name))

            def norm(name, T):
                for t in tiles_of(T):
                    if t % 2 == 0:
                        link(sumsq(small[:, t:t + 1], X[:, t, :], junk_v[:, :]))
                for t in tiles_of(T):
                    if t % 2:
                        dve.wait_ge(*e.at("ssa", name, t))
                rstd(name, small[:, 0:T // P], T // P, D)
                for t in tiles_of(T):
                    if t % 2 == 0:
                        TS(xn[:, t, :], X[:, t, :], small[:, 8 + t:9 + t], None, ALU.mult).then_inc(*e.inc("xn", name, t))

            def turned(name, T, gain, bias):
                xTh, xTl = xT[T]
                for k in range(KD):
                    ps = unit("turn", name, k)
                    dve.wait_ge(*e.at("turn", name, k))
                    whos = range(T // 256) if bias else (0,)
                    dve.wait_ge(*e.at("xh", name, k, whos[-1]))
                    for who in whos:
                        a, b = who * 256, who * 256 + 256
                        m = STT(xTl[:, k, a:b], ps[:, a:b], gain(k, who), xTh[:, k, a:b].bitcast(F32),
                                ALU.mult, ALU.subtract)
                        if bias:
                            link(m)
                            m = TS(xTl[:, k, a:b], xTl[:, k, a:b].bitcast(F32), bias(k, who), None, ALU.add)
                    m.then_inc(*e.inc("xT", name, k, frees=("turn", name, k)))

            def turned_y(name, chunks, T, dsth, dstl, gain=None):
                per = 512 // T
                for u in range((chunks + per - 1) // per):
                    dve.wait_ge(*e.at("ty", name, u))
                    ps = unit("ty", name, u)
                    if gain is None:
                        dve.wait_ge(*e.at("yh", name, u))
                        m = TT(dstl[:, u * per:(u + 1) * per, 0:T], ps[:, :].rearrange("p (j t) -> p j t", t=T),
                               dsth[:, u * per:(u + 1) * per, 0:T].bitcast(F32), ALU.subtract)
                        m.then_inc(*e.inc("yT", name, u, frees=("ty", name, u)))
                    else:
                        n = min(per, chunks - u * per)
                        dve.wait_ge(*e.at("yh", name, u * per + n - 1))
                        for j in range(n):
                            c = u * per + j
                            m = STT(dstl[:, c, 0:T], ps[:, j * T:(j + 1) * T], gain(c),
                                    dsth[:, c, 0:T].bitcast(F32), ALU.mult, ALU.subtract)
                            m.then_inc(*e.inc("yT", name, c, frees=("ty", name, u) if j == n - 1 else None))

            def mod():
                i = mods[0]
                mods[0] += 1
                l, g = divmod(i, 36)
                dve.wait_ge(*e.at("modp", i))
                ps = unit("modp", i)[:, 0:4].rearrange("p (m w) -> p m w", w=2)
                b = cols[:, 2 + l, BM + 2 * g:BM + 2 * g + 2].unsqueeze(2).to_broadcast([P, 2, 2])
                TT(modc[:, l, 2 * g:2 * g + 2, :], ps, b, ALU.add).then_inc(*e.inc("modc", i, frees=("modp", i)))

            def affine(name, l, j):
                g = cols[:, 0, NORMG + 24 * l + 8 * j:NORMG + 24 * l + 8 * j + 8].unsqueeze(2)\
                    .to_broadcast([P, 8, 2])
                m = STT(aff[:, :, :], modc[:, l, (j * 3 + 1) * 8:(j * 3 + 2) * 8, :], 1.0, g, ALU.add, ALU.mult)
                m.then_inc(*e.inc("aff", name))
                dve.wait_ge(*e.at("aff", name))

            def diagonals(name, l, j, dgt, whos):
                for who in whos:
                    if who:
                        dve.wait_ge(*e.at("gbp", name, who - 1, 1))
                    gcol = modc[:, l, (j * 3 + 2) * 8:(j * 3 + 3) * 8, who:who + 1].to_broadcast([P, 8, P])
                    TT(dgt[:, :, :], ident.unsqueeze(1).to_broadcast([P, 8, P]), gcol, ALU.mult).then_inc(*e.inc("diag", name, who))

            def ffn(name, T, with_mods, l=0, j=0, whos=(), nxt=None):
                per = T // 256
                for g in range(GROUPS):
                    ahead(until, (name, "gate", g))
                    ahead(until, (name, "up", g))
                    for i in range(per):
                        b = (g * per + i) % 2
                        o = (g * per + i) * 512
                        dve.wait_ge(*e.at("sg", name, g, i))
                        dve.wait_ge(*e.at("up", name, g, i))
                        TT(sg[:, b, :], sg[:, b, :], unit("up", name, g, i)[:, :], ALU.mult).then_inc(*e.inc("ht", name, g, i, frees=("up", name, g, i)))
                    for i in range(per):
                        b = (g * per + i) % 2
                        o = (g * per + i) * 512
                        dve.wait_ge(*e.at("ht", name, g, i))
                        dve.wait_ge(*e.at("hhi", name, g, i))
                        TT(hl[:, o:o + 512], sg[:, b, :], hh[:, o:o + 512].bitcast(F32), ALU.subtract).then_inc(*e.inc("hidden", name, g, i))
                    if with_mods:
                        mod()
                if whos:
                    dve.wait_ge(*e.at("up", name, GROUPS - 1, per - 1))
                    diagonals(name, l, j, dg, whos)
                i = 0
                for n in range(2):
                    for d in range(6):
                        ahead(until, (name, "down", n, d))
                        if with_mods and i < MODS_PER_FFN - GROUPS:
                            mod()
                        i += 1
                    for t in tiles_of(T):
                        dve.wait_ge(*e.at("down", name, n, t))
                        ps = unit("down", name, n, t)
                        if not whos:
                            m = STT(stripe(X, n, t), ps[:, :], 0.5, stripe(X, n, t), ALU.mult, ALU.add)
                            m.then_inc(*e.inc("Xd", name, n, t, also=[("X", nxt, t)], frees=("down", name, n, t)))
                        else:
                            dve.wait_ge(*e.at("gb", name, t // 2, 1))
                            m = TT(sg[:, t % 2, :], ps[:, :], stripe(gb, n, t // 2), ALU.mult)
                            m.then_inc(*e.inc("sgg", name, n, t, frees=("down", name, n, t)))
                            dve.wait_ge(*e.at("sgg", name, n, t))
                            m = TT(stripe(X, n, t), sg[:, t % 2, :], stripe(X, n, t), ALU.add)
                            m.then_inc(*e.inc("Xd", name, n, t, also=[("X", nxt, t)]))
                dve.wait_ge(*e.at("Xd", name, 1, T // P - 1))

            until(0)
            for i in range(4):
                dve.wait_ge(*e.at("cols", i))
                V.tensor_copy(cols[:, i, 0:ROWS[i]], unit("cols", i)[:, 0:ROWS[i]]).then_inc(*e.inc("cols_copied", i, also=[("aff", n) for n in [("f1", 0), ("f1", 1), ("mx", 0), ("mx", 1), ("f2", 0), ("f2", 1)]], frees=("cols", i)))
            dve.wait_ge(L.sem("params_landed"), L.all_params())
            dve.wait_ge(*e.at("cols_copied", 3))
            pos = bsum[:, 4:6]
            link(V.tensor_copy(pos, bsum[:, 0:2].bitcast(I32)))
            for t in range(2):
                a = cs16[:, t, 0, :]
                r = small[:, 144:160]
                link(TS(a, cst[:, C_FREQ:C_FREQ + 16], bsum[:, 4 + t:5 + t], None, ALU.mult))
                link(TS(r, a, 1.0 / TWO_PI, None, ALU.mult))
                link(TS(r, r, 12582912.0, None, ALU.add))
                link(TS(r, r, -12582912.0, None, ALU.add))
                for c in (TP1, TP2, TP3):
                    link(STT(a, r, -c, a, ALU.mult, ALU.add))
                link(TS(cs16[:, t, 1, :], a, -1.0, None, ALU.mult))
                link(TT(cs16[:, t, 1, :], cs16[:, t, 1, :], a, ALU.min))
                link(TS(cs16[:, t, 1, :], cs16[:, t, 1, :], TWO_PI / 4, None, ALU.add))
                TS(a, a, 3.1415925, -3.1415925, ALU.min, ALU.max).then_inc(*e.inc("angles"))

            def log1p(x, s, y, q):
                link(TS(s, x, 2.0, None, ALU.add))
                link(V.reciprocal(s, s))
                link(TT(s, s, x, ALU.mult))
                link(TT(y, s, s, ALU.mult))
                link(TS(q, y, 1.0 / 17, None, ALU.mult))
                for k in (15, 13, 11, 9, 7, 5, 3):
                    link(STT(q, q, 1.0 / k, y, ALU.add, ALU.mult))
                link(STT(q, q, 1.0, s, ALU.add, ALU.mult))
                return q

            d = lgs[:, 0, :]
            link(TS(lgs[:, 1, :], d, -1.0, None, ALU.mult))
            TT(lgs[:, 1, :], lgs[:, 1, :], d, ALU.min).then_inc(*e.inc("lgx"))
            dve.wait_ge(*e.at("lge"))
            q = log1p(lgs[:, 1, :], lgs[:, 5, :], lgs[:, 6, :], lgs[:, 7, :])
            link(TS(d, d, 0.0, None, ALU.min))
            link(STT(lgs[:, 2, :], q, -2.0, d, ALU.mult, ALU.add))
            link(TS(lgs[:, 3, :], lgs[:, 2, :], 256.0, None, ALU.mult))
            TS(lgs[:, 4, :], lgs[:, 2, :], -1.0, None, ALU.mult).then_inc(*e.inc("lg"))
            dve.wait_ge(*e.at("lg"))
            dve.wait_ge(*e.at("alog"))
            link(TS(dtb[:, 1, :, :], dtb[:, 1, :, :], -1.0, None, ALU.mult))

            gain1 = lambda row: (lambda k, who: col(0, row + k))
            gain2 = lambda k, who: aff[:, k, who:who + 1]

            def bias2(l, j):
                return lambda k, who: modc[:, l, (j * 3) * 8 + k, who:who + 1]

            def heads(a, n, width):
                return a.unsqueeze(2).to_broadcast([P, n, width])

            def mixers(l):
                nm = ("mx", l)
                norm(nm, 256)
                turned(nm, 256, gain1(NORMX + 8 * l), None)
                for i in range(4):
                    ahead(until, ("xbc", l, i))
                ahead(until, ("dt", l))
                dtv, dte = small[:, 16:32], small[:, 64:80]
                for t in range(2):
                    dve.wait_ge(*e.at("dtp", l, t))
                    m = TT(small[:, 16 + 8 * t:24 + 8 * t], unit("dtp", l, t)[:, 0:8], dtb[:, 0, l, :], ALU.add)
                    m.then_inc(*e.inc("dtr", l, t, frees=("dtp", l, t)))
                    dve.wait_ge(*e.at("dtr", l, t))
                link(TS(dte, dtv, -1.0, None, ALU.mult))
                TT(dte, dte, dtv, ALU.min).then_inc(*e.inc("dtn", l))
                for i in range(4):
                    dve.wait_ge(*e.at("xr", l, i))
                for tap in range(4):
                    for ch in range(8):
                        wc = col(1, CVW + 32 * l + 8 * tap + ch)
                        src = xr[:, ch, tap:tap + 256]
                        if tap == 0:
                            m = TS(cv[:, ch, :], src, wc, None, ALU.mult)
                        else:
                            m = STT(cv[:, ch, :], src, wc, cv[:, ch, :], ALU.mult, ALU.add)
                    if tap < 3:
                        link(m)
                    else:
                        m.then_inc(*e.inc("conv", l))
                    ahead(until, (("z", l), tap % 2))
                dve.wait_ge(*e.at("dte", l))
                q = log1p(dte, small[:, 160:176], small[:, 176:192], small[:, 192:208])
                link(TS(dtv, dtv, 0.0, None, ALU.max))
                link(STT(dtv, q, 2.0, dtv, ALU.mult, ALU.add))
                for t in range(2):
                    link(TT(small[:, 32 + 8 * t:40 + 8 * t], small[:, 16 + 8 * t:24 + 8 * t], dtb[:, 1, l, :], ALU.mult))
                for n in range(2):
                    for half in range(2):
                        ahead(until, (("uv", l, n), half))
                for half in range(2):
                    ahead(until, (("cq", l), half))
                for half in range(2):
                    ahead(until, (("ckv", l), half))
                for t in range(2):
                    dve.wait_ge(*e.at("uv", l, 1, t))
                    link(sumsq(small[:, 48 + t:49 + t], gv[:, t, :], junk512))
                rstd(("gv", l), small[:, 48:50], 2, 512)
                dve.wait_ge(L.sem("vgain_landed"), 16 * (l + 1))
                for t in range(2):
                    STT(gv[:, t, :], gv[:, t, :], small[:, 50 + t:51 + t], vgain[:, :], ALU.mult, ALU.mult).then_inc(*e.inc("gvn", l, t))
                for name, a, n, s in (("cq", cq, 384, 208), ("ck", ckv, 256, 212)):
                    for t in range(2):
                        dve.wait_ge(*e.at({"cq": "cq", "ck": "ckv"}[name], l, t))
                        link(sumsq(small[:, s + t:s + t + 1], a[:, t, 0:n], junk512[:, 0:n]))
                    rstd((name, l), small[:, s:s + 2], 2, n)
                    for t in range(2):
                        TS(a[:, t, 0:n], a[:, t, 0:n], small[:, s + 2 + t:s + 3 + t], None, ALU.mult).then_inc(*e.inc(name + "n", l, t))
                dve.wait_ge(*e.at("wst", l))
                TT(wT[:, :, :], unit("wst", l)[:, :].rearrange("p (g t) -> p g t", g=4),
                          upper.unsqueeze(1).to_broadcast([P, 4, P]), ALU.mult).then_inc(*e.inc("wT", l, frees=("wst", l)))
                for t in range(2):
                    dve.wait_ge(*e.at("spp", l, t))
                    dve.wait_ge(*e.at("uv", l, 0, t))
                    ps = unit("spp", l, t)
                    for g in range(4):
                        s = slice(g * P, (g + 1) * P)
                        m = STT(gu[:, t, s], ps[:, s], col(1, BS + 4 * l + g), gu[:, t, s], ALU.add, ALU.mult)
                    m.then_inc(*e.inc("ya", l, t, frees=("spp", l, t)))

                def gate(br):
                    for n in range(2):
                        for half in range(2):
                            ahead(until, (("g", l, br, n), half))

                def branch(br):
                    for n in range(2):
                        ahead(until, ("b", l, br, n))
                        for t in range(2):
                            dve.wait_ge(*e.at("bp", l, br, n, t))
                            dve.wait_ge(*e.at("gate_rows", l, br, n, t))
                            ps = unit("bp", l, br, n, t)
                            if br == 2:
                                TT(stripe(merged, n, t), ps[:, :], stripe(gates, n, t), ALU.mult).then_inc(*e.inc("merged", l, br, n, t, also=[("bfree", l, br, n, t)], frees=("bp", l, br, n, t)))
                            else:
                                m = TT(tmp[:, t, :], ps[:, :], stripe(gates, n, t), ALU.mult)
                                m.then_inc(*e.inc("mtmp", l, br, n, t, frees=("bp", l, br, n, t)))
                                dve.wait_ge(*e.at("mtmp", l, br, n, t))
                                TT(stripe(merged, n, t), tmp[:, t, :], stripe(merged, n, t), ALU.add).then_inc(*e.inc("merged", l, br, n, t, also=[("mg", l, t)] if br == 1 and n == 1 else []))

                for c in range(2):
                    t = c
                    if c:
                        dve.wait_ge(*e.at("yd", l, 0))
                    TT(E_[:, :, :], upper.unsqueeze(1).to_broadcast([P, 8, P]),
                              heads(small[:, 32 + 8 * c:40 + 8 * c], 8, P), ALU.mult).then_inc(*e.inc("daU", l, c))
                    if c == 0:
                        gate(2)
                    dve.wait_ge(*e.at("xs", l, t))
                    if c:
                        dve.wait_ge(*e.at("stp", l))
                    link(TT(xdt[:, :].rearrange("p (h d) -> p h d", d=64),
                              xs[:, t, :].rearrange("p (h d) -> p h d", d=64),
                              heads(small[:, 16 + 8 * c:24 + 8 * c], 8, 64), ALU.mult))
                    dve.wait_ge(*e.at("csp", l, c))
                    csc = small[:, 80:96]
                    V.tensor_copy(csc, unit("csp", l, c)[:, 0:16]).then_inc(*e.inc("csc", l, c, frees=("csp", l, c)))
                    dve.wait_ge(*e.at("csc", l, c))
                    V.tensor_copy(small[:, 96:104], csc[:, 0:8])
                    TT(small[:, 104:112], csc[:, 8:16], csc[:, 0:8], ALU.subtract).then_inc(*e.inc("dec", l, c))
                    for h2 in range(2):
                        dve.wait_ge(*e.at("csb", l, c, h2))
                    for h2 in range(2):
                        for h in range(4):
                            m = TS(E_[:, 4 * h2 + h, :], unit("csb", l, c, h2)[:, h * P:(h + 1) * P],
                                   csc[:, 4 * h2 + h:4 * h2 + h + 1], 0.0, ALU.subtract, ALU.min)
                        m.then_inc(*e.inc("diff_half", l, c, h2, also=[("diff", l, c)], frees=("csb", l, c, h2)))
                    dve.wait_ge(*e.at("cbp", l, c))
                    TT(cbm[:, :, :], unit("cbp", l, c)[:, 0:256].rearrange("p (g t) -> p g t", g=2),
                              upper.unsqueeze(1).to_broadcast([P, 2, P]), ALU.mult).then_inc(*e.inc("cbm", l, c, frees=("cbp", l, c)))
                    dve.wait_ge(*e.at("expE", l, c))
                    dve.wait_ge(*e.at("cbm", l, c))
                    for g in range(2):
                        m = TT(E_[:, 4 * g:4 * g + 4, :], E_[:, 4 * g:4 * g + 4, :],
                               cbm[:, g:g + 1, :].to_broadcast([P, 4, P]), ALU.mult)
                    m.then_inc(*e.inc("MT", l, c))
                    dve.wait_ge(*e.at("expc", l, c))
                    h64 = lambda a: a.rearrange("p (h d) -> p h d", d=64)
                    if c == 0:
                        TT(h64(xdd[:, :]), h64(xdt[:, :]), heads(small[:, 104:112], 8, 64), ALU.mult).then_inc(*e.inc("xdd", l))
                    link(TT(h64(tmp[:, 0, :]), h64(xs[:, t, :]), heads(dtb[:, 2, l, :], 8, 64), ALU.mult))
                    dve.wait_ge(*e.at("yd", l, c))
                    m = TT(tmp[:, 0, :], unit("yd", l, c)[:, :], tmp[:, 0, :], ALU.add)
                    m.then_inc(*e.inc("yd_in", l, c, frees=("yd", l, c)))
                    dve.wait_ge(*e.at("yd_in", l, c))
                    if c:
                        dve.wait_ge(*e.at("yo", l))
                        m = TT(h64(tmp[:, 1, :]), h64(unit("yo", l)[:, :]), heads(small[:, 96:104], 8, 64), ALU.mult)
                        m.then_inc(*e.inc("yo_in", l, frees=("yo", l)))
                        dve.wait_ge(*e.at("yo_in", l))
                        link(TT(tmp[:, 0, :], tmp[:, 0, :], tmp[:, 1, :], ALU.add))
                    dve.wait_ge(*e.at("z", l, t))
                    link(TT(z[:, t, :], z[:, t, :], tmp[:, 0, :], ALU.mult))
                    for g in range(2):
                        link(sumsq(small[:, 216 + g:217 + g], z[:, t, g * 256:(g + 1) * 256], tmp[:, 1, 0:256]))
                    rstd(("yc", l, c), small[:, 216:218], 2, 256)
                    for g in range(2):
                        m = TS(z[:, t, g * 256:(g + 1) * 256], z[:, t, g * 256:(g + 1) * 256],
                               small[:, 218 + g:219 + g], None, ALU.mult)
                    m.then_inc(*e.inc("yc", l, c))
                turned_y(("c", l), 4, 256, *ytT[0], gain=lambda c: col(0, SSN + 4 * l + c))
                branch(2)
                gate(0)
                turned_y(("a", l), 4, 256, *ytT[1])
                branch(0)
                turned_y(("cq", l), 3, 256, cqTh, cqTl, lambda c: col(0, QN + 3 * l + c))
                turned_y(("ck", l), 2, 256, ckTh, ckTl, lambda c: col(0, KVN + 2 * l + c))
                for n in range(2):
                    ahead(until, ("q", l, n))
                ahead(until, ("kv", l))
                for n in range(2):
                    for t in range(2):
                        dve.wait_ge(*e.at("q", l, n, t))
                        dve.wait_ge(*e.at("kv", l, n, t))
                for t in range(2):
                    kk = kv[:, t, :].rearrange("p (h d) -> p h d", d=P)
                    V.tensor_copy(qk[:, t, 8:16, 0:64], kk[:, :, 0:64])
                    link(V.tensor_copy(qk[:, t, 8:16, 64:96],
                                         ckv[:, t, 256:288].unsqueeze(1).to_broadcast([P, 8, 32])))
                for t in range(2):
                    a = qk[:, t, :, :]
                    link(TT(sq[:, :, :], a, a, ALU.mult))
                    link(V.tensor_reduce(small[:, 224:240], sq[:, :, :], AX, ALU.add))
                    rstd(("qk", l, t), small[:, 224:240], 16, QK)
                    link(TT(a, a, heads(small[:, 240:256], 16, QK), ALU.mult))
                    for i in range(2):
                        m = TT(qk[:, t, 8 * i:8 * i + 8, :], qk[:, t, 8 * i:8 * i + 8, :],
                               qkg[:, l, i:i + 1, :].to_broadcast([P, 8, QK]), ALU.mult)
                    link(m)
                    x1, x2 = a[:, :, 64:80], a[:, :, 80:96]
                    sn, cn = (cs16[:, t, i:i + 1, :].to_broadcast([P, 16, 16]) for i in range(2))
                    dve.wait_ge(*e.at("sincos"))
                    q4 = [sq[:, :, 16 * i:16 * i + 16] for i in range(4)]
                    TT(q4[0], x1, cn, ALU.mult)
                    TT(q4[1], x2, sn, ALU.mult)
                    TT(q4[2], x2, cn, ALU.mult)
                    link(TT(q4[3], x1, sn, ALU.mult))
                    TT(x1, q4[0], q4[1], ALU.subtract)
                    TT(x2, q4[2], q4[3], ALU.add).then_inc(*e.inc("qkr", l, t))
                    dve.wait_ge(*e.at("qkr", l, t))
                    if t == 0:
                        ahead(until, (("g", l, 1, 0), 0))
                gate(1)
                for i in range(HEADS + 2):
                    if i < HEADS:
                        h = i
                        o = 112 + 8 * (h % 2)
                        dve.wait_ge(*e.at("sc", l, h))
                        ps = unit("sc", l, h)
                        dv = ps[:, :].rearrange("p (a b) -> p a b", b=P)[:, 0:4:3, :]
                        link(TT(dv, dv, cst[:, C_CAUSAL:C_CAUSAL + P].unsqueeze(1).to_broadcast([P, 2, P]), ALU.add))
                        V.tensor_reduce(small[:, o:o + 1], ps[:, 0:P], AX, ALU.max)
                        link(V.tensor_reduce(small[:, o + 1:o + 2], ps[:, 256:512], AX, ALU.max))
                        TS(small[:, o + 2:o + 4], small[:, o:o + 2], -QK ** -0.5, None, ALU.mult).then_inc(*e.inc("nmax", l, h))
                    if i >= 2:
                        h = i - 2
                        o = 112 + 8 * (h % 2)
                        dve.wait_ge(*e.at("op", l, h))
                        for t in range(2):
                            m = TS(yb[:, t, h * 64:(h + 1) * 64], unit("op", l, h)[:, 64 * t:64 * t + 64],
                                   small[:, o + 6 + t:o + 7 + t], None, ALU.mult)
                        m.then_inc(*e.inc("yb_head", l, h, also=[("yb", l, 0), ("yb", l, 1)], frees=("op", l, h)))
                    if 1 <= i <= HEADS:
                        h = i - 1
                        o = 112 + 8 * (h % 2)
                        dve.wait_ge(*e.at("pr", l, h))
                        link(V.reciprocal(small[:, o + 6:o + 8], small[:, o + 4:o + 6]))
                turned_y(("b", l), 4, 256, *ytT[0])
                branch(1)
                turned_y(("m", l), 8, 256, *xT[256])
                for n in range(2):
                    for half in range(2):
                        ahead(until, (("wo", l, n), half))
                    for t in range(2):
                        dve.wait_ge(*e.at("wop", l, n, t))
                        m = TT(stripe(X, n, t), unit("wop", l, n, t)[:, :], stripe(X, n, t), ALU.add)
                        m.then_inc(*e.inc("Xw", l, n, t, also=[("X", ("f2", l), t)], frees=("wop", l, n, t)))
                dve.wait_ge(*e.at("Xw", l, 1, 1))

            junk512 = tmp[:, 1, :]
            for l in range(DEPTH):
                if l == 0:
                    dve.wait_ge(L.sem("x_landed"), 16)
                    V.memset(small[:, 0:4], 0.0).then_inc(*e.inc("X", ("f1", 0), 1))
                    dve.wait_ge(*e.at("X", ("f1", 0), 1))
                norm(("f1", l), 256)
                turned(("f1", l), 256, gain1(NORM1 + 8 * l), None)
                ffn(("f1", l), 256, True, nxt=("mx", l))
                mixers(l)
                norm(("f2", l), 256)
                turned(("f2", l), 256, gain1(NORM2 + 8 * l), None)
                ffn(("f2", l), 256, True, nxt=("f1", l + 1) if l == 0 else ("g1", 0))

            def block_two_ffn(name, l, j, T, whos, nxt):
                nm = (name, l)
                if nm == ("g1", 0):
                    V.memset(small[:, 0:4], 0.0).then_inc(*e.inc("ctx_ready", also=[("X", nm, t) for t in (1, 3)]))
                    dve.wait_ge(*e.at("ctx_ready"))
                affine(nm, l, j)
                norm(nm, T)
                turned(nm, T, gain2, bias2(l, j))
                ffn(nm, T, False, l, j, whos, nxt)

            block_two_ffn("g1", 0, 0, 512, (0, 1), ("r",))
            affine(("r",), 0, 1)
            norm(("r",), 512)
            turned(("r",), 512, gain2, bias2(0, 1))
            diagonals(("r",), 0, 1, dgm, (0, 1))
            dist = rcst[:, R_DIST:R_DIST + 512].rearrange("p (j i) -> p j i", j=2)
            cosT, sinT = rcst[:, R_COS:R_COS + 256], rcst[:, R_SIN:R_SIN + 256]
            dve.wait_ge(L.sem("rcst_landed"), 16)
            for h in range(4):
                for part, dst in (("q", rq), ("k", rk)):
                    ahead(until, ("r" + part, h))
                    p0, p1 = (unit("r" + part + "p", h, i)[:, 0:256] for i in range(2))
                    for i in range(2):
                        dve.wait_ge(*e.at("r" + part + "c", h, i))
                    if h:
                        dve.wait_ge(*e.at("rap", h - 1, 2))
                    r0, r1 = rt[:, 0, 0:256], rt[:, 0, 256:512]
                    TT(dst[:, 0, 0:256], p0, cosT, ALU.mult)
                    TT(r0, p1, sinT, ALU.mult)
                    TT(dst[:, 1, 0:256], p1, cosT, ALU.mult)
                    link(TT(r1, p0, sinT, ALU.mult))
                    TT(dst[:, 0, 0:256], dst[:, 0, 0:256], r0, ALU.subtract)
                    m = TT(dst[:, 1, 0:256], dst[:, 1, 0:256], r1, ALU.add)
                    m.then_inc(*e.inc("rope", h, part, also=[("rqk", h)], frees=("r" + part + "p", h, 0)))
                    L.freed[("r" + part + "p", h, 1)] = L.events[("rope", h, part)]
                    dve.wait_ge(*e.at("rope", h, part))
                for part in "vg":
                    for half in range(2):
                        ahead(until, (("r" + part, h), half))
                if h:
                    dve.wait_ge(*e.at("ra", h - 1, 2))
                V.tensor_scalar(WX[:, :, 1, :], dist, 0.0, lgs[:, 2, h:h + 1], ALU.max, ALU.mult)
                link(V.tensor_scalar(wtmp[:, :, 1, :], dist, 0.0, lgs[:, 4, 4 + h:5 + h], ALU.min, ALU.mult))
                TT(WX[:, :, 1, :], WX[:, :, 1, :], wtmp[:, :, 1, :], ALU.add).then_inc(*e.inc("wlog", h))
                dve.wait_ge(*e.at("wexp", h))
                link(TT(WX[:, :, 0, :], WX[:, :, 0, :], wtmp[:, :, 0, :], ALU.add))
                if h:
                    dve.wait_ge(*e.at("rop", h - 1, 3))
                for u in range(3):
                    dve.wait_ge(*e.at("rap", h, u))
                    ps = unit("rap", h, u)[:, :].rearrange("p (a i) -> p a i", a=2)
                    wv = WX[:, :, 1, :] if u == 0 else WX[:, u - 1, :, :]
                    STT(ra[:, u, :].rearrange("p (a i) -> p a i", a=2), ps, 1.0 / 16, wv, ALU.mult, ALU.mult).then_inc(*e.inc("ra", h, u, frees=("rap", h, u)))
                for t in range(4):
                    o = 144 + 16 * (t % 2)
                    dve.wait_ge(*e.at("rop", h, t))
                    ps = unit("rop", h, t)
                    link(V.bn_stats(small[:, o:o + 6], ps[:, :]))
                    link(V.bn_aggr(small[:, o + 6:o + 8], small[:, o:o + 6]))
                    rstd(("ro", h, t), small[:, o + 7:o + 8], 1, 1)
                    m = TS(rt[:, t % 2, :], ps[:, :], small[:, o + 6:o + 7], small[:, o + 8:o + 9],
                           ALU.subtract, ALU.mult)
                    m.then_inc(*e.inc("rn", h, t, frees=("rop", h, t)))
                    dve.wait_ge(*e.at("rn", h, t))
                    dve.wait_ge(*e.at("rg", h, t))
                    TT(rg[:, t, :], rg[:, t, :], rt[:, t % 2, :], ALU.mult).then_inc(*e.inc("ry", h, t))
                turned_y(("r", h), 4, 512, rYh, rYl, lambda c, h=h: col(1, GN + 4 * h + c))
                for n in range(2):
                    ahead(until, ("rw", h, n))
                    for t in range(4):
                        if h:
                            dve.wait_ge(*e.at("rwp", h, n, t))
                            if h == 1:
                                dve.wait_ge(*e.at("Y0", n, t))
                            TT(stripe(Y, n, t), unit("rwp", h, n, t)[:, :], stripe(Y, n, t), ALU.add).then_inc(*e.inc("Y", h, n, t, frees=("rwp", h, n, t)))
            dve.wait_ge(*e.at("Y", 3, 1, 3))
            for t in range(4):
                dve.wait_ge(*e.at("gb", ("r",), t // 2, 1))
                link(TT(Y[:, t, :], Y[:, t, :], gbm[:, t // 2, :], ALU.mult))
                TT(X[:, t, :], X[:, t, :], Y[:, t, :], ALU.add).then_inc(*e.inc("Xr", t, also=[("X", ("g2", 0), t)]))
            dve.wait_ge(*e.at("Xr", 3))
            block_two_ffn("g2", 0, 2, 512, (0, 1), ("g1", 1))
            block_two_ffn("g1", 1, 0, 512, (0, 1), ("n",))
            affine(("n",), 1, 1)
            norm(("n",), 512)
            turned(("n",), 512, gain2, bias2(1, 1))
            for j in range(4):
                ahead(until, ("nq", j))
            for j in range(4):
                ahead(until, ("nk", j))
            for n in range(2):
                for half in range(2):
                    ahead(until, (("nv", n), half))
            diagonals(("n",), 1, 1, dgm, (0,))
            items = [(h, t) for h in range(16) for t in range(2)]
            for i in range(len(items) + 2):
                if i < len(items):
                    h, t = items[i]
                    o = 128 + 4 * (i % 4)
                    dve.wait_ge(*e.at("nsp", h, t))
                    ps = unit("nsp", h, t)
                    link(V.tensor_reduce(small[:, o:o + 1], ps[:, :], AX, ALU.max))
                    TS(small[:, o + 1:o + 2], small[:, o:o + 1], -1.0, None, ALU.mult).then_inc(*e.inc("nnm", h, t))
                if i >= 2:
                    h, t = items[i - 2]
                    o = 128 + 4 * ((i - 2) % 4)
                    dve.wait_ge(*e.at("nop", h, t))
                    TS(ny[:, t, h * 64:(h + 1) * 64], unit("nop", h, t)[:, 0:64], small[:, o + 3:o + 4], None,
                              ALU.mult).then_inc(*e.inc("ny_head", h, t, also=[("ny", t)], frees=("nop", h, t)))
                if 1 <= i <= len(items):
                    h, t = items[i - 1]
                    o = 128 + 4 * ((i - 1) % 4)
                    dve.wait_ge(*e.at("npr", h, t))
                    link(V.reciprocal(small[:, o + 3:o + 4], small[:, o + 2:o + 3]))
                    dve.wait_ge(*e.at("nptp", h, t))
                    if h:
                        dve.wait_ge(*e.at("nop", h - 1, t))
                    V.tensor_copy(npT[:, t, :], unit("nptp", h, t)[:, :]).then_inc(*e.inc("npT", h, t, frees=("nptp", h, t)))
            turned_y(("n",), 8, 256, *xT[256])
            for n in range(2):
                for half in range(2):
                    ahead(until, (("nw", n), half))
                for t in range(2):
                    dve.wait_ge(*e.at("nwp", n, t))
                    dve.wait_ge(*e.at("gb", ("n",), 0, n))
                    if n or t:
                        dve.wait_ge(*e.at("Xn", *divmod(2 * n + t - 1, 2)))
                    TT(nt[:, :], unit("nwp", n, t)[:, :], stripe(gbm, n, 0), ALU.mult).then_inc(*e.inc("nt", n, t, frees=("nwp", n, t)))
                    dve.wait_ge(*e.at("nt", n, t))
                    TT(stripe(X, n, t), stripe(X, n, t), nt[:, :], ALU.add).then_inc(*e.inc("Xn", n, t, also=[("X", ("g2", 1), t)]))
            dve.wait_ge(*e.at("Xn", 1, 1))
            block_two_ffn("g2", 1, 2, 256, (0,), ("last",))
            norm(("last",), 256)
            dve.wait_ge(L.sem("fg_landed"), 16)
            for t in range(2):
                dve.wait_ge(*e.at("xn", ("last",), t))
                TT(fo[:, t, :], xn[:, t, :], fg[:, :], ALU.mult).then_inc(*e.inc("out_row", t))

        @block.gpsimd
        def _(pool):
            e = Signals(L, "pool")
            minus_half = bsum[:, 8:9]

            def rstd(name, dst, src, n):
                pool.wait_ge(*e.at("ms", name))
                nc.gpsimd.tensor_tensor(dst, src, minus_half.to_broadcast([P, n]), ALU.pow).then_inc(*e.inc("rstd", name))

            def norm(name, T):
                rstd(name, small[:, 8:8 + T // P], small[:, 0:T // P], T // P)

            nc.gpsimd.memset(minus_half, -0.5).then_inc(L.sem("minus_half"), 1)
            pool.wait_ge(L.sem("minus_half"), 1)
            norm(("f1", 0), 256)
            for l in range(DEPTH):
                if l:
                    norm(("f1", l), 256)
                norm(("mx", l), 256)
                pool.wait_ge(*e.at("turn", ("mx", l), KD - 1))
                nc.gpsimd.memset(xr[:, :, 0:3], 0.0).then_inc(*e.inc("xr0", l))
                if l:
                    pool.wait_ge(*e.at("gvn", l - 1, 1))
                pool.dma_start(vgain[:, :], wide_row(w["gm_v_norm"][l], 512)).then_inc(L.sem("vgain_landed"), 16)
                pool.dma_start(ws[:, :, :], w["gm_w_s"][l].rearrange("g t s -> t g s"))\
                    .then_inc(L.sem("ws_landed"), 16)
                L.events[("ws", l)] = ("ws_landed", 16 * (l + 1))
                rstd(("gv", l), small[:, 50:52], small[:, 48:50], 2)
                rstd(("cq", l), small[:, 210:212], small[:, 208:210], 2)
                rstd(("ck", l), small[:, 214:216], small[:, 212:214], 2)
                for c in range(2):
                    rstd(("yc", l, c), small[:, 218:220], small[:, 216:218], 2)
                for t in range(2):
                    rstd(("qk", l, t), small[:, 240:256], small[:, 224:240], 16)
                norm(("f2", l), 256)
            norm(("g1", 0), 512)
            norm(("r",), 512)
            pool.dma_start(rcst[:, :], consts["rcst"]).then_inc(L.sem("rcst_landed"), 16)
            for h in range(4):
                for t in range(4):
                    o = 144 + 16 * (t % 2)
                    rstd(("ro", h, t), small[:, o + 8:o + 9], small[:, o + 7:o + 8], 1)
            norm(("g2", 0), 512)
            norm(("g1", 1), 512)
            norm(("n",), 512)
            rpb = w["nat_rpb_2"]
            for q4 in range(4):
                if q4 >= 2:
                    pool.wait_ge(*e.at("nbias_used", q4 - 2))
                else:
                    pool.wait_ge(*e.at("xT", ("n",), KD - 1))
                b = nbias[q4 % 2]
                for t in range(2):
                    for r in range(2):
                        for h in range(4):
                            off = rpb.offset + (4 * q4 + h) * 465 + (7 - 2 * t - r) * 31 + 15 - 63
                            pool.dma_start(b[64 * r:64 * r + 64, t, h, :].rearrange("p (a c) -> p a c", a=4),
                                           bass.AP(rpb.tensor, off, [[1, 64], [31, 4], [1, 64]]))\
                                .then_inc(L.sem(f"bias{q4 % 2}_landed"), 16)
                pool.wait_ge(L.sem(f"bias{q4 % 2}_landed"), 256 * (q4 // 2 + 1))
                mask = cst[:, C_NAT:C_NAT + 64].unsqueeze(1).to_broadcast([P, 32, 64])
                bv = b[:, :, :, :].rearrange("p t h (a c) -> p (t h a) c", c=64)
                nc.gpsimd.tensor_tensor(bv, bv, mask, ALU.add).then_inc(*e.inc("nbias", q4))
            norm(("g2", 1), 256)
            pool.dma_start(fg[:, :], wide_row(w["final_norm_g_2"], D)).then_inc(L.sem("fg_landed"), 16)
            norm(("last",), 256)
    return L


_INS = ["x", "positions", "ffn1_norm", "ffn1_w_in", "ffn1_w_out", "mix_norm", "w_in", "gm_v_norm", "gm_w_s", "gm_b_s",
        "mla_q_norm", "mla_kv_norm", "mla_w_uq", "mla_w_ukv", "mla_q_gain", "mla_k_gain", "ssd_conv_w",
        "ssd_conv_b", "ssd_dt_bias", "ssd_a_log", "ssd_d", "ssd_norm", "w_branch", "w_out", "ffn2_norm", "ffn2_w_in",
        "ffn2_w_out", "c_2", "ctx_2", "c_ctx_2", "w_mod_2", "b_mod_2", "norm_g_2", "ffn_w_in_2", "ffn_w_out_2",
        "ret_w_in_2", "ret_w_out_2", "ret_gn_g_2", "ret_decay_f_2", "ret_decay_b_2", "nat_w_qkv_2", "nat_w_o_2",
        "nat_rpb_2", "final_norm_g_2"]


def constants():
    import numpy as np
    i = np.arange(P)
    cst = np.zeros((P, C_END), np.float32)
    cst[:, C_IDENT:C_IDENT + P] = np.eye(P)
    cst[:, C_U:C_U + P] = i[:, None] <= i[None, :]
    cst[:, C_CAUSAL:C_CAUSAL + P] = np.where(i[None, :] <= i[:, None], 0.0, NEG)
    cst[:, C_ONES:C_ONES + P] = 1.0
    c = 63 - i % 64
    cst[:, C_FLIP:C_FLIP + P] = (i[None, :] == 64 * (i[:, None] // 64) + c[:, None])
    first = np.clip(c - 8, 0, 48)
    k = np.arange(64)
    inside = (k[None, :] >= first[:, None]) & (k[None, :] < first[:, None] + 16)
    cst[:, C_NAT:C_NAT + 64] = np.where(inside, 0.0, NEG)
    theta = np.float32(10000.0)
    cst[:, C_FREQ:C_FREQ + 16] = 1.0 / theta ** (np.arange(0, 32, 2, dtype=np.float32) / np.float32(32))
    rcst = np.zeros((P, R_END), np.float32)
    inv = theta ** (-np.arange(0, 256, 2, dtype=np.float32) / np.float32(256))
    ang = (np.arange(256, dtype=np.float32)[None, :] * inv[:, None]).astype(np.float32)
    rcst[:, R_COS:R_COS + 256] = np.cos(ang)
    rcst[:, R_SIN:R_SIN + 256] = np.sin(ang)
    for jt in range(2):
        o = R_DIST + 256 * jt
        rcst[:, o:o + 256] = np.arange(256)[None, :] - (i[:, None] + P * jt)
    return {"cst": cst, "rcst": rcst}


def kernel(**inputs):
    import numpy as _np
    import concourse.bacc as _bacc
    from concourse import mybir as _mybir
    from concourse.bass_utils import run_bass_kernel_spmd as _run

    tables = constants()
    arrays = {f"in_{name}_dram": _np.ascontiguousarray(inputs[name]) for name in _INS}
    arrays.update({f"const_{name}_dram": a for name, a in tables.items()})

    def written(known):
        nc = _bacc.Bacc("TRN2", target_bir_lowering=False, num_devices=1)

        def dram(name):
            a = arrays[name]
            return nc.dram_tensor(name, a.shape, _mybir.dt.from_np(a.dtype), kind="ExternalInput").ap()

        w = {name: dram(f"in_{name}_dram") for name in _INS}
        consts = {name: dram(f"const_{name}_dram") for name in tables}
        out = nc.dram_tensor("out_dram", (1, SEQ, D), F32, kind="ExternalOutput").ap()
        return nc, build(nc, w, consts, out, known)

    _, ledger = written(None)
    nc, _ = written(ledger)
    r = _run(nc, [arrays], core_ids=[0])
    return r.results[0]["out_dram"]
```

```python
from contextlib import ExitStack

import concourse.bass as bass
from concourse import mybir

F32 = mybir.dt.float32
F32R = mybir.dt.float32r
I32 = mybir.dt.int32
ALU = mybir.AluOpType
ACT = mybir.ActivationFunctionType
AX = mybir.AxisListType.X

P = 128
D = 1024
KD = D // P
SEQ = 256
DEPTH = 2
DFF = 2816
KF = DFF // P
GROUPS = DFF // 256
EPS = 1e-6
HEADS = 8
QK = 96
ROPE0 = 64
NEG = -1e30
UV, CQ, CKV, ZC, XBC, DT, GATES = 0, 1024, 1408, 1696, 2208, 3232, 3240
BANKS = 8
NRAW = 3
NSPLIT = 4
SLAB = 2048
PART = SLAB // 2
MODS_PER_FFN = 9
C_IDENT, C_U, C_CAUSAL, C_ONES, C_NAT, C_FREQ, C_FLIP, C_END = (
    0, 128, 256, 384, 512, 576, 592, 720)
R_COS, R_SIN, R_DIST, R_END = 0, 256, 512, 1024
TWO_PI = 6.283185307179586
TP1, TP2 = 6.28125, 0.0019350051879882812
TP3 = TWO_PI - TP1 - TP2


KINDS = {
    "pe": {"projected": "xbc dtp zp uvp cqp ckvp gp bp qp kvp wop rqp rkp rvp rgp rwp nqp nkp nvp nwp",
           "turned": "turn ty xst bt wst qkt cols", "scores": "sc nsp rap", "probs_turned": "ptp nptp",
           "attended": "op nop rop", "scan_sums": "csb csp cbp spp", "scan_out": "yd stp yo"},
    "act": {"projection_kept": "xr z uv cq ckv xs btok q kv rqc rkc rv rg Y0 nq nk nv gate_rows",
            "columns_hi": "xh yh qkT pT", "parameters": "sincos lge alog scc_half scc sc4hi",
            "probs": "pr npr", "scan": "cv dte expE expc st wexp", "squares": "ssa xn"},
    "dve": {"parameters": "cols_copied angles lgx lg ctx_ready modc modrow modt sc4", "columns_lo": "xT yT npT",
            "scan_in": "dtr dtn conv daU csc dec wlog rope", "scan_weights": "diff_half cbm MT xdd ra",
            "scan_rows": "yd_in yo_in yc gvn cqn ckn ya qkr rn ry",
            "merged": "merged mtmp", "attention_max": "nmax nnm", "attended": "yb_head ny_head",
            "residual": "Xd Xw Xr Xn sgg nt Y", "mean_square": "ms", "gate_diagonals": "diag aff wT"},
    "pool": {"rstd": "rstd", "padding": "xr0 nbias"},
}
KIND = {(engine, stage): kind for engine, kinds in KINDS.items()
        for kind, stages in kinds.items() for stage in stages.split()}


class Ledger:

    def __init__(self, nc, ctx, known):
        self.nc, self.ctx, self.known = nc, ctx, known
        self.events, self.count, self.sems = {}, {}, {}
        self.bank_of, self.freed, self.units, self.order, self.params = {}, {}, 0, [], 16

    def sem(self, name):
        if name not in self.sems:
            self.sems[name] = self.ctx.enter_context(self.nc.semaphore(name))
        return self.sems[name]

    def value(self, event):
        name, n = self.known.events[event] if self.known else ("first_writing", 1)
        return self.sem(name), n

    def reader_of(self, unit):
        name, n = self.known.freed[unit] if self.known else ("first_writing", 1)
        return self.sem(name), n

    def all_params(self):
        return self.known.params if self.known else 16


class Signals:

    def __init__(self, ledger, name):
        self.l, self.name = ledger, name

    def inc(self, stage, *key, also=(), frees=None):
        name = f"{self.name}_{KIND.get((self.name, stage), stage)}"
        n = self.l.count[name] = self.l.count.get(name, 0) + 1
        for event in ((stage, *key), *also):
            self.l.events[event] = (name, n)
        if frees is not None:
            self.l.freed[frees] = (name, n)
        return self.l.sem(name), 1

    def at(self, *event):
        return self.l.value(event)


class Slabs:

    def __init__(self):
        self.items, self.index, self.parts, self.part_index = [], {}, [], {}

    def add(self, key, src, kt, n, by_columns=False):
        self.index[key] = len(self.items)
        if by_columns:
            pieces = [(0, kt, c, P) for c in range(0, n, P)]
        else:
            per = max(1, PART // n)
            pieces = [(k, min(per, kt - k), 0, n) for k in range(0, kt, per)]
        for i, piece in enumerate(pieces):
            self.part_index[key, i] = len(self.parts)
            self.parts.append((key, i, *piece))
        self.items.append((key, src, kt, n, len(pieces)))


def plan(w):
    s = Slabs()

    def rows(m, k0, kt, c0, n):
        return m[k0 * P:(k0 + kt) * P, c0:c0 + n].rearrange("(k p) n -> p k n", p=P)

    def mod(i, half):
        l, g = divmod(i, 18)
        s.add(("mod", i, half), rows(w["w_mod_2"][l], 4 * half, 4, 512 * g, 512), 4, 512)

    def ffn(name, w_up, w_down, mod0=None):
        for g in range(GROUPS):
            for half, part in enumerate(("gate", "up")):
                s.add((name, part, g), rows(w_up, 0, KD, DFF * half + 256 * g, 256), KD, 256, by_columns=True)
                if mod0 is not None and g < MODS_PER_FFN:
                    mod(mod0 + g, half)
        for n in range(2):
            for d in range(6):
                kt = min(4, KF - 4 * d)
                s.add((name, "down", n, d), rows(w_down, 4 * d, kt, 512 * n, 512), kt, 512)

    def wide(name, m, c0, n):
        for half in range(2):
            s.add((name, half), rows(m, 4 * half, 4, c0, n), 4, n)

    for l in range(DEPTH):
        m = w["w_in"][l]
        ffn(("f1", l), w["ffn1_w_in"][l], w["ffn1_w_out"][l], 18 * l)
        for i in range(4):
            s.add(("xbc", l, i), rows(m, 0, KD, XBC + 256 * i, 256), KD, 256, by_columns=True)
        s.add(("dt", l), rows(m, 0, KD, DT, 8), KD, 8)
        wide(("z", l), m, ZC, 512)
        for n in range(2):
            wide(("uv", l, n), m, UV + 512 * n, 512)
        wide(("cq", l), m, CQ, 384)
        wide(("ckv", l), m, CKV, 288)

        def gate(br):
            for n in range(2):
                wide(("g", l, br, n), m, GATES + D * br + 512 * n, 512)

        def branch(br):
            for n in range(2):
                s.add(("b", l, br, n), rows(w["w_branch"][l, br], 0, 4, 512 * n, 512), 4, 512)

        gate(0)
        branch(0)
        gate(2)
        for n in range(2):
            s.add(("q", l, n), rows(w["mla_w_uq"][l], 0, 3, 384 * n, 384), 3, 384)
        s.add(("kv", l), rows(w["mla_w_ukv"][l], 0, 2, 0, 1024), 2, 1024)
        branch(2)
        gate(1)
        branch(1)
        for n in range(2):
            wide(("wo", l, n), w["w_out"][l], 512 * n, 512)
        ffn(("f2", l), w["ffn2_w_in"][l], w["ffn2_w_out"][l], 18 * l + MODS_PER_FFN)
    ffn(("g1", 0), w["ffn_w_in_2"][0, 0], w["ffn_w_out_2"][0, 0])
    for h in range(4):
        m = w["ret_w_in_2"][0]
        for i, part in enumerate("qk"):
            s.add(("r" + part, h), rows(m, 0, KD, 1024 * i + 256 * h, 256), KD, 256, by_columns=True)
        for i, part in enumerate("vg"):
            wide(("r" + part, h), m, 2048 * (i + 1) + 512 * h, 512)
        for n in range(2):
            s.add(("rw", h, n), rows(w["ret_w_out_2"][0], 4 * h, 4, 512 * n, 512), 4, 512)
    ffn(("g2", 0), w["ffn_w_in_2"][0, 1], w["ffn_w_out_2"][0, 1])
    ffn(("g1", 1), w["ffn_w_in_2"][1, 0], w["ffn_w_out_2"][1, 0])
    m = w["nat_w_qkv_2"][0]
    for i, part in enumerate("qk"):
        for j in range(4):
            s.add(("n" + part, j), rows(m, 0, KD, 1024 * i + 256 * j, 256), KD, 256, by_columns=True)
    for n in range(2):
        wide(("nv", n), m, 2048 + 512 * n, 512)
    for n in range(2):
        wide(("nw", n), w["nat_w_o_2"][0], 512 * n, 512)
    ffn(("g2", 1), w["ffn_w_in_2"][1, 1], w["ffn_w_out_2"][1, 1])
    return s


def build(nc, w, consts, out, known):
    slabs = plan(w)
    with ExitStack() as ctx:
        L = Ledger(nc, ctx, known)
        base = [nc.sbuf_base + 64 & ~63]

        def place(name, shape, dt=F32, off=None):
            size = 4
            for x in shape[1:]:
                size *= x
            size = (size + 63) // 64 * 64
            if off is None:
                off = base[0]
                base[0] += size
            return nc.alloc_sbuf_tensor_at(name, list(shape), dt, offset=off)

        raw = [place(f"raw{i}", [P, SLAB]) for i in range(NRAW)]
        whi = [place(f"whi{i}", [P, PART], F32R) for i in range(NSPLIT)]
        wlo = [place(f"wlo{i}", [P, PART], F32R) for i in range(NSPLIT)]
        cst = place("cst", [P, C_END])
        X = place("X", [P, 4, D])
        cols = place("cols", [P, 4, P])
        modc = place("modc", [P, DEPTH, 72, 2])
        scc = place("scc", [P, KD, 2])
        sc4 = place("sc4", [P, KD, 4], F32R)
        modt = place("modt", [P, 4, 4])
        small = place("small", [P, 256])
        cs16 = place("cs16", [P, 2, 2, 16])
        aff = place("aff", [P, KD, 2])
        dtb = place("dtb", [P, 3, DEPTH, 8])
        qkg = place("qkg", [P, DEPTH, 2, QK])
        vgain = place("vgain", [P, 512])
        lgs = place("lgs", [P, 8, 8])
        bsum = place("bsum", [P, 16])
        R0 = base[0]
        KB = 1024
        xT = {512: (place("xTh", [P, KD, 512], F32R), place("xTl", [P, KD, 512], F32R)),
              256: (place("xTh256", [P, KD, 256], F32R, off=R0), place("xTl256", [P, KD, 256], F32R, off=R0 + 8 * KB))}
        A0 = base[0]
        B0 = A0 - 16 * KB

        def arena(name, shape, off, dt=F32):
            t = nc.alloc_sbuf_tensor_at(name, list(shape), dt, offset=A0 + off)
            return t

        xn = arena("xn", [P, 4, D], 0)
        junk_a = arena("junk_a", [P, D], 16 * KB)
        junk_v = arena("junk_v", [P, D], 20 * KB)
        rowt = arena("rowt", [P, 4, P], 24 * KB)
        hh = arena("hh", [P, KF * 512], 0, F32R)
        hl = arena("hl", [P, KF * 512], 44 * KB, F32R)
        sg = arena("sg", [P, 2, 512], 88 * KB)
        modrow = arena("modrow", [4, 512], 40 * KB)
        gb = nc.alloc_sbuf_tensor_at("gb", [P, 2, D], F32, offset=A0 - 16 * KB)
        dg = nc.alloc_sbuf_tensor_at("dg", [P, KD, P], F32, offset=A0 - 8 * KB)
        def barena(name, shape, off, dt=F32):
            return nc.alloc_sbuf_tensor_at(name, list(shape), dt, offset=B0 + off)

        xr = barena("xr", [P, 8, 259], 0)
        cv = barena("cv", [P, 8, 256], 9 * KB)
        xs = barena("xs", [P, 2, 512], 17 * KB)
        E_ = barena("E", [P, 8, P], 21 * KB)
        xdt = barena("xdt", [P, 512], 25 * KB)
        xdd = barena("xdd", [P, 512], 27 * KB)
        st = barena("st", [P, 512], 29 * KB)
        btok = barena("btok", [P, 2, P], 31 * KB)
        cbm = barena("cbm", [P, 2, P], 32 * KB)
        gu = barena("gu", [P, 2, 512], 33 * KB)
        gv = barena("gv", [P, 2, 512], 37 * KB)
        z = barena("z", [P, 2, 512], 41 * KB)
        cq = barena("cq", [P, 2, 384], 45 * KB)
        ckv = barena("ckv", [P, 2, 288], 48 * KB)
        wT = barena("wT", [P, 4, P], 51 * KB)
        ws = barena("ws", [P, 4, P], 53 * KB)
        merged = barena("merged", [P, 2, D], 55 * KB)
        gates = barena("gates", [P, 2, D], 63 * KB)
        ytT = [(barena(f"yth{i}", [P, 4, 256], 71 * KB + 8 * i * KB, F32R),
                barena(f"ytl{i}", [P, 4, 256], 75 * KB + 8 * i * KB, F32R)) for i in range(2)]
        tmp = barena("tmp", [P, 2, 512], 87 * KB)
        qkT = barena("qkT", [P, HEADS, 512], 0)
        kv = barena("kv", [P, 2, D], 17 * KB)
        sq = barena("sq", [P, 16, QK], 25 * KB)
        cqTh = barena("cqTh", [P, 3, 256], 33 * KB, F32R)
        cqTl = barena("cqTl", [P, 3, 256], 36 * KB, F32R)
        ckTh = barena("ckTh", [P, 2, 256], 51 * KB, F32R)
        ckTl = barena("ckTl", [P, 2, 256], 53 * KB, F32R)
        qk = barena("qk", [P, 2, 16, QK], 91 * KB)
        yb = barena("yb", [P, 2, 512], 91 * KB)
        pr = barena("pr", [P, 2, 384], 103 * KB)
        pT = barena("pT", [P, 384], 89 * KB)
        rq = arena("rq", [P, 2, 512], 0)
        rk = arena("rk", [P, 2, 512], 4 * KB)
        rv = arena("rv", [P, 4, 512], 8 * KB)
        rg = arena("rg", [P, 4, 512], 16 * KB)
        ra = arena("ra", [P, 3, 512], 24 * KB)
        WX = arena("WX", [P, 2, 2, 256], 30 * KB)
        wtmp = arena("wtmp", [P, 2, 2, 256], 34 * KB)
        rYh = arena("rYh", [P, 4, 512], 38 * KB, F32R)
        rYl = arena("rYl", [P, 4, 512], 46 * KB, F32R)
        Y = arena("Y", [P, 4, D], 54 * KB)
        rt = arena("rt", [P, 2, 512], 70 * KB)
        gbm = arena("gbm", [P, 2, D], 74 * KB)
        dgm = arena("dgm", [P, KD, P], 82 * KB)
        rcst = arena("rcst", [P, R_END], 86 * KB)
        nq = arena("nq", [P, 8, 256], 0)
        nk = arena("nk", [P, 8, 512], 8 * KB)
        nv = arena("nv", [P, 4, D], 24 * KB)
        nbias = [arena(f"nbias{i}", [P, 2, 4, 256], (40 + 8 * i) * KB) for i in range(2)]
        npr = arena("npr", [P, 2, 512], 56 * KB)
        npT = arena("npT", [P, 2, 512], 60 * KB)
        ny = arena("ny", [P, 2, D], 64 * KB)
        nt = arena("nt", [P, 512], 72 * KB)
        fg = arena("fg", [P, D], 70 * KB)
        fo = arena("fo", [P, 2, D], 74 * KB)

        ident = cst[:, C_IDENT:C_IDENT + P]
        upper = cst[:, C_U:C_U + P]
        ones = cst[:, C_ONES:C_ONES + P]
        bank = [ctx.enter_context(nc.psum_tensor(f"bank{i}", [P, 512], F32)) for i in range(BANKS)]
        landed = [ctx.enter_context(nc.semaphore(f"raw{i}_landed")) for i in range(NRAW)]
        block = ctx.enter_context(nc.Block())

        def unit(*key):
            return bank[L.known.bank_of[key]] if L.known else bank[0]

        def col(table, row, n=1):
            return cols[:, table, row:row + n]

        NORM1, NORMX, NORM2, NORMG, QN, KVN, SSN = 0, 16, 32, 48, 96, 102, 106
        CVB, CVW, GN, BS = 0, 16, 80, 96
        BM, CC = 0, 72

        def row_loads():
            f = lambda name, pat: w[name].rearrange(pat, p=P)
            yield rowt[NORM1:NORM1 + 16, 0, :], f("ffn1_norm", "l (k p) -> (l k) p")
            yield rowt[NORMX:NORMX + 16, 0, :], f("mix_norm", "l (k p) -> (l k) p")
            yield rowt[NORM2:NORM2 + 16, 0, :], f("ffn2_norm", "l (k p) -> (l k) p")
            yield rowt[NORMG:NORMG + 48, 0, :], f("norm_g_2", "l j (k p) -> (l j k) p")
            yield rowt[QN:QN + 6, 0, :], f("mla_q_norm", "l (k p) -> (l k) p")
            yield rowt[KVN:KVN + 4, 0, :], f("mla_kv_norm", "l (k p) -> (l k) p")
            yield rowt[SSN:SSN + 8, 0, :], f("ssd_norm", "l (k p) -> (l k) p")
            yield rowt[CVB:CVB + 16, 1, :], f("ssd_conv_b", "l (k p) -> (l k) p")
            yield rowt[CVW:CVW + 64, 1, :], f("ssd_conv_w", "l j (k p) -> (l j k) p")
            yield rowt[GN:GN + 16, 1, :], f("ret_gn_g_2", "l (k p) -> (l k) p")
            yield rowt[BS:BS + 8, 1, :], w["gm_b_s"].rearrange("l g t -> (l g) t")
            for l in range(DEPTH):
                yield rowt[BM:BM + 72, 2 + l, :], w["b_mod_2"][l].rearrange("(k p) -> k p", p=P)
            yield rowt[CC:CC + 8, 2, :], f("c_2", "l (k p) -> (l k) p")
            yield rowt[CC + 8:CC + 16, 2, :], w["c_ctx_2"].rearrange("(k p) -> k p", p=P)

        ROWS = (114, 104, 88, 72)

        def wide_row(a, n):
            return bass.AP(a.tensor, a.offset, [[0, P], [1, n]])

        def stripe(t, n, l):
            return t[:, l, n * 512:(n + 1) * 512]

        def view(tile, key):
            _, _, kt, n, _ = slabs.items[slabs.index[key]]
            return tile[:, 0:kt * n].rearrange("p (k n) -> p k n", n=n)

        def part_views(key, part):
            i = slabs.part_index[key, part]
            _, _, k0, kt, c0, n = slabs.parts[i]
            src = view(raw[slabs.index[key] % NRAW], key)[:, k0:k0 + kt, c0:c0 + n]
            hi, lo = (t[i % NSPLIT][:, 0:kt * n].rearrange("p (k n) -> p k n", n=n) for t in (whi, wlo))
            return src, hi, lo

        def arrival(key):
            s = slabs.index[key]
            return landed[s % NRAW], 16 * (s // NRAW + 1)

        @block.sync
        def _(sp):
            e = Signals(L, "sp")
            n_first = [0]

            def first(dst, src):
                sp.dma_start(dst, src).then_inc(L.sem("params_landed"), 16)
                n_first[0] += 16

            def slab_range(a, b):
                for s in range(a, b):
                    key, src, _, _, _ = slabs.items[s]
                    if s >= NRAW:
                        old, _, _, _, parts = slabs.items[s - NRAW]
                        sp.wait_ge(*e.at("hi", old, parts - 1))
                        sp.wait_ge(*e.at("lo", old, parts - 1))
                    sp.dma_start(view(raw[s % NRAW], key), src).then_inc(landed[s % NRAW], 16)

            sp.dma_start(X[:, 0:2, :], w["x"][0].rearrange("(t p) n -> p t n", p=P))\
              .then_inc(L.sem("x_landed"), 16)
            slab_range(0, NRAW)
            first(cst[:, :], consts["cst"])
            for dst, src in row_loads():
                first(dst, src)
            for l in range(DEPTH):
                for i, name in enumerate(("ssd_dt_bias", "ssd_a_log", "ssd_d")):
                    first(dtb[:, i, l, :], wide_row(w[name][l], 8))
                for i, name in enumerate(("mla_q_gain", "mla_k_gain")):
                    first(qkg[:, l, i, :], wide_row(w[name][l], QK))
            first(lgs[:, 0, 0:4], wide_row(w["ret_decay_f_2"][0], 4))
            first(lgs[:, 0, 4:8], wide_row(w["ret_decay_b_2"][0], 4))
            with nc.allow_non_contiguous_dma(reason="256 positions, one to a partition and tile"):
                first(bsum[:, 0:2].bitcast(I32), w["positions"][0].rearrange("(t p) -> p t", p=P))
            first(X[:, 2:4, :], w["ctx_2"][0].rearrange("(t p) n -> p t n", p=P))
            L.params = n_first[0]
            slab_range(NRAW, len(slabs.items))
            sp.wait_ge(*e.at("out_row", 1))
            sp.dma_start(out[0].rearrange("(t p) n -> p t n", p=P), fo[:, :, :])\
              .then_inc(L.sem("out_written"), 16)
            sp.wait_ge(L.sem("out_written"), 16)

        def tiles_of(T):
            return range(T // P)

        @block.tensor
        def _(pe):
            e = Signals(L, "pe")

            def new(*key):
                u = L.units
                L.units += 1
                L.bank_of[key] = u % BANKS
                L.order.append(key)
                if u >= BANKS:
                    pe.wait_ge(*L.reader_of(L.order[u - BANKS]))
                return bank[u % BANKS]

            def mm3(ps, lh, ll, rh, rl, start, stop):
                pe.matmul(ps, lh, rh, start=start, stop=False, skip_group_check=True)
                pe.matmul(ps, lh, rl, start=False, stop=False, skip_group_check=True)
                return pe.matmul(ps, ll, rh, start=False, stop=stop, skip_group_check=True)

            def mod(i, half, ps):
                if i == 0:
                    pe.wait_ge(*e.at("sc4"))
                for part in range(2):
                    wh, wl = split_ready(("mod", i, half), part)
                    for j in range(2):
                        k = 4 * half + 2 * part + j
                        pe.matmul(ps[0:4, :], sc4[:, k, :], wh[:, j, :], start=k == 0, stop=False,
                                  skip_group_check=True)
                        m = pe.matmul(ps[0:2, :], sc4[:, k, 0:2], wl[:, j, :], start=False, stop=k == KD - 1,
                                      skip_group_check=True)
                    if k < KD - 1:
                        m.then_inc(*e.inc("used", ("mod", i, half), part))
                    else:
                        m.then_inc(*e.inc("modp", i, also=[("used", ("mod", i, 1), 1)]))

            def mod_turn(i):
                pe.wait_ge(*e.at("modrow", i))
                ps = new("modtp", i)
                for c in range(4):
                    m = pe.transpose(ps[:, 4 * c:4 * c + 4], modrow[0:4, c * P:(c + 1) * P], ident[0:4, 0:4])
                m.then_inc(*e.inc("modtp", i))

            def split_ready(key, part):
                pe.wait_ge(*e.at("hi", key, part))
                pe.wait_ge(*e.at("lo", key, part))
                return part_views(key, part)[1:]

            def feature_major(key, T, units, xh, xl):
                u = 0
                for mc in range(2):
                    wh, wl = split_ready(key, mc)
                    if T == 512 or mc == 0:
                        ps = new(*units[u])
                    o = 0 if T == 512 else mc * 256
                    for k in range(KD):
                        m = mm3(ps[:, o:o + T], wh[:, k, :], wl[:, k, :], xh[:, k, 0:T], xl[:, k, 0:T],
                                k == 0, k == KD - 1)
                    if T == 512 or mc == 1:
                        m.then_inc(*e.inc(*units[u], also=[("used", key, mc)]))
                        u += 1
                    else:
                        m.then_inc(*e.inc("used", key, mc))

            def rows_by(key, name, ps, xh, xl, k0, total):
                tiles = sorted(ps)
                for part in range(slabs.items[slabs.index[key]][4]):
                    wh, wl = split_ready(key, part)
                    kt, n = wh.shape[1], wh.shape[2]
                    last = k0 + kt == total
                    for t in tiles:
                        for k in range(kt):
                            m = mm3(ps[t][:, 0:n], xh[:, k0 + k, t * P:(t + 1) * P], xl[:, k0 + k, t * P:(t + 1) * P],
                                    wh[:, k, :], wl[:, k, :], k0 + k == 0, k0 + k == total - 1)
                        if last:
                            m.then_inc(*e.inc(*name, t, also=[("used", key, part)] if t == tiles[-1] else []))
                    if not last:
                        m.then_inc(*e.inc("used", key, part))
                    k0 += kt
                return k0

            def token_major(keys, name, tiles, xh, xl):
                ps = {t: new(*name, t) for t in tiles}
                total = sum(slabs.items[slabs.index[k]][2] for k in keys)
                k0 = 0
                for key in keys:
                    k0 = rows_by(key, name, ps, xh, xl, k0, total)

            def turn_in(name, T, ready):
                for k in range(KD):
                    ps = new("turn", name, k)
                    for t in tiles_of(T):
                        if k == 0:
                            pe.wait_ge(*e.at(*ready, t))
                        m = pe.transpose(ps[:, t * P:(t + 1) * P], xn[:, t, k * P:(k + 1) * P], ident)
                    m.then_inc(*e.inc("turn", name, k))

            def turn_y(name, src, chunks, T, ready, c0=0):
                per = 512 // T
                for u in range((chunks + per - 1) // per):
                    ps = new("ty", name, u)
                    for j in range(per):
                        if u * per + j >= chunks:
                            break
                        c = u * per + j
                        for t in tiles_of(T):
                            pe.wait_ge(*e.at(*ready, t))
                            m = pe.transpose(ps[:, j * T + t * P:j * T + (t + 1) * P],
                                             src[:, t, c * P:(c + 1) * P], ident)
                    m.then_inc(*e.inc("ty", name, u))

            def broadcast_gate(name, dgt, whos):
                for who in whos:
                    pe.wait_ge(*e.at("diag", name, who))
                    for n in range(2):
                        ps = new("gbp", name, who, n)
                        m = pe.matmul(ps[:, :], ones, dgt[:, 4 * n:4 * n + 4, :], start=True, stop=True)
                        m.then_inc(*e.inc("gbp", name, who, n))

            def ffn(name, T, mod0, gate_whos):
                turn_in(name, T, ("xn", name))
                for g in range(GROUPS):
                    if g == 0:
                        pe.wait_ge(*e.at("xT", name, KD - 1))
                    for half, part in enumerate(("gate", "up")):
                        feature_major((name, part, g), T, [(part, name, g, i) for i in range(T // 256)], *xT[T])
                        if mod0 is not None:
                            if half == 0 and 0 < g <= MODS_PER_FFN:
                                mod_turn(mod0 + g - 1)
                            if g < MODS_PER_FFN:
                                if half == 0:
                                    ps = new("modp", mod0 + g)
                                mod(mod0 + g, half, ps)
                if gate_whos:
                    broadcast_gate(name, dg, gate_whos)
                pe.wait_ge(*e.at("hidden", name, GROUPS - 1, T // 256 - 1))
                hv = (hh[:, 0:KF * T].rearrange("p (k t) -> p k t", t=T),
                      hl[:, 0:KF * T].rearrange("p (k t) -> p k t", t=T))
                for n in range(2):
                    ps = {t: new("down", name, n, t) for t in tiles_of(T)}
                    k0 = 0
                    for d in range(6):
                        k0 = rows_by((name, "down", n, d), ("down", name, n), ps, *hv, k0, KF)

            pe.wait_ge(L.sem("params_landed"), L.all_params())
            for i in range(4):
                ps = new("cols", i)
                m = pe.transpose(ps[:, 0:ROWS[i]], rowt[0:ROWS[i], i, :], ident[0:ROWS[i], 0:ROWS[i]])
                m.then_inc(*e.inc("cols", i))

            def mixers(l):
                nm = ("mx", l)
                turn_in(nm, 256, ("xn", nm))
                pe.wait_ge(*e.at("xT", nm, KD - 1))
                for i in range(4):
                    feature_major(("xbc", l, i), 256, [("xbc", l, i)], *xT[256])
                token_major([("dt", l)], ("dtp", l), range(2), *xT[256])
                token_major([(("z", l), 0), (("z", l), 1)], ("zp", l), range(2), *xT[256])
                for n in range(2):
                    token_major([(("uv", l, n), 0), (("uv", l, n), 1)], ("uvp", l, n), range(2), *xT[256])
                token_major([(("cq", l), 0), (("cq", l), 1)], ("cqp", l), range(2), *xT[256])
                token_major([(("ckv", l), 0), (("ckv", l), 1)], ("ckvp", l), range(2), *xT[256])
                for t in range(2):
                    pe.wait_ge(*e.at("cv", l))
                    ps = new("xst", l, t)
                    for c in range(4):
                        m = pe.transpose(ps[:, c * P:(c + 1) * P], cv[:, c, t * P:(t + 1) * P], ident)
                    m.then_inc(*e.inc("xst", l, t))
                ps = new("bt", l)
                for g in range(2):
                    m = pe.transpose(ps[:, g * P:(g + 1) * P], cv[:, 4 + g, 0:P], ident)
                m.then_inc(*e.inc("bt", l))
                def gate(br):
                    for n in range(2):
                        token_major([(("g", l, br, n), 0), (("g", l, br, n), 1)], ("gp", l, br, n), range(2),
                                    *xT[256])

                def branch(br, yT):
                    for n in range(2):
                        token_major([("b", l, br, n)], ("bp", l, br, n), range(2), *yT)

                def scan_sums(c):
                    pe.wait_ge(*e.at("daU", l, c))
                    for h2 in range(2):
                        ps = new("csb", l, c, h2)
                        m = pe.matmul(ps[:, :], ones, E_[:, 4 * h2:4 * h2 + 4, :], start=True, stop=True)
                        m.then_inc(*e.inc("csb", l, c, h2))
                    ps = new("csp", l, c)
                    m = pe.matmul(ps[:, 0:8], upper, small[:, 32 + 8 * c:40 + 8 * c], start=True, stop=True)
                    m = pe.matmul(ps[:, 8:16], ones, small[:, 32 + 8 * c:40 + 8 * c], start=True, stop=True)
                    m.then_inc(*e.inc("csp", l, c))
                    ps = new("cbp", l, c)
                    for g in range(2):
                        m = pe.matmul(ps[:, g * P:(g + 1) * P], cv[:, 4 + g, c * P:(c + 1) * P],
                                      cv[:, 6 + g, c * P:(c + 1) * P], start=True, stop=True)
                    m.then_inc(*e.inc("cbp", l, c))

                def scan_inside(c):
                    pe.wait_ge(*e.at("MT", l, c))
                    ps = new("yd", l, c)
                    for h in range(8):
                        m = pe.matmul(ps[:, h * 64:(h + 1) * 64], E_[:, h, :], xdt[:, h * 64:(h + 1) * 64],
                                      start=True, stop=True)
                    m.then_inc(*e.inc("yd", l, c))

                scan_sums(0)
                pe.wait_ge(*e.at("ws", l))
                ps = new("wst", l)
                for g in range(4):
                    m = pe.transpose(ps[:, g * P:(g + 1) * P], ws[:, g, :], ident)
                m.then_inc(*e.inc("wst", l))
                gate(0)
                for t in range(2):
                    pe.wait_ge(*e.at("gvn", l, t))
                    if t == 0:
                        pe.wait_ge(*e.at("wT", l))
                    ps = new("spp", l, t)
                    for g in range(4):
                        m = pe.matmul(ps[:, g * P:(g + 1) * P], wT[:, g, :], gv[:, t, g * P:(g + 1) * P],
                                      start=True, stop=True)
                    m.then_inc(*e.inc("spp", l, t))
                scan_inside(0)
                pe.wait_ge(*e.at("btok", l))
                pe.wait_ge(*e.at("xdd", l))
                ps = new("stp", l)
                for g in range(2):
                    m = pe.matmul(ps[:, g * 256:(g + 1) * 256], btok[:, g, :],
                                  xdd[:, g * 256:(g + 1) * 256], start=True, stop=True)
                m.then_inc(*e.inc("stp", l))
                turn_y(("a", l), gu, 4, 256, ("ya", l))
                pe.wait_ge(*e.at("yT", ("a", l), 1))
                branch(0, ytT[1])
                turn_y(("cq", l), cq, 3, 256, ("cqn", l))
                turn_y(("ck", l), ckv, 2, 256, ("ckn", l))
                scan_sums(1)
                gate(2)
                scan_inside(1)
                pe.wait_ge(*e.at("st", l))
                ps = new("yo", l)
                for g in range(2):
                    m = pe.matmul(ps[:, g * 256:(g + 1) * 256], cv[:, 6 + g, P:2 * P],
                                  st[:, g * 256:(g + 1) * 256], start=True, stop=True)
                m.then_inc(*e.inc("yo", l))
                pe.wait_ge(*e.at("yT", ("cq", l), 2))
                for n in range(2):
                    token_major([("q", l, n)], ("qp", l, n), range(2), cqTh, cqTl)
                pe.wait_ge(*e.at("yT", ("ck", l), 1))
                ps = {(n, t): new("kvp", l, n, t) for n in range(2) for t in range(2)}
                for k in range(2):
                    wh, wl = split_ready(("kv", l), k)
                    for n, t in ps:
                        m = mm3(ps[n, t][:, :], ckTh[:, k, t * P:(t + 1) * P], ckTl[:, k, t * P:(t + 1) * P],
                                wh[:, 0, n * 512:(n + 1) * 512], wl[:, 0, n * 512:(n + 1) * 512], k == 0, k == 1)
                        if k == 1:
                            also = [("used", ("kv", l), 1)] if n + t == 2 else []
                            m.then_inc(*e.inc("kvp", l, n, t, also=also))
                    if k == 0:
                        m.then_inc(*e.inc("used", ("kv", l), 0))
                turn_y(("c", l), z, 4, 256, ("yc", l))
                pe.wait_ge(*e.at("yT", ("c", l), 3))
                branch(2, ytT[0])
                gate(1)
                for t in range(2):
                    pe.wait_ge(*e.at("qkr", l, t))
                for h in range(HEADS):
                    ps = new("qkt", l, h)
                    for i in range(2):
                        for t in range(2):
                            m = pe.transpose(ps[0:QK, 256 * i + t * P:256 * i + (t + 1) * P],
                                             qk[:, t, 8 * i + h, :], ident)
                    m.then_inc(*e.inc("qkt", l, h))
                for i in range(HEADS + 2):
                    if i < HEADS:
                        h = i
                        pe.wait_ge(*e.at("qkT", l, h))
                        ps = new("sc", l, h)
                        m = pe.matmul(ps[:, 0:P], qkT[0:QK, h, 0:P], qkT[0:QK, h, 256:384], start=True, stop=True)
                        m = pe.matmul(ps[:, 256:512], qkT[0:QK, h, P:256], qkT[0:QK, h, 256:512],
                                      start=True, stop=True)
                        m.then_inc(*e.inc("sc", l, h))
                    if 1 <= i <= HEADS:
                        h = i - 1
                        pe.wait_ge(*e.at("pr", l, h))
                        ps = new("ptp", l, h)
                        for j in range(3):
                            m = pe.transpose(ps[:, j * P:(j + 1) * P], pr[:, h % 2, j * P:(j + 1) * P], ident)
                        m.then_inc(*e.inc("ptp", l, h))
                    if i >= 2:
                        h = i - 2
                        pe.wait_ge(*e.at("pT", l, h))
                        ps = new("op", l, h)
                        v0, v1 = (kv[:, t, h * P + 64:(h + 1) * P] for t in range(2))
                        m = pe.matmul(ps[:, 0:64], pT[:, 0:P], v0, start=True, stop=True)
                        m = pe.matmul(ps[:, 64:128], pT[:, P:2 * P], v0, start=True, stop=False)
                        m = pe.matmul(ps[:, 64:128], pT[:, 2 * P:3 * P], v1, start=False, stop=True)
                        m.then_inc(*e.inc("op", l, h))
                turn_y(("b", l), yb, 4, 256, ("yb", l))
                pe.wait_ge(*e.at("yT", ("b", l), 1))
                branch(1, ytT[1])
                turn_y(("m", l), merged, 8, 256, ("mg", l))
                pe.wait_ge(*e.at("yT", ("m", l), 3))
                for n in range(2):
                    token_major([(("wo", l, n), 0), (("wo", l, n), 1)], ("wop", l, n), range(2), *xT[256])

            for l in range(DEPTH):
                ffn(("f1", l), 256, 18 * l, ())
                mixers(l)
                ffn(("f2", l), 256, 18 * l + MODS_PER_FFN, ())

            ffn(("g1", 0), 512, None, (0, 1))
            turn_in(("r",), 512, ("xn", ("r",)))
            pe.wait_ge(*e.at("xT", ("r",), KD - 1))
            broadcast_gate(("r",), dgm, (0, 1))
            for h in range(4):
                for part in "qk":
                    feature_major(("r" + part, h), 512, [("r" + part + "p", h, i) for i in range(2)], *xT[512])
                for part in "vg":
                    token_major([(("r" + part, h), 0), (("r" + part, h), 1)], ("r" + part + "p", h),
                                range(4), *xT[512])
                pe.wait_ge(*e.at("rqk", h))
                ps = new("rap", h, 0)
                for jt in range(2):
                    for k in range(2):
                        m = pe.matmul(ps[:, 256 * jt:256 * jt + 256], rk[:, k, jt * P:(jt + 1) * P],
                                      rq[:, k, 0:256], start=k == 0, stop=k == 1, skip_group_check=True)
                m.then_inc(*e.inc("rap", h, 0))
                for jt in range(2):
                    ps = new("rap", h, 1 + jt)
                    for k in range(2):
                        m = pe.matmul(ps[:, :], rk[:, k, 256 + jt * P:256 + (jt + 1) * P], rq[:, k, :],
                                      start=k == 0, stop=k == 1)
                    m.then_inc(*e.inc("rap", h, 1 + jt))
                pe.wait_ge(*e.at("ra", h, 2))
                pe.wait_ge(*e.at("rv", h, 3))
                for t in range(4):
                    ps = new("rop", h, t)
                    if t < 2:
                        pairs = [(ra[:, 0, 256 * jt + t * P:256 * jt + (t + 1) * P], jt) for jt in range(2)]
                        pairs += [(ra[:, 1 + jt, t * P:(t + 1) * P], 2 + jt) for jt in range(2)]
                    else:
                        pairs = [(ra[:, 1 + jt, t * P:(t + 1) * P], 2 + jt) for jt in range(2)]
                    for i, (a, j) in enumerate(pairs):
                        m = pe.matmul(ps[:, :], a, rv[:, j, :], start=i == 0, stop=i == len(pairs) - 1)
                    m.then_inc(*e.inc("rop", h, t))
                turn_y(("r", h), rg, 4, 512, ("ry", h))
                pe.wait_ge(*e.at("yT", ("r", h), 3))
                for n in range(2):
                    token_major([("rw", h, n)], ("rwp", h, n), range(4), rYh, rYl)
            ffn(("g2", 0), 512, None, (0, 1))
            ffn(("g1", 1), 512, None, (0, 1))
            turn_in(("n",), 512, ("xn", ("n",)))
            pe.wait_ge(*e.at("xT", ("n",), KD - 1))
            for j in range(4):
                feature_major(("nq", j), 256, [("nqp", j)], *xT[512])
            for j in range(4):
                feature_major(("nk", j), 512, [("nkp", j, i) for i in range(2)], *xT[512])
            for n in range(2):
                token_major([(("nv", n), 0), (("nv", n), 1)], ("nvp", n), range(4), *xT[512])
            pe.wait_ge(*e.at("nq", 3))
            pe.wait_ge(*e.at("nk", 3, 1))
            pe.wait_ge(*e.at("nv", 1, 3))
            items = [(h, t) for h in range(16) for t in range(2)]
            for i in range(len(items) + 2):
                if i < len(items):
                    h, t = items[i]
                    p0 = 64 * (h % 2)
                    ps = new("nsp", h, t)
                    pe.matmul(ps[:, :], nq[p0:p0 + 64, h // 2, t * P:(t + 1) * P],
                              nk[p0:p0 + 64, h // 2, :], start=True, stop=False, skip_group_check=True)
                    pe.wait_ge(*e.at("nbias", h // 4))
                    m = pe.matmul(ps[:, 0:256], cst[:, C_FLIP:C_FLIP + P], nbias[h // 4 % 2][:, t, h % 4, :],
                                  start=False, stop=True, skip_group_check=True)
                    m.then_inc(*e.inc("nsp", h, t, also=[("nbias_used", h // 4)]))
                if 1 <= i <= len(items):
                    h, t = items[i - 1]
                    pe.wait_ge(*e.at("npr", h, t))
                    ps = new("nptp", h, t)
                    for j in range(4):
                        m = pe.transpose(ps[:, j * P:(j + 1) * P], npr[:, t, j * P:(j + 1) * P], ident)
                    m.then_inc(*e.inc("nptp", h, t))
                if i >= 2:
                    h, t = items[i - 2]
                    pe.wait_ge(*e.at("npT", h, t))
                    ps = new("nop", h, t)
                    for j in range(4):
                        m = pe.matmul(ps[:, 0:64], npT[:, t, j * P:(j + 1) * P], nv[:, j, h * 64:(h + 1) * 64],
                                      start=j == 0, stop=j == 3)
                    m.then_inc(*e.inc("nop", h, t))
            broadcast_gate(("n",), dgm, (0,))
            turn_y(("n",), ny, 8, 256, ("ny",))
            pe.wait_ge(*e.at("yT", ("n",), 3))
            for n in range(2):
                token_major([(("nw", n), 0), (("nw", n), 1)], ("nwp", n), range(2), *xT[256])
            ffn(("g2", 1), 256, None, (0,))

        idx = slabs.index

        def ahead(until, key):
            parts = slabs.items[idx[key]][4]
            until(slabs.part_index[key, parts - 1] + NSPLIT - 1)

        @block.scalar
        def _(act):
            e = Signals(L, "act")
            split = [0]

            def until(s):
                while split[0] <= min(s, len(slabs.parts) - 1):
                    i = split[0]
                    key, part = slabs.parts[i][0:2]
                    split[0] += 1
                    src, hi, _ = part_views(key, part)
                    act.wait_ge(*arrival(key))
                    if i >= NSPLIT:
                        act.wait_ge(*e.at("used", *slabs.parts[i - NSPLIT][0:2]))
                    nc.scalar.activation(hi, src, ACT.Copy).then_inc(*e.inc("hi", key, part))

            A = nc.scalar.activation

            def norm(name, T):
                for t in tiles_of(T):
                    if t % 2:
                        act.wait_ge(*e.at("X", name, t))
                        if t > 1:
                            act.wait_ge(*e.at("ssa", name, t - 2))
                        A(junk_a[:, :], X[:, t, :], ACT.Square, accum_out=small[:, t:t + 1]).then_inc(*e.inc("ssa", name, t))
                for t in tiles_of(T):
                    if t % 2:
                        act.wait_ge(*e.at("rstd", name))
                        A(xn[:, t, :], X[:, t, :], ACT.Copy, scale=small[:, 8 + t:9 + t]).then_inc(*e.inc("xn", name, t))

            def turned(name, T, gain, bias):
                xTh = xT[T][0]
                for k in range(KD):
                    act.wait_ge(*e.at("turn", name, k))
                    act.wait_ge(*e.at("aff", name))
                    A(xTh[:, k, 0:256], unit("turn", name, k)[:, 0:256], ACT.Identity,
                             scale=gain(k, 0), bias=bias(k, 0) if bias else 0.0).then_inc(*e.inc("xh", name, k, 0))
                    if T == 512:
                        A(xTh[:, k, 256:512], unit("turn", name, k)[:, 256:512], ACT.Identity,
                                 scale=gain(k, 1), bias=bias(k, 1)).then_inc(*e.inc("xh", name, k, 1))

            def turned_y(name, chunks, T, dst, gain=None):
                per = 512 // T
                for u in range((chunks + per - 1) // per):
                    act.wait_ge(*e.at("ty", name, u))
                    if gain is None:
                        m = A(dst[:, u * per:(u + 1) * per, 0:T], unit("ty", name, u)[:, :]
                              .rearrange("p (j t) -> p j t", t=T), ACT.Copy)
                        m.then_inc(*e.inc("yh", name, u))
                    else:
                        for j in range(min(per, chunks - u * per)):
                            c = u * per + j
                            m = A(dst[:, c, 0:T], unit("ty", name, u)[:, j * T:(j + 1) * T], ACT.Copy, scale=gain(c))
                            m.then_inc(*e.inc("yh", name, c))

            def ffn(name, T, gate_whos, mod0=None):
                for g in range(GROUPS):
                    for i in range(T // 256):
                        ahead(until, (name, "gate", g))
                        act.wait_ge(*e.at("gate", name, g, i))
                        b = (g * (T // 256) + i) % 2
                        if (g * (T // 256) + i) >= 2:
                            g2, i2 = divmod(g * (T // 256) + i - 2, T // 256)
                            act.wait_ge(*e.at("hidden", name, g2, i2))
                        A(sg[:, b, :], unit("gate", name, g, i)[:, :], ACT.Silu).then_inc(*e.inc("sg", name, g, i, frees=("gate", name, g, i)))
                    ahead(until, (name, "up", g))
                    for i in range(T // 256):
                        b = (g * (T // 256) + i) % 2
                        o = (g * (T // 256) + i) * 512
                        act.wait_ge(*e.at("ht", name, g, i))
                        A(hh[:, o:o + 512], sg[:, b, :], ACT.Copy).then_inc(*e.inc("hhi", name, g, i))
                    if mod0 is not None and g < MODS_PER_FFN:
                        for half in range(2):
                            ahead(until, ("mod", mod0 + g, half))
                for who in gate_whos:
                    for n in range(2):
                        act.wait_ge(*e.at("gbp", name, who, n))
                        A(gb[:, who, n * 512:(n + 1) * 512], unit("gbp", name, who, n)[:, :], ACT.Copy,
                                 scale=0.5).then_inc(*e.inc("gb", name, who, n, frees=("gbp", name, who, n)))
                for n in range(2):
                    for d in range(6):
                        ahead(until, (name, "down", n, d))

            until(NSPLIT - 2)
            act.wait_ge(L.sem("params_landed"), L.all_params())
            act.wait_ge(*e.at("angles"))
            A(cs16[:, :, :, :], cs16[:, :, :, :], ACT.Sin).then_inc(*e.inc("sincos"))
            act.wait_ge(*e.at("lgx"))
            A(lgs[:, 1, :], lgs[:, 1, :], ACT.Exp).then_inc(*e.inc("lge"))
            A(dtb[:, 1, :, :], dtb[:, 1, :, :], ACT.Exp).then_inc(*e.inc("alog"))
            act.wait_ge(*e.at("cols_copied", 2))
            A(scc[:, :, 0], cols[:, 2, CC:CC + 8], ACT.Silu).then_inc(*e.inc("scc_half", 0))
            A(scc[:, :, 1], cols[:, 2, CC + 8:CC + 16], ACT.Silu).then_inc(*e.inc("scc"))
            act.wait_ge(*e.at("scc"))
            A(sc4[:, :, 0:2], scc[:, :, :], ACT.Copy).then_inc(*e.inc("sc4hi"))

            gain1 = lambda row: (lambda k, who: col(0, row + k))
            gain2 = lambda k, who: aff[:, k, who:who + 1]

            def bias2(l, j):
                return lambda k, who: modc[:, l, (j * 3) * 8 + k, who:who + 1]

            def mixers(l):
                nm = ("mx", l)
                norm(nm, 256)
                turned(nm, 256, gain1(NORMX + 8 * l), None)
                for i in range(4):
                    ahead(until, ("xbc", l, i))
                    act.wait_ge(*e.at("xbc", l, i))
                    if i == 0:
                        act.wait_ge(*e.at("xr0", l))
                    A(xr[:, 2 * i:2 * i + 2, 3:259], unit("xbc", l, i)[:, :].rearrange("p (m t) -> p m t", m=2),
                             ACT.Copy).then_inc(*e.inc("xr", l, i, frees=("xbc", l, i)))
                ahead(until, ("dt", l))
                ahead(until, (("z", l), 0))
                ahead(until, (("z", l), 1))
                for t in range(2):
                    act.wait_ge(*e.at("zp", l, t))
                    A(z[:, t, :], unit("zp", l, t)[:, :], ACT.Silu).then_inc(*e.inc("z", l, t, frees=("zp", l, t)))
                act.wait_ge(*e.at("dtn", l))
                A(small[:, 64:80], small[:, 64:80], ACT.Exp).then_inc(*e.inc("dte", l))
                for ch in range(8):
                    act.wait_ge(*e.at("conv", l))
                    m = A(cv[:, ch, :], cv[:, ch, :], ACT.Silu, bias=col(1, CVB + 8 * l + ch))
                m.then_inc(*e.inc("cv", l))
                for n in range(2):
                    for half in range(2):
                        ahead(until, (("uv", l, n), half))
                    for t in range(2):
                        act.wait_ge(*e.at("uvp", l, n, t))
                        dst = gv if n else gu
                        A(dst[:, t, :], unit("uvp", l, n, t)[:, :], ACT.Gelu).then_inc(*e.inc("uv", l, n, t, frees=("uvp", l, n, t)))
                for half in range(2):
                    ahead(until, (("cq", l), half))
                for t in range(2):
                    act.wait_ge(*e.at("cqp", l, t))
                    A(cq[:, t, :], unit("cqp", l, t)[:, 0:384], ACT.Copy).then_inc(*e.inc("cq", l, t, frees=("cqp", l, t)))
                for half in range(2):
                    ahead(until, (("ckv", l), half))
                for t in range(2):
                    act.wait_ge(*e.at("ckvp", l, t))
                    A(ckv[:, t, :], unit("ckvp", l, t)[:, 0:288], ACT.Copy).then_inc(*e.inc("ckv", l, t, frees=("ckvp", l, t)))
                for t in range(2):
                    act.wait_ge(*e.at("xst", l, t))
                    A(xs[:, t, :], unit("xst", l, t)[:, :], ACT.Copy).then_inc(*e.inc("xs", l, t, frees=("xst", l, t)))
                act.wait_ge(*e.at("bt", l))
                A(btok[:, :, :], unit("bt", l)[:, 0:256].rearrange("p (g n) -> p g n", g=2), ACT.Copy).then_inc(*e.inc("btok", l, frees=("bt", l)))

                def gate(br, n):
                    for half in range(2):
                        ahead(until, (("g", l, br, n), half))
                    for t in range(2):
                        act.wait_ge(*e.at("gp", l, br, n, t))
                        if br != 0:
                            act.wait_ge(*e.at("merged", l, {2: 0, 1: 2}[br], n, t))
                        A(stripe(gates, n, t), unit("gp", l, br, n, t)[:, :], ACT.Sigmoid)\
                            .then_inc(*e.inc("gate_rows", l, br, n, t, frees=("gp", l, br, n, t)))

                def branch(br):
                    for n in range(2):
                        ahead(until, ("b", l, br, n))

                def scan_exps(c):
                    act.wait_ge(*e.at("diff", l, c))
                    A(E_[:, :, :], E_[:, :, :], ACT.Exp).then_inc(*e.inc("expE", l, c))
                    act.wait_ge(*e.at("dec", l, c))
                    A(small[:, 96:112], small[:, 96:112], ACT.Exp).then_inc(*e.inc("expc", l, c))

                gate(0, 0)
                scan_exps(0)
                gate(0, 1)
                act.wait_ge(*e.at("stp", l))
                A(st[:, :], unit("stp", l)[:, :], ACT.Copy).then_inc(*e.inc("st", l, frees=("stp", l)))
                turned_y(("a", l), 4, 256, ytT[1][0])
                branch(0)
                turned_y(("cq", l), 3, 256, cqTh, lambda c: col(0, QN + 3 * l + c))
                turned_y(("ck", l), 2, 256, ckTh, lambda c: col(0, KVN + 2 * l + c))
                gate(2, 0)
                scan_exps(1)
                gate(2, 1)
                for n in range(2):
                    ahead(until, ("q", l, n))
                    for t in range(2):
                        act.wait_ge(*e.at("qp", l, n, t))
                        A(qk[:, t, 4 * n:4 * n + 4, :],
                                 unit("qp", l, n, t)[:, 0:384].rearrange("p (h d) -> p h d", d=QK), ACT.Copy).then_inc(*e.inc("q", l, n, t, frees=("qp", l, n, t)))
                ahead(until, ("kv", l))
                act.wait_ge(*e.at("yd_in", l, 1))
                for n in range(2):
                    for t in range(2):
                        act.wait_ge(*e.at("kvp", l, n, t))
                        A(stripe(kv, n, t), unit("kvp", l, n, t)[:, :], ACT.Copy).then_inc(*e.inc("kv", l, n, t, frees=("kvp", l, n, t)))
                turned_y(("c", l), 4, 256, ytT[0][0], lambda c: col(0, SSN + 4 * l + c))
                branch(2)
                gate(1, 0)
                gate(1, 1)
                for h in range(HEADS):
                    act.wait_ge(*e.at("qkt", l, h))
                    A(qkT[0:QK, h, :], unit("qkt", l, h)[0:QK, :], ACT.Copy).then_inc(*e.inc("qkT", l, h, frees=("qkt", l, h)))
                for i in range(HEADS + 1):
                    if i < HEADS:
                        h = i
                        act.wait_ge(*e.at("nmax", l, h))
                        if h >= 2:
                            act.wait_ge(*e.at("ptp", l, h - 2))
                        o = 112 + 8 * (h % 2)
                        A(pr[:, h % 2, 0:P], unit("sc", l, h)[:, 0:P], ACT.Exp, scale=QK ** -0.5,
                          bias=small[:, o + 2:o + 3], accum_out=small[:, o + 4:o + 5])
                        m = A(pr[:, h % 2, P:384], unit("sc", l, h)[:, 256:512], ACT.Exp, scale=QK ** -0.5,
                              bias=small[:, o + 3:o + 4], accum_out=small[:, o + 5:o + 6])
                        m.then_inc(*e.inc("pr", l, h, frees=("sc", l, h)))
                    if i >= 1:
                        h = i - 1
                        act.wait_ge(*e.at("ptp", l, h))
                        if h >= 1:
                            act.wait_ge(*e.at("op", l, h - 1))
                        A(pT[:, :], unit("ptp", l, h)[:, 0:384], ACT.Copy).then_inc(*e.inc("pT", l, h, frees=("ptp", l, h)))
                turned_y(("b", l), 4, 256, ytT[1][0])
                branch(1)
                turned_y(("m", l), 8, 256, xT[256][0])
                for n in range(2):
                    for half in range(2):
                        ahead(until, (("wo", l, n), half))

            for l in range(DEPTH):
                norm(("f1", l), 256)
                turned(("f1", l), 256, gain1(NORM1 + 8 * l), None)
                ffn(("f1", l), 256, (), 18 * l)
                mixers(l)
                norm(("f2", l), 256)
                turned(("f2", l), 256, gain1(NORM2 + 8 * l), None)
                ffn(("f2", l), 256, (), 18 * l + MODS_PER_FFN)

            def block_two_ffn(name, l, j, T, whos):
                norm((name, l), T)
                turned((name, l), T, gain2, bias2(l, j))
                ffn((name, l), T, whos)

            block_two_ffn("g1", 0, 0, 512, (0, 1))
            norm(("r",), 512)
            turned(("r",), 512, gain2, bias2(0, 1))
            for who in range(2):
                for n in range(2):
                    act.wait_ge(*e.at("gbp", ("r",), who, n))
                    A(gbm[:, who, n * 512:(n + 1) * 512], unit("gbp", ("r",), who, n)[:, :], ACT.Copy).then_inc(*e.inc("gb", ("r",), who, n, frees=("gbp", ("r",), who, n)))
            for h in range(4):
                for part, dst in (("q", rq), ("k", rk)):
                    ahead(until, ("r" + part, h))
                    for i in range(2):
                        act.wait_ge(*e.at("r" + part + "p", h, i))
                        if h:
                            act.wait_ge(*e.at("rap", h - 1, 2))
                        A(dst[:, i, 256:512], unit("r" + part + "p", h, i)[:, 256:512], ACT.Copy).then_inc(*e.inc("r" + part + "c", h, i))
                for half in range(2):
                    ahead(until, (("rv", h), half))
                for t in range(4):
                    act.wait_ge(*e.at("rvp", h, t))
                    if h:
                        act.wait_ge(*e.at("rop", h - 1, 3))
                    A(rv[:, t, :], unit("rvp", h, t)[:, :], ACT.Copy).then_inc(*e.inc("rv", h, t, frees=("rvp", h, t)))
                for half in range(2):
                    ahead(until, (("rg", h), half))
                for t in range(4):
                    act.wait_ge(*e.at("rgp", h, t))
                    if h:
                        act.wait_ge(*e.at("ty", ("r", h - 1), 3))
                    A(rg[:, t, :], unit("rgp", h, t)[:, :], ACT.Silu).then_inc(*e.inc("rg", h, t, frees=("rgp", h, t)))
                dist = rcst[:, R_DIST:R_DIST + 512].rearrange("p (j i) -> p j i", j=2)
                act.wait_ge(*e.at("lg"))
                if h:
                    act.wait_ge(*e.at("ra", h - 1, 2))
                act.wait_ge(*e.at("wlog", h))
                A(WX[:, :, 1, :], WX[:, :, 1, :], ACT.Exp)
                A(WX[:, :, 0, :], dist, ACT.Exp, scale=lgs[:, 2, h:h + 1], bias=lgs[:, 3, h:h + 1])
                m = A(wtmp[:, :, 0, :], dist, ACT.Exp, scale=lgs[:, 4, 4 + h:5 + h], bias=lgs[:, 3, 4 + h:5 + h])
                m.then_inc(*e.inc("wexp", h))
                turned_y(("r", h), 4, 512, rYh, lambda c, h=h: col(1, GN + 4 * h + c))
                for n in range(2):
                    ahead(until, ("rw", h, n))
                    if h == 0:
                        for t in range(4):
                            act.wait_ge(*e.at("rwp", 0, n, t))
                            A(stripe(Y, n, t), unit("rwp", 0, n, t)[:, :], ACT.Copy).then_inc(*e.inc("Y0", n, t, frees=("rwp", 0, n, t)))
            block_two_ffn("g2", 0, 2, 512, (0, 1))
            block_two_ffn("g1", 1, 0, 512, (0, 1))
            norm(("n",), 512)
            turned(("n",), 512, gain2, bias2(1, 1))
            for j in range(4):
                ahead(until, ("nq", j))
                act.wait_ge(*e.at("nqp", j))
                A(nq[:, 2 * j:2 * j + 2, :], unit("nqp", j)[:, :].rearrange("p (m t) -> p m t", m=2), ACT.Copy,
                         scale=0.125).then_inc(*e.inc("nq", j, frees=("nqp", j)))
            for j in range(4):
                ahead(until, ("nk", j))
                for i in range(2):
                    act.wait_ge(*e.at("nkp", j, i))
                    A(nk[:, 2 * j + i, :], unit("nkp", j, i)[:, :], ACT.Copy).then_inc(*e.inc("nk", j, i, frees=("nkp", j, i)))
            for n in range(2):
                for half in range(2):
                    ahead(until, (("nv", n), half))
                for t in range(4):
                    act.wait_ge(*e.at("nvp", n, t))
                    A(stripe(nv, n, t), unit("nvp", n, t)[:, :], ACT.Copy).then_inc(*e.inc("nv", n, t, frees=("nvp", n, t)))
            items = [(h, t) for h in range(16) for t in range(2)]
            for i, (h, t) in enumerate(items):
                act.wait_ge(*e.at("nnm", h, t))
                if h:
                    act.wait_ge(*e.at("nptp", h - 1, t))
                o = 128 + 4 * (i % 4)
                m = A(npr[:, t, :], unit("nsp", h, t)[:, :], ACT.Exp, bias=small[:, o + 1:o + 2],
                      accum_out=small[:, o + 2:o + 3])
                m.then_inc(*e.inc("npr", h, t, frees=("nsp", h, t)))
            for n in range(2):
                act.wait_ge(*e.at("gbp", ("n",), 0, n))
                A(gbm[:, 0, n * 512:(n + 1) * 512], unit("gbp", ("n",), 0, n)[:, :], ACT.Copy).then_inc(*e.inc("gb", ("n",), 0, n, frees=("gbp", ("n",), 0, n)))
            turned_y(("n",), 8, 256, xT[256][0])
            for n in range(2):
                for half in range(2):
                    ahead(until, (("nw", n), half))
            block_two_ffn("g2", 1, 2, 256, (0,))
            norm(("last",), 256)

        @block.vector
        def _(dve):
            e = Signals(L, "dve")
            chained = [0]

            def link(ins):
                chained[0] += 1
                ins.then_inc(L.sem("dve_chain"), 1)
                dve.wait_ge(L.sem("dve_chain"), chained[0])

            split = [0]

            def until(s):
                while split[0] <= min(s, len(slabs.parts) - 1):
                    key, part = slabs.parts[split[0]][0:2]
                    split[0] += 1
                    src, hi, lo = part_views(key, part)
                    dve.wait_ge(*e.at("hi", key, part))
                    nc.vector.tensor_tensor(lo, src, hi.bitcast(F32), ALU.subtract).then_inc(*e.inc("lo", key, part))

            V = nc.vector
            TT, TS, STT = V.tensor_tensor, V.tensor_scalar, V.scalar_tensor_tensor

            def sumsq(dst, a, junk):
                return V.tensor_tensor_reduce(junk, a, a, 1.0, 0.0, ALU.mult, ALU.add, dst)

            def rstd(name, src, n, width):
                TS(src, src, 1.0 / width, EPS, ALU.mult, ALU.add).then_inc(*e.inc("ms", name))
                dve.wait_ge(*e.at("rstd", name))

            def norm(name, T):
                for t in tiles_of(T):
                    if t % 2 == 0:
                        link(sumsq(small[:, t:t + 1], X[:, t, :], junk_v[:, :]))
                for t in tiles_of(T):
                    if t % 2:
                        dve.wait_ge(*e.at("ssa", name, t))
                rstd(name, small[:, 0:T // P], T // P, D)
                for t in tiles_of(T):
                    if t % 2 == 0:
                        TS(xn[:, t, :], X[:, t, :], small[:, 8 + t:9 + t], None, ALU.mult).then_inc(*e.inc("xn", name, t))

            def turned(name, T, gain, bias):
                xTh, xTl = xT[T]
                for k in range(KD):
                    ps = unit("turn", name, k)
                    dve.wait_ge(*e.at("turn", name, k))
                    whos = range(T // 256) if bias else (0,)
                    dve.wait_ge(*e.at("xh", name, k, whos[-1]))
                    for who in whos:
                        a, b = who * 256, who * 256 + 256
                        m = STT(xTl[:, k, a:b], ps[:, a:b], gain(k, who), xTh[:, k, a:b].bitcast(F32),
                                ALU.mult, ALU.subtract)
                        if bias:
                            link(m)
                            m = TS(xTl[:, k, a:b], xTl[:, k, a:b].bitcast(F32), bias(k, who), None, ALU.add)
                    m.then_inc(*e.inc("xT", name, k, frees=("turn", name, k)))

            def turned_y(name, chunks, T, dsth, dstl, gain=None):
                per = 512 // T
                for u in range((chunks + per - 1) // per):
                    dve.wait_ge(*e.at("ty", name, u))
                    ps = unit("ty", name, u)
                    if gain is None:
                        dve.wait_ge(*e.at("yh", name, u))
                        m = TT(dstl[:, u * per:(u + 1) * per, 0:T], ps[:, :].rearrange("p (j t) -> p j t", t=T),
                               dsth[:, u * per:(u + 1) * per, 0:T].bitcast(F32), ALU.subtract)
                        m.then_inc(*e.inc("yT", name, u, frees=("ty", name, u)))
                    else:
                        n = min(per, chunks - u * per)
                        dve.wait_ge(*e.at("yh", name, u * per + n - 1))
                        for j in range(n):
                            c = u * per + j
                            m = STT(dstl[:, c, 0:T], ps[:, j * T:(j + 1) * T], gain(c),
                                    dsth[:, c, 0:T].bitcast(F32), ALU.mult, ALU.subtract)
                            m.then_inc(*e.inc("yT", name, c, frees=("ty", name, u) if j == n - 1 else None))

            def mod_row(i):
                dve.wait_ge(*e.at("modp", i))
                if i:
                    dve.wait_ge(*e.at("modtp", i - 1))
                V.tensor_copy(modrow[:, :], unit("modp", i)[0:4, :]).then_inc(*e.inc("modrow", i, frees=("modp", i)))

            def mod_cols(i):
                l, g = divmod(i, 18)
                dve.wait_ge(*e.at("modtp", i))
                ps = unit("modtp", i)[:, 0:16].rearrange("p (c w) -> p c w", w=4)
                V.tensor_copy(modt[:, :, :], ps).then_inc(*e.inc("modt", i, frees=("modtp", i)))
                dve.wait_ge(*e.at("modt", i))
                link(TT(modt[:, :, 0:2], modt[:, :, 0:2], modt[:, :, 2:4], ALU.add))
                b = cols[:, 2 + l, BM + 4 * g:BM + 4 * g + 4].unsqueeze(2).to_broadcast([P, 4, 2])
                TT(modc[:, l, 4 * g:4 * g + 4, :], modt[:, :, 0:2], b, ALU.add).then_inc(*e.inc("modc", i))

            def affine(name, l, j):
                g = cols[:, 0, NORMG + 24 * l + 8 * j:NORMG + 24 * l + 8 * j + 8].unsqueeze(2)\
                    .to_broadcast([P, 8, 2])
                m = STT(aff[:, :, :], modc[:, l, (j * 3 + 1) * 8:(j * 3 + 2) * 8, :], 1.0, g, ALU.add, ALU.mult)
                m.then_inc(*e.inc("aff", name))
                dve.wait_ge(*e.at("aff", name))

            def diagonals(name, l, j, dgt, whos):
                for who in whos:
                    if who:
                        dve.wait_ge(*e.at("gbp", name, who - 1, 1))
                    gcol = modc[:, l, (j * 3 + 2) * 8:(j * 3 + 3) * 8, who:who + 1].to_broadcast([P, 8, P])
                    TT(dgt[:, :, :], ident.unsqueeze(1).to_broadcast([P, 8, P]), gcol, ALU.mult).then_inc(*e.inc("diag", name, who))

            def ffn(name, T, mod0, l=0, j=0, whos=(), nxt=None):
                per = T // 256
                for g in range(GROUPS):
                    ahead(until, (name, "gate", g))
                    ahead(until, (name, "up", g))
                    for i in range(per):
                        b = (g * per + i) % 2
                        o = (g * per + i) * 512
                        dve.wait_ge(*e.at("sg", name, g, i))
                        dve.wait_ge(*e.at("up", name, g, i))
                        TT(sg[:, b, :], sg[:, b, :], unit("up", name, g, i)[:, :], ALU.mult).then_inc(*e.inc("ht", name, g, i, frees=("up", name, g, i)))
                    for i in range(per):
                        b = (g * per + i) % 2
                        o = (g * per + i) * 512
                        dve.wait_ge(*e.at("ht", name, g, i))
                        dve.wait_ge(*e.at("hhi", name, g, i))
                        TT(hl[:, o:o + 512], sg[:, b, :], hh[:, o:o + 512].bitcast(F32), ALU.subtract).then_inc(*e.inc("hidden", name, g, i))
                    if mod0 is not None:
                        if 0 < g <= MODS_PER_FFN:
                            mod_cols(mod0 + g - 1)
                        if g < MODS_PER_FFN:
                            for half in range(2):
                                ahead(until, ("mod", mod0 + g, half))
                            mod_row(mod0 + g)
                if whos:
                    dve.wait_ge(*e.at("up", name, GROUPS - 1, per - 1))
                    diagonals(name, l, j, dg, whos)
                for n in range(2):
                    for d in range(6):
                        ahead(until, (name, "down", n, d))
                    for t in tiles_of(T):
                        dve.wait_ge(*e.at("down", name, n, t))
                        ps = unit("down", name, n, t)
                        if not whos:
                            m = STT(stripe(X, n, t), ps[:, :], 0.5, stripe(X, n, t), ALU.mult, ALU.add)
                            m.then_inc(*e.inc("Xd", name, n, t, also=[("X", nxt, t)], frees=("down", name, n, t)))
                        else:
                            dve.wait_ge(*e.at("gb", name, t // 2, 1))
                            m = TT(sg[:, t % 2, :], ps[:, :], stripe(gb, n, t // 2), ALU.mult)
                            m.then_inc(*e.inc("sgg", name, n, t, frees=("down", name, n, t)))
                            dve.wait_ge(*e.at("sgg", name, n, t))
                            m = TT(stripe(X, n, t), sg[:, t % 2, :], stripe(X, n, t), ALU.add)
                            m.then_inc(*e.inc("Xd", name, n, t, also=[("X", nxt, t)]))
                dve.wait_ge(*e.at("Xd", name, 1, T // P - 1))

            until(NSPLIT - 2)
            for i in range(4):
                dve.wait_ge(*e.at("cols", i))
                V.tensor_copy(cols[:, i, 0:ROWS[i]], unit("cols", i)[:, 0:ROWS[i]]).then_inc(*e.inc("cols_copied", i, also=[("aff", n) for n in [("f1", 0), ("f1", 1), ("mx", 0), ("mx", 1), ("f2", 0), ("f2", 1)]], frees=("cols", i)))
            dve.wait_ge(L.sem("params_landed"), L.all_params())
            dve.wait_ge(*e.at("cols_copied", 3))
            pos = bsum[:, 4:6]
            link(V.tensor_copy(pos, bsum[:, 0:2].bitcast(I32)))
            for t in range(2):
                a = cs16[:, t, 0, :]
                r = small[:, 144:160]
                link(TS(a, cst[:, C_FREQ:C_FREQ + 16], bsum[:, 4 + t:5 + t], None, ALU.mult))
                link(TS(r, a, 1.0 / TWO_PI, None, ALU.mult))
                link(TS(r, r, 12582912.0, None, ALU.add))
                link(TS(r, r, -12582912.0, None, ALU.add))
                for c in (TP1, TP2, TP3):
                    link(STT(a, r, -c, a, ALU.mult, ALU.add))
                link(TS(cs16[:, t, 1, :], a, -1.0, None, ALU.mult))
                link(TT(cs16[:, t, 1, :], cs16[:, t, 1, :], a, ALU.min))
                link(TS(cs16[:, t, 1, :], cs16[:, t, 1, :], TWO_PI / 4, None, ALU.add))
                TS(a, a, 3.1415925, -3.1415925, ALU.min, ALU.max).then_inc(*e.inc("angles"))

            def log1p(x, s, y, q):
                link(TS(s, x, 2.0, None, ALU.add))
                link(V.reciprocal(s, s))
                link(TT(s, s, x, ALU.mult))
                link(TT(y, s, s, ALU.mult))
                link(TS(q, y, 1.0 / 17, None, ALU.mult))
                for k in (15, 13, 11, 9, 7, 5, 3):
                    link(STT(q, q, 1.0 / k, y, ALU.add, ALU.mult))
                link(STT(q, q, 1.0, s, ALU.add, ALU.mult))
                return q

            d = lgs[:, 0, :]
            link(TS(lgs[:, 1, :], d, -1.0, None, ALU.mult))
            TT(lgs[:, 1, :], lgs[:, 1, :], d, ALU.min).then_inc(*e.inc("lgx"))
            dve.wait_ge(*e.at("lge"))
            q = log1p(lgs[:, 1, :], lgs[:, 5, :], lgs[:, 6, :], lgs[:, 7, :])
            link(TS(d, d, 0.0, None, ALU.min))
            link(STT(lgs[:, 2, :], q, -2.0, d, ALU.mult, ALU.add))
            link(TS(lgs[:, 3, :], lgs[:, 2, :], 256.0, None, ALU.mult))
            TS(lgs[:, 4, :], lgs[:, 2, :], -1.0, None, ALU.mult).then_inc(*e.inc("lg"))
            dve.wait_ge(*e.at("lg"))
            dve.wait_ge(*e.at("alog"))
            link(TS(dtb[:, 1, :, :], dtb[:, 1, :, :], -1.0, None, ALU.mult))

            gain1 = lambda row: (lambda k, who: col(0, row + k))
            gain2 = lambda k, who: aff[:, k, who:who + 1]

            def bias2(l, j):
                return lambda k, who: modc[:, l, (j * 3) * 8 + k, who:who + 1]

            dve.wait_ge(*e.at("sc4hi"))
            TT(sc4[:, :, 2:4], scc[:, :, :], sc4[:, :, 0:2].bitcast(F32), ALU.subtract).then_inc(*e.inc("sc4"))

            def heads(a, n, width):
                return a.unsqueeze(2).to_broadcast([P, n, width])

            def mixers(l):
                nm = ("mx", l)
                norm(nm, 256)
                turned(nm, 256, gain1(NORMX + 8 * l), None)
                for i in range(4):
                    ahead(until, ("xbc", l, i))
                ahead(until, ("dt", l))
                dtv, dte = small[:, 16:32], small[:, 64:80]
                for t in range(2):
                    dve.wait_ge(*e.at("dtp", l, t))
                    m = TT(small[:, 16 + 8 * t:24 + 8 * t], unit("dtp", l, t)[:, 0:8], dtb[:, 0, l, :], ALU.add)
                    m.then_inc(*e.inc("dtr", l, t, frees=("dtp", l, t)))
                    dve.wait_ge(*e.at("dtr", l, t))
                link(TS(dte, dtv, -1.0, None, ALU.mult))
                TT(dte, dte, dtv, ALU.min).then_inc(*e.inc("dtn", l))
                for i in range(4):
                    dve.wait_ge(*e.at("xr", l, i))
                for tap in range(4):
                    for ch in range(8):
                        wc = col(1, CVW + 32 * l + 8 * tap + ch)
                        src = xr[:, ch, tap:tap + 256]
                        if tap == 0:
                            m = TS(cv[:, ch, :], src, wc, None, ALU.mult)
                        else:
                            m = STT(cv[:, ch, :], src, wc, cv[:, ch, :], ALU.mult, ALU.add)
                    if tap < 3:
                        link(m)
                    else:
                        m.then_inc(*e.inc("conv", l))
                    ahead(until, (("z", l), tap % 2))
                dve.wait_ge(*e.at("dte", l))
                q = log1p(dte, small[:, 160:176], small[:, 176:192], small[:, 192:208])
                link(TS(dtv, dtv, 0.0, None, ALU.max))
                link(STT(dtv, q, 2.0, dtv, ALU.mult, ALU.add))
                for t in range(2):
                    link(TT(small[:, 32 + 8 * t:40 + 8 * t], small[:, 16 + 8 * t:24 + 8 * t], dtb[:, 1, l, :], ALU.mult))
                h64 = lambda a: a.rearrange("p (h d) -> p h d", d=64)

                def gate(br, n, half):
                    ahead(until, (("g", l, br, n), half))

                def branch(br):
                    for n in range(2):
                        ahead(until, ("b", l, br, n))
                        for t in range(2):
                            dve.wait_ge(*e.at("bp", l, br, n, t))
                            dve.wait_ge(*e.at("gate_rows", l, br, n, t))
                            ps = unit("bp", l, br, n, t)
                            if br == 0:
                                TT(stripe(merged, n, t), ps[:, :], stripe(gates, n, t), ALU.mult)\
                                    .then_inc(*e.inc("merged", l, br, n, t, frees=("bp", l, br, n, t)))
                            else:
                                m = TT(tmp[:, t, :], ps[:, :], stripe(gates, n, t), ALU.mult)
                                m.then_inc(*e.inc("mtmp", l, br, n, t, frees=("bp", l, br, n, t)))
                                dve.wait_ge(*e.at("mtmp", l, br, n, t))
                                TT(stripe(merged, n, t), tmp[:, t, :], stripe(merged, n, t), ALU.add)\
                                    .then_inc(*e.inc("merged", l, br, n, t, also=[("mg", l, t)] if br == 1 and n == 1 else []))

                def scan_decays(c):
                    TT(E_[:, :, :], upper.unsqueeze(1).to_broadcast([P, 8, P]),
                       heads(small[:, 32 + 8 * c:40 + 8 * c], 8, P), ALU.mult).then_inc(*e.inc("daU", l, c))

                def scan_differences(c):
                    dve.wait_ge(*e.at("xs", l, c))
                    if c:
                        dve.wait_ge(*e.at("stp", l))
                    link(TT(h64(xdt[:, :]), h64(xs[:, c, :]), heads(small[:, 16 + 8 * c:24 + 8 * c], 8, 64), ALU.mult))
                    dve.wait_ge(*e.at("csp", l, c))
                    csc = small[:, 80:96]
                    V.tensor_copy(csc, unit("csp", l, c)[:, 0:16]).then_inc(*e.inc("csc", l, c, frees=("csp", l, c)))
                    dve.wait_ge(*e.at("csc", l, c))
                    V.tensor_copy(small[:, 96:104], csc[:, 0:8])
                    TT(small[:, 104:112], csc[:, 8:16], csc[:, 0:8], ALU.subtract).then_inc(*e.inc("dec", l, c))
                    for h2 in range(2):
                        dve.wait_ge(*e.at("csb", l, c, h2))
                    for h2 in range(2):
                        for h in range(4):
                            m = TS(E_[:, 4 * h2 + h, :], unit("csb", l, c, h2)[:, h * P:(h + 1) * P],
                                   csc[:, 4 * h2 + h:4 * h2 + h + 1], 0.0, ALU.subtract, ALU.min)
                        m.then_inc(*e.inc("diff_half", l, c, h2, also=[("diff", l, c)], frees=("csb", l, c, h2)))
                    dve.wait_ge(*e.at("cbp", l, c))
                    TT(cbm[:, :, :], unit("cbp", l, c)[:, 0:256].rearrange("p (g t) -> p g t", g=2),
                       upper.unsqueeze(1).to_broadcast([P, 2, P]), ALU.mult).then_inc(*e.inc("cbm", l, c, frees=("cbp", l, c)))

                def scan_weights(c):
                    dve.wait_ge(*e.at("expE", l, c))
                    dve.wait_ge(*e.at("cbm", l, c))
                    for g in range(2):
                        m = TT(E_[:, 4 * g:4 * g + 4, :], E_[:, 4 * g:4 * g + 4, :],
                               cbm[:, g:g + 1, :].to_broadcast([P, 4, P]), ALU.mult)
                    m.then_inc(*e.inc("MT", l, c))
                    dve.wait_ge(*e.at("expc", l, c))
                    if c == 0:
                        TT(h64(xdd[:, :]), h64(xdt[:, :]), heads(small[:, 104:112], 8, 64), ALU.mult).then_inc(*e.inc("xdd", l))

                def scan_rows(c):
                    link(TT(h64(tmp[:, 0, :]), h64(xs[:, c, :]), heads(dtb[:, 2, l, :], 8, 64), ALU.mult))
                    dve.wait_ge(*e.at("yd", l, c))
                    m = TT(tmp[:, 0, :], unit("yd", l, c)[:, :], tmp[:, 0, :], ALU.add)
                    m.then_inc(*e.inc("yd_in", l, c, frees=("yd", l, c)))
                    dve.wait_ge(*e.at("yd_in", l, c))
                    if c:
                        dve.wait_ge(*e.at("yo", l))
                        m = TT(h64(tmp[:, 1, :]), h64(unit("yo", l)[:, :]), heads(small[:, 96:104], 8, 64), ALU.mult)
                        m.then_inc(*e.inc("yo_in", l, frees=("yo", l)))
                        dve.wait_ge(*e.at("yo_in", l))
                        link(TT(tmp[:, 0, :], tmp[:, 0, :], tmp[:, 1, :], ALU.add))
                    dve.wait_ge(*e.at("z", l, c))
                    link(TT(z[:, c, :], z[:, c, :], tmp[:, 0, :], ALU.mult))

                def scan_norm(c):
                    for g in range(2):
                        link(sumsq(small[:, 216 + g:217 + g], z[:, c, g * 256:(g + 1) * 256], tmp[:, 1, 0:256]))
                    rstd(("yc", l, c), small[:, 216:218], 2, 256)
                    for g in range(2):
                        m = TS(z[:, c, g * 256:(g + 1) * 256], z[:, c, g * 256:(g + 1) * 256],
                               small[:, 218 + g:219 + g], None, ALU.mult)
                    m.then_inc(*e.inc("yc", l, c))

                scan_decays(0)
                for n in range(2):
                    for half in range(2):
                        ahead(until, (("uv", l, n), half))
                for half in range(2):
                    ahead(until, (("cq", l), half))
                for half in range(2):
                    ahead(until, (("ckv", l), half))
                for t in range(2):
                    dve.wait_ge(*e.at("uv", l, 1, t))
                    link(sumsq(small[:, 48 + t:49 + t], gv[:, t, :], junk512))
                rstd(("gv", l), small[:, 48:50], 2, 512)
                dve.wait_ge(L.sem("vgain_landed"), 16 * (l + 1))
                for t in range(2):
                    STT(gv[:, t, :], gv[:, t, :], small[:, 50 + t:51 + t], vgain[:, :], ALU.mult, ALU.mult).then_inc(*e.inc("gvn", l, t))
                gate(0, 0, 0)
                scan_differences(0)
                gate(0, 0, 1)
                dve.wait_ge(*e.at("wst", l))
                TT(wT[:, :, :], unit("wst", l)[:, :].rearrange("p (g t) -> p g t", g=4),
                   upper.unsqueeze(1).to_broadcast([P, 4, P]), ALU.mult).then_inc(*e.inc("wT", l, frees=("wst", l)))
                gate(0, 1, 0)
                scan_weights(0)
                for name, a, n, s in (("cq", cq, 384, 208), ("ck", ckv, 256, 212)):
                    for t in range(2):
                        dve.wait_ge(*e.at({"cq": "cq", "ck": "ckv"}[name], l, t))
                        link(sumsq(small[:, s + t:s + t + 1], a[:, t, 0:n], junk512[:, 0:n]))
                    rstd((name, l), small[:, s:s + 2], 2, n)
                    for t in range(2):
                        TS(a[:, t, 0:n], a[:, t, 0:n], small[:, s + 2 + t:s + 3 + t], None, ALU.mult).then_inc(*e.inc(name + "n", l, t))
                gate(0, 1, 1)
                for t in range(2):
                    dve.wait_ge(*e.at("spp", l, t))
                    dve.wait_ge(*e.at("uv", l, 0, t))
                    ps = unit("spp", l, t)
                    for g in range(4):
                        s = slice(g * P, (g + 1) * P)
                        m = STT(gu[:, t, s], ps[:, s], col(1, BS + 4 * l + g), gu[:, t, s], ALU.add, ALU.mult)
                    m.then_inc(*e.inc("ya", l, t, frees=("spp", l, t)))
                turned_y(("a", l), 4, 256, *ytT[1])
                scan_rows(0)
                scan_decays(1)
                branch(0)
                turned_y(("cq", l), 3, 256, cqTh, cqTl, lambda c: col(0, QN + 3 * l + c))
                turned_y(("ck", l), 2, 256, ckTh, ckTl, lambda c: col(0, KVN + 2 * l + c))
                gate(2, 0, 0)
                scan_differences(1)
                gate(2, 0, 1)
                scan_norm(0)
                gate(2, 1, 0)
                scan_weights(1)
                gate(2, 1, 1)
                scan_rows(1)
                ahead(until, ("q", l, 0))
                scan_norm(1)
                ahead(until, ("q", l, 1))
                ahead(until, ("kv", l))
                turned_y(("c", l), 4, 256, *ytT[0], gain=lambda c: col(0, SSN + 4 * l + c))
                branch(2)
                for n in range(2):
                    for t in range(2):
                        dve.wait_ge(*e.at("q", l, n, t))
                        dve.wait_ge(*e.at("kv", l, n, t))
                for t in range(2):
                    kk = kv[:, t, :].rearrange("p (h d) -> p h d", d=P)
                    V.tensor_copy(qk[:, t, 8:16, 0:64], kk[:, :, 0:64])
                    link(V.tensor_copy(qk[:, t, 8:16, 64:96],
                                         ckv[:, t, 256:288].unsqueeze(1).to_broadcast([P, 8, 32])))
                for t in range(2):
                    a = qk[:, t, :, :]
                    gate(1, 0, t)
                    link(TT(sq[:, :, :], a, a, ALU.mult))
                    link(V.tensor_reduce(small[:, 224:240], sq[:, :, :], AX, ALU.add))
                    rstd(("qk", l, t), small[:, 224:240], 16, QK)
                    link(TT(a, a, heads(small[:, 240:256], 16, QK), ALU.mult))
                    for i in range(2):
                        m = TT(qk[:, t, 8 * i:8 * i + 8, :], qk[:, t, 8 * i:8 * i + 8, :],
                               qkg[:, l, i:i + 1, :].to_broadcast([P, 8, QK]), ALU.mult)
                    link(m)
                    gate(1, 1, t)
                    x1, x2 = a[:, :, 64:80], a[:, :, 80:96]
                    sn, cn = (cs16[:, t, i:i + 1, :].to_broadcast([P, 16, 16]) for i in range(2))
                    dve.wait_ge(*e.at("sincos"))
                    q4 = [sq[:, :, 16 * i:16 * i + 16] for i in range(4)]
                    TT(q4[0], x1, cn, ALU.mult)
                    TT(q4[1], x2, sn, ALU.mult)
                    TT(q4[2], x2, cn, ALU.mult)
                    link(TT(q4[3], x1, sn, ALU.mult))
                    TT(x1, q4[0], q4[1], ALU.subtract)
                    TT(x2, q4[2], q4[3], ALU.add).then_inc(*e.inc("qkr", l, t))
                    dve.wait_ge(*e.at("qkr", l, t))
                for i in range(HEADS + 2):
                    if i < HEADS:
                        h = i
                        o = 112 + 8 * (h % 2)
                        dve.wait_ge(*e.at("sc", l, h))
                        ps = unit("sc", l, h)
                        dv = ps[:, :].rearrange("p (a b) -> p a b", b=P)[:, 0:4:3, :]
                        link(TT(dv, dv, cst[:, C_CAUSAL:C_CAUSAL + P].unsqueeze(1).to_broadcast([P, 2, P]), ALU.add))
                        V.tensor_reduce(small[:, o:o + 1], ps[:, 0:P], AX, ALU.max)
                        link(V.tensor_reduce(small[:, o + 1:o + 2], ps[:, 256:512], AX, ALU.max))
                        TS(small[:, o + 2:o + 4], small[:, o:o + 2], -QK ** -0.5, None, ALU.mult).then_inc(*e.inc("nmax", l, h))
                    if i >= 2:
                        h = i - 2
                        o = 112 + 8 * (h % 2)
                        dve.wait_ge(*e.at("op", l, h))
                        for t in range(2):
                            m = TS(yb[:, t, h * 64:(h + 1) * 64], unit("op", l, h)[:, 64 * t:64 * t + 64],
                                   small[:, o + 6 + t:o + 7 + t], None, ALU.mult)
                        m.then_inc(*e.inc("yb_head", l, h, also=[("yb", l, 0), ("yb", l, 1)], frees=("op", l, h)))
                    if 1 <= i <= HEADS:
                        h = i - 1
                        o = 112 + 8 * (h % 2)
                        dve.wait_ge(*e.at("pr", l, h))
                        link(V.reciprocal(small[:, o + 6:o + 8], small[:, o + 4:o + 6]))
                turned_y(("b", l), 4, 256, *ytT[1])
                branch(1)
                turned_y(("m", l), 8, 256, *xT[256])
                for n in range(2):
                    for half in range(2):
                        ahead(until, (("wo", l, n), half))
                    for t in range(2):
                        dve.wait_ge(*e.at("wop", l, n, t))
                        m = TT(stripe(X, n, t), unit("wop", l, n, t)[:, :], stripe(X, n, t), ALU.add)
                        m.then_inc(*e.inc("Xw", l, n, t, also=[("X", ("f2", l), t)], frees=("wop", l, n, t)))
                dve.wait_ge(*e.at("Xw", l, 1, 1))

            junk512 = tmp[:, 1, :]
            for l in range(DEPTH):
                if l == 0:
                    dve.wait_ge(L.sem("x_landed"), 16)
                    V.memset(small[:, 0:4], 0.0).then_inc(*e.inc("X", ("f1", 0), 1))
                    dve.wait_ge(*e.at("X", ("f1", 0), 1))
                norm(("f1", l), 256)
                turned(("f1", l), 256, gain1(NORM1 + 8 * l), None)
                ffn(("f1", l), 256, 18 * l, nxt=("mx", l))
                mixers(l)
                norm(("f2", l), 256)
                turned(("f2", l), 256, gain1(NORM2 + 8 * l), None)
                ffn(("f2", l), 256, 18 * l + MODS_PER_FFN, nxt=("f1", l + 1) if l == 0 else ("g1", 0))

            def block_two_ffn(name, l, j, T, whos, nxt):
                nm = (name, l)
                if nm == ("g1", 0):
                    V.memset(small[:, 0:4], 0.0).then_inc(*e.inc("ctx_ready", also=[("X", nm, t) for t in (1, 3)]))
                    dve.wait_ge(*e.at("ctx_ready"))
                affine(nm, l, j)
                norm(nm, T)
                turned(nm, T, gain2, bias2(l, j))
                ffn(nm, T, None, l, j, whos, nxt)

            block_two_ffn("g1", 0, 0, 512, (0, 1), ("r",))
            affine(("r",), 0, 1)
            norm(("r",), 512)
            turned(("r",), 512, gain2, bias2(0, 1))
            diagonals(("r",), 0, 1, dgm, (0, 1))
            dist = rcst[:, R_DIST:R_DIST + 512].rearrange("p (j i) -> p j i", j=2)
            cosT, sinT = rcst[:, R_COS:R_COS + 256], rcst[:, R_SIN:R_SIN + 256]
            dve.wait_ge(L.sem("rcst_landed"), 16)
            for h in range(4):
                for part, dst in (("q", rq), ("k", rk)):
                    ahead(until, ("r" + part, h))
                    p0, p1 = (unit("r" + part + "p", h, i)[:, 0:256] for i in range(2))
                    for i in range(2):
                        dve.wait_ge(*e.at("r" + part + "c", h, i))
                    if h:
                        dve.wait_ge(*e.at("rap", h - 1, 2))
                    r0, r1 = rt[:, 0, 0:256], rt[:, 0, 256:512]
                    TT(dst[:, 0, 0:256], p0, cosT, ALU.mult)
                    TT(r0, p1, sinT, ALU.mult)
                    TT(dst[:, 1, 0:256], p1, cosT, ALU.mult)
                    link(TT(r1, p0, sinT, ALU.mult))
                    TT(dst[:, 0, 0:256], dst[:, 0, 0:256], r0, ALU.subtract)
                    m = TT(dst[:, 1, 0:256], dst[:, 1, 0:256], r1, ALU.add)
                    m.then_inc(*e.inc("rope", h, part, also=[("rqk", h)], frees=("r" + part + "p", h, 0)))
                    L.freed[("r" + part + "p", h, 1)] = L.events[("rope", h, part)]
                    dve.wait_ge(*e.at("rope", h, part))
                for part in "vg":
                    for half in range(2):
                        ahead(until, (("r" + part, h), half))
                if h:
                    dve.wait_ge(*e.at("ra", h - 1, 2))
                V.tensor_scalar(WX[:, :, 1, :], dist, 0.0, lgs[:, 2, h:h + 1], ALU.max, ALU.mult)
                link(V.tensor_scalar(wtmp[:, :, 1, :], dist, 0.0, lgs[:, 4, 4 + h:5 + h], ALU.min, ALU.mult))
                TT(WX[:, :, 1, :], WX[:, :, 1, :], wtmp[:, :, 1, :], ALU.add).then_inc(*e.inc("wlog", h))
                dve.wait_ge(*e.at("wexp", h))
                link(TT(WX[:, :, 0, :], WX[:, :, 0, :], wtmp[:, :, 0, :], ALU.add))
                if h:
                    dve.wait_ge(*e.at("rop", h - 1, 3))
                for u in range(3):
                    dve.wait_ge(*e.at("rap", h, u))
                    ps = unit("rap", h, u)[:, :].rearrange("p (a i) -> p a i", a=2)
                    wv = WX[:, :, 1, :] if u == 0 else WX[:, u - 1, :, :]
                    STT(ra[:, u, :].rearrange("p (a i) -> p a i", a=2), ps, 1.0 / 16, wv, ALU.mult, ALU.mult).then_inc(*e.inc("ra", h, u, frees=("rap", h, u)))
                for t in range(4):
                    o = 144 + 16 * (t % 2)
                    dve.wait_ge(*e.at("rop", h, t))
                    ps = unit("rop", h, t)
                    link(V.bn_stats(small[:, o:o + 6], ps[:, :]))
                    link(V.bn_aggr(small[:, o + 6:o + 8], small[:, o:o + 6]))
                    rstd(("ro", h, t), small[:, o + 7:o + 8], 1, 1)
                    m = TS(rt[:, t % 2, :], ps[:, :], small[:, o + 6:o + 7], small[:, o + 8:o + 9],
                           ALU.subtract, ALU.mult)
                    m.then_inc(*e.inc("rn", h, t, frees=("rop", h, t)))
                    dve.wait_ge(*e.at("rn", h, t))
                    dve.wait_ge(*e.at("rg", h, t))
                    TT(rg[:, t, :], rg[:, t, :], rt[:, t % 2, :], ALU.mult).then_inc(*e.inc("ry", h, t))
                turned_y(("r", h), 4, 512, rYh, rYl, lambda c, h=h: col(1, GN + 4 * h + c))
                for n in range(2):
                    ahead(until, ("rw", h, n))
                    for t in range(4):
                        if h:
                            dve.wait_ge(*e.at("rwp", h, n, t))
                            if h == 1:
                                dve.wait_ge(*e.at("Y0", n, t))
                            TT(stripe(Y, n, t), unit("rwp", h, n, t)[:, :], stripe(Y, n, t), ALU.add).then_inc(*e.inc("Y", h, n, t, frees=("rwp", h, n, t)))
            dve.wait_ge(*e.at("Y", 3, 1, 3))
            for t in range(4):
                dve.wait_ge(*e.at("gb", ("r",), t // 2, 1))
                link(TT(Y[:, t, :], Y[:, t, :], gbm[:, t // 2, :], ALU.mult))
                TT(X[:, t, :], X[:, t, :], Y[:, t, :], ALU.add).then_inc(*e.inc("Xr", t, also=[("X", ("g2", 0), t)]))
            dve.wait_ge(*e.at("Xr", 3))
            block_two_ffn("g2", 0, 2, 512, (0, 1), ("g1", 1))
            block_two_ffn("g1", 1, 0, 512, (0, 1), ("n",))
            affine(("n",), 1, 1)
            norm(("n",), 512)
            turned(("n",), 512, gain2, bias2(1, 1))
            for j in range(4):
                ahead(until, ("nq", j))
            for j in range(4):
                ahead(until, ("nk", j))
            for n in range(2):
                for half in range(2):
                    ahead(until, (("nv", n), half))
            diagonals(("n",), 1, 1, dgm, (0,))
            items = [(h, t) for h in range(16) for t in range(2)]
            for i in range(len(items) + 2):
                if i < len(items):
                    h, t = items[i]
                    o = 128 + 4 * (i % 4)
                    dve.wait_ge(*e.at("nsp", h, t))
                    ps = unit("nsp", h, t)
                    link(V.tensor_reduce(small[:, o:o + 1], ps[:, :], AX, ALU.max))
                    TS(small[:, o + 1:o + 2], small[:, o:o + 1], -1.0, None, ALU.mult).then_inc(*e.inc("nnm", h, t))
                if i >= 2:
                    h, t = items[i - 2]
                    o = 128 + 4 * ((i - 2) % 4)
                    dve.wait_ge(*e.at("nop", h, t))
                    TS(ny[:, t, h * 64:(h + 1) * 64], unit("nop", h, t)[:, 0:64], small[:, o + 3:o + 4], None,
                              ALU.mult).then_inc(*e.inc("ny_head", h, t, also=[("ny", t)], frees=("nop", h, t)))
                if 1 <= i <= len(items):
                    h, t = items[i - 1]
                    o = 128 + 4 * ((i - 1) % 4)
                    dve.wait_ge(*e.at("npr", h, t))
                    link(V.reciprocal(small[:, o + 3:o + 4], small[:, o + 2:o + 3]))
                    dve.wait_ge(*e.at("nptp", h, t))
                    if h:
                        dve.wait_ge(*e.at("nop", h - 1, t))
                    V.tensor_copy(npT[:, t, :], unit("nptp", h, t)[:, :]).then_inc(*e.inc("npT", h, t, frees=("nptp", h, t)))
            turned_y(("n",), 8, 256, *xT[256])
            for n in range(2):
                for half in range(2):
                    ahead(until, (("nw", n), half))
                for t in range(2):
                    dve.wait_ge(*e.at("nwp", n, t))
                    dve.wait_ge(*e.at("gb", ("n",), 0, n))
                    if n or t:
                        dve.wait_ge(*e.at("Xn", *divmod(2 * n + t - 1, 2)))
                    TT(nt[:, :], unit("nwp", n, t)[:, :], stripe(gbm, n, 0), ALU.mult).then_inc(*e.inc("nt", n, t, frees=("nwp", n, t)))
                    dve.wait_ge(*e.at("nt", n, t))
                    TT(stripe(X, n, t), stripe(X, n, t), nt[:, :], ALU.add).then_inc(*e.inc("Xn", n, t, also=[("X", ("g2", 1), t)]))
            dve.wait_ge(*e.at("Xn", 1, 1))
            block_two_ffn("g2", 1, 2, 256, (0,), ("last",))
            norm(("last",), 256)
            dve.wait_ge(L.sem("fg_landed"), 16)
            for t in range(2):
                dve.wait_ge(*e.at("xn", ("last",), t))
                TT(fo[:, t, :], xn[:, t, :], fg[:, :], ALU.mult).then_inc(*e.inc("out_row", t))

        @block.gpsimd
        def _(pool):
            e = Signals(L, "pool")
            minus_half = bsum[:, 8:9]

            def rstd(name, dst, src, n):
                pool.wait_ge(*e.at("ms", name))
                nc.gpsimd.tensor_tensor(dst, src, minus_half.to_broadcast([P, n]), ALU.pow).then_inc(*e.inc("rstd", name))

            def norm(name, T):
                rstd(name, small[:, 8:8 + T // P], small[:, 0:T // P], T // P)

            nc.gpsimd.memset(minus_half, -0.5).then_inc(L.sem("minus_half"), 1)
            pool.wait_ge(L.sem("minus_half"), 1)
            norm(("f1", 0), 256)
            for l in range(DEPTH):
                if l:
                    norm(("f1", l), 256)
                norm(("mx", l), 256)
                pool.wait_ge(*e.at("turn", ("mx", l), KD - 1))
                nc.gpsimd.memset(xr[:, :, 0:3], 0.0).then_inc(*e.inc("xr0", l))
                if l:
                    pool.wait_ge(*e.at("gvn", l - 1, 1))
                pool.dma_start(vgain[:, :], wide_row(w["gm_v_norm"][l], 512)).then_inc(L.sem("vgain_landed"), 16)
                pool.dma_start(ws[:, :, :], w["gm_w_s"][l].rearrange("g t s -> t g s"))\
                    .then_inc(L.sem("ws_landed"), 16)
                L.events[("ws", l)] = ("ws_landed", 16 * (l + 1))
                rstd(("gv", l), small[:, 50:52], small[:, 48:50], 2)
                rstd(("cq", l), small[:, 210:212], small[:, 208:210], 2)
                rstd(("ck", l), small[:, 214:216], small[:, 212:214], 2)
                for c in range(2):
                    rstd(("yc", l, c), small[:, 218:220], small[:, 216:218], 2)
                for t in range(2):
                    rstd(("qk", l, t), small[:, 240:256], small[:, 224:240], 16)
                norm(("f2", l), 256)
            norm(("g1", 0), 512)
            norm(("r",), 512)
            pool.dma_start(rcst[:, :], consts["rcst"]).then_inc(L.sem("rcst_landed"), 16)
            for h in range(4):
                for t in range(4):
                    o = 144 + 16 * (t % 2)
                    rstd(("ro", h, t), small[:, o + 8:o + 9], small[:, o + 7:o + 8], 1)
            norm(("g2", 0), 512)
            norm(("g1", 1), 512)
            norm(("n",), 512)
            rpb = w["nat_rpb_2"]
            for q4 in range(4):
                if q4 >= 2:
                    pool.wait_ge(*e.at("nbias_used", q4 - 2))
                else:
                    pool.wait_ge(*e.at("xT", ("n",), KD - 1))
                b = nbias[q4 % 2]
                for t in range(2):
                    for r in range(2):
                        for h in range(4):
                            off = rpb.offset + (4 * q4 + h) * 465 + (7 - 2 * t - r) * 31 + 15 - 63
                            pool.dma_start(b[64 * r:64 * r + 64, t, h, :].rearrange("p (a c) -> p a c", a=4),
                                           bass.AP(rpb.tensor, off, [[1, 64], [31, 4], [1, 64]]))\
                                .then_inc(L.sem(f"bias{q4 % 2}_landed"), 16)
                pool.wait_ge(L.sem(f"bias{q4 % 2}_landed"), 256 * (q4 // 2 + 1))
                mask = cst[:, C_NAT:C_NAT + 64].unsqueeze(1).to_broadcast([P, 32, 64])
                bv = b[:, :, :, :].rearrange("p t h (a c) -> p (t h a) c", c=64)
                nc.gpsimd.tensor_tensor(bv, bv, mask, ALU.add).then_inc(*e.inc("nbias", q4))
            norm(("g2", 1), 256)
            pool.dma_start(fg[:, :], wide_row(w["final_norm_g_2"], D)).then_inc(L.sem("fg_landed"), 16)
            norm(("last",), 256)
    return L


_INS = ["x", "positions", "ffn1_norm", "ffn1_w_in", "ffn1_w_out", "mix_norm", "w_in", "gm_v_norm", "gm_w_s", "gm_b_s",
        "mla_q_norm", "mla_kv_norm", "mla_w_uq", "mla_w_ukv", "mla_q_gain", "mla_k_gain", "ssd_conv_w",
        "ssd_conv_b", "ssd_dt_bias", "ssd_a_log", "ssd_d", "ssd_norm", "w_branch", "w_out", "ffn2_norm", "ffn2_w_in",
        "ffn2_w_out", "c_2", "ctx_2", "c_ctx_2", "w_mod_2", "b_mod_2", "norm_g_2", "ffn_w_in_2", "ffn_w_out_2",
        "ret_w_in_2", "ret_w_out_2", "ret_gn_g_2", "ret_decay_f_2", "ret_decay_b_2", "nat_w_qkv_2", "nat_w_o_2",
        "nat_rpb_2", "final_norm_g_2"]


def constants():
    import numpy as np
    i = np.arange(P)
    cst = np.zeros((P, C_END), np.float32)
    cst[:, C_IDENT:C_IDENT + P] = np.eye(P)
    cst[:, C_U:C_U + P] = i[:, None] <= i[None, :]
    cst[:, C_CAUSAL:C_CAUSAL + P] = np.where(i[None, :] <= i[:, None], 0.0, NEG)
    cst[:, C_ONES:C_ONES + P] = 1.0
    c = 63 - i % 64
    cst[:, C_FLIP:C_FLIP + P] = (i[None, :] == 64 * (i[:, None] // 64) + c[:, None])
    first = np.clip(c - 8, 0, 48)
    k = np.arange(64)
    inside = (k[None, :] >= first[:, None]) & (k[None, :] < first[:, None] + 16)
    cst[:, C_NAT:C_NAT + 64] = np.where(inside, 0.0, NEG)
    theta = np.float32(10000.0)
    cst[:, C_FREQ:C_FREQ + 16] = 1.0 / theta ** (np.arange(0, 32, 2, dtype=np.float32) / np.float32(32))
    rcst = np.zeros((P, R_END), np.float32)
    inv = theta ** (-np.arange(0, 256, 2, dtype=np.float32) / np.float32(256))
    ang = (np.arange(256, dtype=np.float32)[None, :] * inv[:, None]).astype(np.float32)
    rcst[:, R_COS:R_COS + 256] = np.cos(ang)
    rcst[:, R_SIN:R_SIN + 256] = np.sin(ang)
    for jt in range(2):
        o = R_DIST + 256 * jt
        rcst[:, o:o + 256] = np.arange(256)[None, :] - (i[:, None] + P * jt)
    return {"cst": cst, "rcst": rcst}


def kernel(**inputs):
    import numpy as _np
    import concourse.bacc as _bacc
    from concourse import mybir as _mybir
    from concourse.bass_utils import run_bass_kernel_spmd as _run

    tables = constants()
    arrays = {f"in_{name}_dram": _np.ascontiguousarray(inputs[name]) for name in _INS}
    arrays.update({f"const_{name}_dram": a for name, a in tables.items()})

    def written(known):
        nc = _bacc.Bacc("TRN2", target_bir_lowering=False, num_devices=1)

        def dram(name):
            a = arrays[name]
            return nc.dram_tensor(name, a.shape, _mybir.dt.from_np(a.dtype), kind="ExternalInput").ap()

        w = {name: dram(f"in_{name}_dram") for name in _INS}
        consts = {name: dram(f"const_{name}_dram") for name in tables}
        out = nc.dram_tensor("out_dram", (1, SEQ, D), F32, kind="ExternalOutput").ap()
        return nc, build(nc, w, consts, out, known)

    _, ledger = written(None)
    nc, _ = written(ledger)
    r = _run(nc, [arrays], core_ids=[0])
    return r.results[0]["out_dram"]
```

```python
from contextlib import ExitStack

import concourse.bass as bass
from concourse import mybir

F32 = mybir.dt.float32
F32R = mybir.dt.float32r
I32 = mybir.dt.int32
ALU = mybir.AluOpType
ACT = mybir.ActivationFunctionType
AX = mybir.AxisListType.X

P = 128
D = 1024
KD = D // P
SEQ = 256
DEPTH = 2
DFF = 2816
KF = DFF // P
GROUPS = DFF // 256
EPS = 1e-6
HEADS = 8
QK = 96
ROPE0 = 64
NEG = -1e30
UV, CQ, CKV, ZC, XBC, DT, GATES = 0, 1024, 1408, 1696, 2208, 3232, 3240
BANKS = 8
NRAW = 3
NSPLIT = 4
SLAB = 2048
PART = SLAB // 2
MODS_PER_FFN = 9
C_IDENT, C_U, C_CAUSAL, C_ONES, C_NAT, C_FREQ, C_FLIP, C_END = (
    0, 128, 256, 384, 512, 576, 592, 720)
R_COS, R_SIN, R_DIST, R_END = 0, 256, 512, 1024
TWO_PI = 6.283185307179586
TP1, TP2 = 6.28125, 0.0019350051879882812
TP3 = TWO_PI - TP1 - TP2


KINDS = {
    "pe": {"projected": "xbc dtp zp uvp cqp ckvp gp bp qp kvp wop rqp rkp rvp rgp rwp nqp nkp nvp nwp",
           "turned": "turn ty xst bt wst qkt cols", "scores": "sc nsp rap", "probs_turned": "ptp nptp",
           "attended": "op nop rop", "scan_sums": "csb csp cbp spp", "scan_out": "yd stp yo"},
    "act": {"projection_kept": "xr z uv cq ckv xs btok q kv rqc rkc rv rg Y0 nq nk nv gate_rows",
            "columns_hi": "xv xh yh qkT pT", "parameters": "sincos lge alog scc_half scc sc4hi",
            "probs": "pr npr", "scan": "cv dte expE expc st wexp", "squares": "ssa xn"},
    "dve": {"parameters": "cols_copied angles lgx lg ctx_ready modc modrow modt sc4", "columns_lo": "xT yT npT",
            "scan_in": "dtr dtn conv daU csc dec wlog rope", "scan_weights": "diff_half cbm MT xdd ra",
            "scan_rows": "yd_in yo_in yc gvn cqn ckn ya qkr rn ry",
            "merged": "merged mtmp", "attention_max": "nmax nnm", "attended": "yb_head ny_head",
            "residual": "X sgg nt Y", "mean_square": "ms", "gate_diagonals": "diag aff wT"},
    "pool": {"rstd": "rstd", "padding": "xr0 nbias"},
}
KIND = {(engine, stage): kind for engine, kinds in KINDS.items()
        for kind, stages in kinds.items() for stage in stages.split()}


class Ledger:

    def __init__(self, nc, ctx, known):
        self.nc, self.ctx, self.known = nc, ctx, known
        self.events, self.count, self.sems = {}, {}, {}
        self.bank_of, self.freed, self.units, self.order, self.params = {}, {}, 0, [], 16

    def sem(self, name):
        if name not in self.sems:
            self.sems[name] = self.ctx.enter_context(self.nc.semaphore(name))
        return self.sems[name]

    def value(self, event):
        name, n = self.known.events[event] if self.known else ("first_writing", 1)
        return self.sem(name), n

    def reader_of(self, unit):
        name, n = self.known.freed[unit] if self.known else ("first_writing", 1)
        return self.sem(name), n

    gains = 16

    def all_params(self):
        return self.known.params if self.known else 16


class Signals:

    def __init__(self, ledger, name):
        self.l, self.name = ledger, name

    def inc(self, stage, *key, also=(), frees=None):
        name = f"{self.name}_{KIND.get((self.name, stage), stage)}"
        n = self.l.count[name] = self.l.count.get(name, 0) + 1
        for event in ((stage, *key), *also):
            self.l.events[event] = (name, n)
        if frees is not None:
            self.l.freed[frees] = (name, n)
        return self.l.sem(name), 1

    def at(self, *event):
        return self.l.value(event)


class Slabs:

    def __init__(self):
        self.items, self.index, self.parts, self.part_index = [], {}, [], {}

    def add(self, key, src, kt, n, by_columns=False):
        self.index[key] = len(self.items)
        if by_columns:
            pieces = [(0, kt, c, P) for c in range(0, n, P)]
        else:
            per = max(1, PART // n)
            pieces = [(k, min(per, kt - k), 0, n) for k in range(0, kt, per)]
        for i, piece in enumerate(pieces):
            self.part_index[key, i] = len(self.parts)
            self.parts.append((key, i, *piece))
        self.items.append((key, src, kt, n, len(pieces)))


def plan(w):
    s = Slabs()

    def rows(m, k0, kt, c0, n):
        return m[k0 * P:(k0 + kt) * P, c0:c0 + n].rearrange("(k p) n -> p k n", p=P)

    def mod(i, half):
        l, g = divmod(i, 18)
        s.add(("mod", i, half), rows(w["w_mod_2"][l], 4 * half, 4, 512 * g, 512), 4, 512)

    def ffn(name, w_up, w_down, mod0=None):
        for g in range(GROUPS):
            for half, part in enumerate(("gate", "up")):
                s.add((name, part, g), rows(w_up, 0, KD, DFF * half + 256 * g, 256), KD, 256, by_columns=True)
                if mod0 is not None and 0 < g <= MODS_PER_FFN:
                    mod(mod0 + g - 1, half)
        for n in range(2):
            for d in range(6):
                kt = min(4, KF - 4 * d)
                s.add((name, "down", n, d), rows(w_down, 4 * d, kt, 512 * n, 512), kt, 512)

    def wide(name, m, c0, n):
        for half in range(2):
            s.add((name, half), rows(m, 4 * half, 4, c0, n), 4, n)

    for l in range(DEPTH):
        m = w["w_in"][l]
        ffn(("f1", l), w["ffn1_w_in"][l], w["ffn1_w_out"][l], 18 * l)
        for i in range(4):
            s.add(("xbc", l, i), rows(m, 0, KD, XBC + 256 * i, 256), KD, 256, by_columns=True)
        s.add(("dt", l), rows(m, 0, KD, DT, 8), KD, 8)
        wide(("z", l), m, ZC, 512)
        for n in range(2):
            wide(("uv", l, n), m, UV + 512 * n, 512)
        wide(("cq", l), m, CQ, 384)
        wide(("ckv", l), m, CKV, 288)

        def gate(br):
            for n in range(2):
                wide(("g", l, br, n), m, GATES + D * br + 512 * n, 512)

        def branch(br):
            for n in range(2):
                s.add(("b", l, br, n), rows(w["w_branch"][l, br], 0, 4, 512 * n, 512), 4, 512)

        gate(0)
        branch(0)
        gate(2)
        for n in range(2):
            s.add(("q", l, n), rows(w["mla_w_uq"][l], 0, 3, 384 * n, 384), 3, 384)
        s.add(("kv", l), rows(w["mla_w_ukv"][l], 0, 2, 0, 1024), 2, 1024)
        branch(2)
        gate(1)
        branch(1)
        for n in range(2):
            wide(("wo", l, n), w["w_out"][l], 512 * n, 512)
        ffn(("f2", l), w["ffn2_w_in"][l], w["ffn2_w_out"][l], 18 * l + MODS_PER_FFN)
    ffn(("g1", 0), w["ffn_w_in_2"][0, 0], w["ffn_w_out_2"][0, 0])
    for h in range(4):
        m = w["ret_w_in_2"][0]
        for i, part in enumerate("qk"):
            s.add(("r" + part, h), rows(m, 0, KD, 1024 * i + 256 * h, 256), KD, 256, by_columns=True)
        for i, part in enumerate("vg"):
            wide(("r" + part, h), m, 2048 * (i + 1) + 512 * h, 512)
        for n in range(2):
            s.add(("rw", h, n), rows(w["ret_w_out_2"][0], 4 * h, 4, 512 * n, 512), 4, 512)
    ffn(("g2", 0), w["ffn_w_in_2"][0, 1], w["ffn_w_out_2"][0, 1])
    ffn(("g1", 1), w["ffn_w_in_2"][1, 0], w["ffn_w_out_2"][1, 0])
    m = w["nat_w_qkv_2"][0]
    for i, part in enumerate("qk"):
        for j in range(4):
            s.add(("n" + part, j), rows(m, 0, KD, 1024 * i + 256 * j, 256), KD, 256, by_columns=True)
    for n in range(2):
        wide(("nv", n), m, 2048 + 512 * n, 512)
    for n in range(2):
        wide(("nw", n), w["nat_w_o_2"][0], 512 * n, 512)
    ffn(("g2", 1), w["ffn_w_in_2"][1, 1], w["ffn_w_out_2"][1, 1])
    return s


def build(nc, w, consts, out, known):
    slabs = plan(w)
    with ExitStack() as ctx:
        L = Ledger(nc, ctx, known)
        base = [nc.sbuf_base + 64 & ~63]

        def place(name, shape, dt=F32, off=None):
            size = 4
            for x in shape[1:]:
                size *= x
            size = (size + 63) // 64 * 64
            if off is None:
                off = base[0]
                base[0] += size
            return nc.alloc_sbuf_tensor_at(name, list(shape), dt, offset=off)

        raw = [place(f"raw{i}", [P, SLAB]) for i in range(NRAW)]
        whi = [place(f"whi{i}", [P, PART], F32R) for i in range(NSPLIT)]
        wlo = [place(f"wlo{i}", [P, PART], F32R) for i in range(NSPLIT)]
        cst = place("cst", [P, C_END])
        X = place("X", [P, 4, D])
        cols = place("cols", [P, 4, P])
        modc = place("modc", [P, DEPTH, 72, 2])
        scc = place("scc", [P, KD, 2])
        sc4 = place("sc4", [P, KD, 4], F32R)
        modt = place("modt", [P, 4, 4])
        small = place("small", [P, 256])
        cs16 = place("cs16", [P, 2, 2, 16])
        aff = place("aff", [P, KD, 2])
        dtb = place("dtb", [P, 3, DEPTH, 8])
        qkg = place("qkg", [P, DEPTH, 2, QK])
        vgain = place("vgain", [P, 512])
        lgs = place("lgs", [P, 8, 8])
        bsum = place("bsum", [P, 16])
        R0 = base[0]
        KB = 1024
        xT = {512: (place("xTh", [P, KD, 512], F32R), place("xTl", [P, KD, 512], F32R)),
              256: (place("xTh256", [P, KD, 256], F32R, off=R0), place("xTl256", [P, KD, 256], F32R, off=R0 + 8 * KB))}
        A0 = base[0]
        B0 = A0 - 16 * KB

        def arena(name, shape, off, dt=F32):
            t = nc.alloc_sbuf_tensor_at(name, list(shape), dt, offset=A0 + off)
            return t

        xn = arena("xn", [P, 4, D], 0)
        junk_v = arena("junk_v", [P, 512], -4 * KB)
        junk_a = arena("junk_a", [P, 512], -2 * KB)
        rowt = arena("rowt", [P, 4, P], 24 * KB)
        hh = arena("hh", [P, KF * 512], 0, F32R)
        hl = arena("hl", [P, KF * 512], 44 * KB, F32R)
        sg = arena("sg", [P, 2, 512], 88 * KB)
        modrow = arena("modrow", [4, 512], 40 * KB)
        gb = nc.alloc_sbuf_tensor_at("gb", [P, 2, D], F32, offset=A0 - 16 * KB)
        dg = nc.alloc_sbuf_tensor_at("dg", [P, KD, P], F32, offset=A0 - 8 * KB)
        def barena(name, shape, off, dt=F32):
            return nc.alloc_sbuf_tensor_at(name, list(shape), dt, offset=B0 + off)

        xr = barena("xr", [P, 8, 259], 0)
        cv = barena("cv", [P, 8, 256], 9 * KB)
        xs = barena("xs", [P, 2, 512], 17 * KB)
        E_ = barena("E", [P, 8, P], 21 * KB)
        xdt = barena("xdt", [P, 512], 25 * KB)
        xdd = barena("xdd", [P, 512], 27 * KB)
        st = barena("st", [P, 512], 29 * KB)
        btok = barena("btok", [P, 2, P], 31 * KB)
        cbm = barena("cbm", [P, 2, P], 32 * KB)
        gu = barena("gu", [P, 2, 512], 33 * KB)
        gv = barena("gv", [P, 2, 512], 37 * KB)
        z = barena("z", [P, 2, 512], 41 * KB)
        cq = barena("cq", [P, 2, 384], 45 * KB)
        ckv = barena("ckv", [P, 2, 288], 48 * KB)
        wT = barena("wT", [P, 4, P], 51 * KB)
        ws = barena("ws", [P, 4, P], 53 * KB)
        merged = barena("merged", [P, 2, D], 55 * KB)
        gates = barena("gates", [P, 2, D], 63 * KB)
        ytT = [(barena(f"yth{i}", [P, 4, 256], 71 * KB + 8 * i * KB, F32R),
                barena(f"ytl{i}", [P, 4, 256], 75 * KB + 8 * i * KB, F32R)) for i in range(2)]
        tmp = barena("tmp", [P, 2, 512], 87 * KB)
        qkT = barena("qkT", [P, HEADS, 512], 0)
        kv = barena("kv", [P, 2, D], 17 * KB)
        sq = barena("sq", [P, 16, QK], 25 * KB)
        cqTh = barena("cqTh", [P, 3, 256], 33 * KB, F32R)
        cqTl = barena("cqTl", [P, 3, 256], 36 * KB, F32R)
        ckTh = barena("ckTh", [P, 2, 256], 51 * KB, F32R)
        ckTl = barena("ckTl", [P, 2, 256], 53 * KB, F32R)
        qk = barena("qk", [P, 2, 16, QK], 91 * KB)
        yb = barena("yb", [P, 2, 512], 91 * KB)
        pr = barena("pr", [P, 2, 384], 103 * KB)
        pT = barena("pT", [P, 384], 89 * KB)
        rq = arena("rq", [P, 2, 512], 0)
        rk = arena("rk", [P, 2, 512], 4 * KB)
        rv = arena("rv", [P, 4, 512], 8 * KB)
        rg = arena("rg", [P, 4, 512], 16 * KB)
        ra = arena("ra", [P, 3, 512], 24 * KB)
        WX = arena("WX", [P, 2, 2, 256], 30 * KB)
        wtmp = arena("wtmp", [P, 2, 2, 256], 34 * KB)
        rYh = arena("rYh", [P, 4, 512], 38 * KB, F32R)
        rYl = arena("rYl", [P, 4, 512], 46 * KB, F32R)
        Y = arena("Y", [P, 4, D], 54 * KB)
        rt = arena("rt", [P, 2, 512], 70 * KB)
        gbm = arena("gbm", [P, 2, D], 74 * KB)
        dgm = arena("dgm", [P, KD, P], 82 * KB)
        rcst = arena("rcst", [P, R_END], 86 * KB)
        nq = arena("nq", [P, 8, 256], 0)
        nk = arena("nk", [P, 8, 512], 8 * KB)
        nv = arena("nv", [P, 4, D], 24 * KB)
        nbias = [arena(f"nbias{i}", [P, 2, 4, 256], (40 + 8 * i) * KB) for i in range(2)]
        npr = arena("npr", [P, 2, 512], 56 * KB)
        npT = arena("npT", [P, 2, 512], 60 * KB)
        ny = arena("ny", [P, 2, D], 64 * KB)
        nt = arena("nt", [P, 512], 72 * KB)
        fg = arena("fg", [P, D], 70 * KB)
        fo = arena("fo", [P, 2, D], 74 * KB)

        ident = cst[:, C_IDENT:C_IDENT + P]
        upper = cst[:, C_U:C_U + P]
        ones = cst[:, C_ONES:C_ONES + P]
        bank = [ctx.enter_context(nc.psum_tensor(f"bank{i}", [P, 512], F32)) for i in range(BANKS)]
        landed = [ctx.enter_context(nc.semaphore(f"raw{i}_landed")) for i in range(NRAW)]
        block = ctx.enter_context(nc.Block())

        def unit(*key):
            return bank[L.known.bank_of[key]] if L.known else bank[0]

        def col(table, row, n=1):
            return cols[:, table, row:row + n]

        NORM1, NORMX, NORM2, NORMG, QN, KVN, SSN = 0, 16, 32, 48, 96, 102, 106
        CVB, CVW, GN, BS = 0, 16, 80, 96
        BM, CC = 0, 72

        def row_loads():
            f = lambda name, pat: w[name].rearrange(pat, p=P)
            yield rowt[NORM1:NORM1 + 16, 0, :], f("ffn1_norm", "l (k p) -> (l k) p")
            yield rowt[NORMX:NORMX + 16, 0, :], f("mix_norm", "l (k p) -> (l k) p")
            yield rowt[NORM2:NORM2 + 16, 0, :], f("ffn2_norm", "l (k p) -> (l k) p")
            yield rowt[NORMG:NORMG + 48, 0, :], f("norm_g_2", "l j (k p) -> (l j k) p")
            yield rowt[QN:QN + 6, 0, :], f("mla_q_norm", "l (k p) -> (l k) p")
            yield rowt[KVN:KVN + 4, 0, :], f("mla_kv_norm", "l (k p) -> (l k) p")
            yield rowt[SSN:SSN + 8, 0, :], f("ssd_norm", "l (k p) -> (l k) p")
            yield rowt[CVB:CVB + 16, 1, :], f("ssd_conv_b", "l (k p) -> (l k) p")
            yield rowt[CVW:CVW + 64, 1, :], f("ssd_conv_w", "l j (k p) -> (l j k) p")
            yield rowt[GN:GN + 16, 1, :], f("ret_gn_g_2", "l (k p) -> (l k) p")
            yield rowt[BS:BS + 8, 1, :], w["gm_b_s"].rearrange("l g t -> (l g) t")
            for l in range(DEPTH):
                yield rowt[BM:BM + 72, 2 + l, :], w["b_mod_2"][l].rearrange("(k p) -> k p", p=P)
            yield rowt[CC:CC + 8, 2, :], f("c_2", "l (k p) -> (l k) p")
            yield rowt[CC + 8:CC + 16, 2, :], w["c_ctx_2"].rearrange("(k p) -> k p", p=P)

        ROWS = (114, 104, 88, 72)
        GAIN_LOADS = 7

        def wide_row(a, n):
            return bass.AP(a.tensor, a.offset, [[0, P], [1, n]])

        def stripe(t, n, l):
            return t[:, l, n * 512:(n + 1) * 512]

        def view(tile, key):
            _, _, kt, n, _ = slabs.items[slabs.index[key]]
            return tile[:, 0:kt * n].rearrange("p (k n) -> p k n", n=n)

        def part_views(key, part):
            i = slabs.part_index[key, part]
            _, _, k0, kt, c0, n = slabs.parts[i]
            src = view(raw[slabs.index[key] % NRAW], key)[:, k0:k0 + kt, c0:c0 + n]
            hi, lo = (t[i % NSPLIT][:, 0:kt * n].rearrange("p (k n) -> p k n", n=n) for t in (whi, wlo))
            return src, hi, lo

        def arrival(key):
            s = slabs.index[key]
            return landed[s % NRAW], 16 * (s // NRAW + 1)

        @block.sync
        def _(sp):
            e = Signals(L, "sp")
            n_first = [0]

            def first(dst, src):
                sp.dma_start(dst, src).then_inc(L.sem("params_landed"), 16)
                n_first[0] += 16

            def slab_range(a, b):
                for s in range(a, b):
                    key, src, _, _, _ = slabs.items[s]
                    if s >= NRAW:
                        old, _, _, _, parts = slabs.items[s - NRAW]
                        sp.wait_ge(*e.at("hi", old, parts - 1))
                        sp.wait_ge(*e.at("lo", old, parts - 1))
                    sp.dma_start(view(raw[s % NRAW], key), src).then_inc(landed[s % NRAW], 16)

            sp.dma_start(X[:, 0:2, :], w["x"][0].rearrange("(t p) n -> p t n", p=P))\
              .then_inc(L.sem("x_landed"), 16)
            sp.dma_start(cst[:, :], consts["cst"]).then_inc(L.sem("gains_landed"), 16)
            loads = list(row_loads())
            for dst, src in loads[:GAIN_LOADS]:
                sp.dma_start(dst, src).then_inc(L.sem("gains_landed"), 16)
            L.gains = 16 * (GAIN_LOADS + 1)
            slab_range(0, NRAW)
            for dst, src in loads[GAIN_LOADS:]:
                first(dst, src)
            for l in range(DEPTH):
                for i, name in enumerate(("ssd_dt_bias", "ssd_a_log", "ssd_d")):
                    first(dtb[:, i, l, :], wide_row(w[name][l], 8))
                for i, name in enumerate(("mla_q_gain", "mla_k_gain")):
                    first(qkg[:, l, i, :], wide_row(w[name][l], QK))
            first(lgs[:, 0, 0:4], wide_row(w["ret_decay_f_2"][0], 4))
            first(lgs[:, 0, 4:8], wide_row(w["ret_decay_b_2"][0], 4))
            with nc.allow_non_contiguous_dma(reason="256 positions, one to a partition and tile"):
                first(bsum[:, 0:2].bitcast(I32), w["positions"][0].rearrange("(t p) -> p t", p=P))
            first(X[:, 2:4, :], w["ctx_2"][0].rearrange("(t p) n -> p t n", p=P))
            L.params = n_first[0]
            slab_range(NRAW, len(slabs.items))
            for t in range(2):
                sp.wait_ge(*e.at("out_row", t))
                sp.dma_start(out[0, t * P:(t + 1) * P, :], fo[:, t, :]).then_inc(L.sem("out_written"), 16)
            sp.wait_ge(L.sem("out_written"), 32)

        def tiles_of(T):
            return range(T // P)

        @block.tensor
        def _(pe):
            e = Signals(L, "pe")

            def new(*key):
                u = L.units
                L.units += 1
                L.bank_of[key] = u % BANKS
                L.order.append(key)
                if u >= BANKS:
                    pe.wait_ge(*L.reader_of(L.order[u - BANKS]))
                return bank[u % BANKS]

            def mm3(ps, lh, ll, rh, rl, start, stop):
                pe.matmul(ps, lh, rh, start=start, stop=False, skip_group_check=True)
                pe.matmul(ps, lh, rl, start=False, stop=False, skip_group_check=True)
                return pe.matmul(ps, ll, rh, start=False, stop=stop, skip_group_check=True)

            def mod(i, half, ps):
                if i == 0:
                    pe.wait_ge(*e.at("sc4"))
                for part in range(2):
                    wh, wl = split_ready(("mod", i, half), part)
                    for j in range(2):
                        k = 4 * half + 2 * part + j
                        pe.matmul(ps[0:4, :], sc4[:, k, :], wh[:, j, :], start=k == 0, stop=False,
                                  skip_group_check=True)
                        m = pe.matmul(ps[0:2, :], sc4[:, k, 0:2], wl[:, j, :], start=False, stop=k == KD - 1,
                                      skip_group_check=True)
                    if k < KD - 1:
                        m.then_inc(*e.inc("used", ("mod", i, half), part))
                    else:
                        m.then_inc(*e.inc("modp", i, also=[("used", ("mod", i, 1), 1)]))

            def mod_turn(i):
                pe.wait_ge(*e.at("modrow", i))
                ps = new("modtp", i)
                for c in range(4):
                    m = pe.transpose(ps[:, 4 * c:4 * c + 4], modrow[0:4, c * P:(c + 1) * P], ident[0:4, 0:4])
                m.then_inc(*e.inc("modtp", i))

            def split_ready(key, part):
                pe.wait_ge(*e.at("hi", key, part))
                pe.wait_ge(*e.at("lo", key, part))
                return part_views(key, part)[1:]

            def feature_major(key, T, units, xh, xl, norm=None):
                u = 0
                for mc in range(2):
                    wh, wl = split_ready(key, mc)
                    if T == 512 or mc == 0:
                        ps = new(*units[u])
                    o = 0 if T == 512 else mc * 256
                    for k in range(KD):
                        if norm and mc == 0:
                            pe.wait_ge(*e.at("xT", norm, k))
                        m = mm3(ps[:, o:o + T], wh[:, k, :], wl[:, k, :], xh[:, k, 0:T], xl[:, k, 0:T],
                                k == 0, k == KD - 1)
                    if T == 512 or mc == 1:
                        m.then_inc(*e.inc(*units[u], also=[("used", key, mc)]))
                        u += 1
                    else:
                        m.then_inc(*e.inc("used", key, mc))

            def rows_by(key, name, ps, xh, xl, k0, total):
                tiles = sorted(ps)
                for part in range(slabs.items[slabs.index[key]][4]):
                    wh, wl = split_ready(key, part)
                    kt, n = wh.shape[1], wh.shape[2]
                    last = k0 + kt == total
                    for t in tiles:
                        for k in range(kt):
                            m = mm3(ps[t][:, 0:n], xh[:, k0 + k, t * P:(t + 1) * P], xl[:, k0 + k, t * P:(t + 1) * P],
                                    wh[:, k, :], wl[:, k, :], k0 + k == 0, k0 + k == total - 1)
                        if last:
                            m.then_inc(*e.inc(*name, t, also=[("used", key, part)] if t == tiles[-1] else []))
                    if not last:
                        m.then_inc(*e.inc("used", key, part))
                    k0 += kt
                return k0

            def rows_by_tile(keys, name, ps, xh, xl, k0, total):
                tiles = sorted(ps)
                for t in tiles:
                    k = k0
                    for key in keys:
                        for part in range(slabs.items[slabs.index[key]][4]):
                            if t == tiles[0]:
                                wh, wl = split_ready(key, part)
                            else:
                                wh, wl = part_views(key, part)[1:]
                            for i in range(wh.shape[1]):
                                m = mm3(ps[t][:, 0:wh.shape[2]], xh[:, k, t * P:(t + 1) * P], xl[:, k, t * P:(t + 1) * P],
                                        wh[:, i, :], wl[:, i, :], k == 0, k == total - 1)
                                k += 1
                            used = [("used", key, part)] if t == tiles[-1] else []
                            if k == total:
                                m.then_inc(*e.inc(*name, t, also=used))
                            elif used:
                                m.then_inc(*e.inc("used", key, part))

            def token_major(keys, name, tiles, xh, xl, by_tile=0):
                ps = {t: new(*name, t) for t in tiles}
                total = sum(slabs.items[slabs.index[k]][2] for k in keys)
                k0 = 0
                for key in keys[:len(keys) - by_tile]:
                    k0 = rows_by(key, name, ps, xh, xl, k0, total)
                if by_tile:
                    rows_by_tile(keys[len(keys) - by_tile:], name, ps, xh, xl, k0, total)

            def turn_in(name, T, ready):
                for half in range(2):
                    ks = range(4 * half, 4 * half + 4)
                    ps = [new("turn", name, k) for k in ks]
                    for t in tiles_of(T):
                        pe.wait_ge(*e.at(*ready, t, half))
                        for k in ks:
                            m = pe.transpose(ps[k % 4][:, t * P:(t + 1) * P], xn[:, t, k * P:(k + 1) * P], ident)
                            if t == T // P - 1:
                                m.then_inc(*e.inc("turn", name, k))

            def turn_y(name, src, chunks, T, ready, c0=0):
                per = 512 // T
                for u in range((chunks + per - 1) // per):
                    ps = new("ty", name, u)
                    for j in range(per):
                        if u * per + j >= chunks:
                            break
                        c = u * per + j
                        for t in tiles_of(T):
                            pe.wait_ge(*e.at(*ready, t))
                            m = pe.transpose(ps[:, j * T + t * P:j * T + (t + 1) * P],
                                             src[:, t, c * P:(c + 1) * P], ident)
                    m.then_inc(*e.inc("ty", name, u))

            def broadcast_gate(name, dgt, whos):
                for who in whos:
                    pe.wait_ge(*e.at("diag", name, who))
                    for n in range(2):
                        ps = new("gbp", name, who, n)
                        m = pe.matmul(ps[:, :], ones, dgt[:, 4 * n:4 * n + 4, :], start=True, stop=True)
                        m.then_inc(*e.inc("gbp", name, who, n))

            def ffn(name, T, mod0, gate_whos):
                turn_in(name, T, ("xn", name))
                for g in range(GROUPS):
                    for half, part in enumerate(("gate", "up")):
                        feature_major((name, part, g), T, [(part, name, g, i) for i in range(T // 256)], *xT[T],
                                      norm=name if g + half == 0 else None)
                        if name == ("f1", 0) and g + half == 0:
                            turn_parameters()
                        if mod0 is not None:
                            if half == 0 and 1 < g <= MODS_PER_FFN + 1:
                                mod_turn(mod0 + g - 2)
                            if 0 < g <= MODS_PER_FFN:
                                if half == 0:
                                    ps = new("modp", mod0 + g - 1)
                                mod(mod0 + g - 1, half, ps)
                if gate_whos:
                    broadcast_gate(name, dg, gate_whos)
                pe.wait_ge(*e.at("hidden", name, GROUPS - 1, T // 256 - 1))
                hv = (hh[:, 0:KF * T].rearrange("p (k t) -> p k t", t=T),
                      hl[:, 0:KF * T].rearrange("p (k t) -> p k t", t=T))
                for n in range(2):
                    ps = {t: new("down", name, n, t) for t in tiles_of(T)}
                    k0 = 0
                    for d in range(6 if n == 0 else 4):
                        k0 = rows_by((name, "down", n, d), ("down", name, n), ps, *hv, k0, KF)
                rows_by_tile([(name, "down", 1, d) for d in (4, 5)], ("down", name, 1), ps, *hv, k0, KF)

            def turn_rows(i):
                ps = new("cols", i)
                m = pe.transpose(ps[:, 0:ROWS[i]], rowt[0:ROWS[i], i, :], ident[0:ROWS[i], 0:ROWS[i]])
                m.then_inc(*e.inc("cols", i))

            def turn_parameters():
                pe.wait_ge(L.sem("params_landed"), L.all_params())
                for i in range(1, 4):
                    turn_rows(i)

            pe.wait_ge(L.sem("gains_landed"), L.gains)
            turn_rows(0)

            def mixers(l):
                nm = ("mx", l)
                turn_in(nm, 256, ("xn", nm))
                for i in range(4):
                    feature_major(("xbc", l, i), 256, [("xbc", l, i)], *xT[256], norm=nm if i == 0 else None)
                token_major([("dt", l)], ("dtp", l), range(2), *xT[256])
                token_major([(("z", l), 0), (("z", l), 1)], ("zp", l), range(2), *xT[256])
                for n in range(2):
                    token_major([(("uv", l, n), 0), (("uv", l, n), 1)], ("uvp", l, n), range(2), *xT[256])
                token_major([(("cq", l), 0), (("cq", l), 1)], ("cqp", l), range(2), *xT[256])
                token_major([(("ckv", l), 0), (("ckv", l), 1)], ("ckvp", l), range(2), *xT[256])
                for t in range(2):
                    pe.wait_ge(*e.at("cv", l))
                    ps = new("xst", l, t)
                    for c in range(4):
                        m = pe.transpose(ps[:, c * P:(c + 1) * P], cv[:, c, t * P:(t + 1) * P], ident)
                    m.then_inc(*e.inc("xst", l, t))
                ps = new("bt", l)
                for g in range(2):
                    m = pe.transpose(ps[:, g * P:(g + 1) * P], cv[:, 4 + g, 0:P], ident)
                m.then_inc(*e.inc("bt", l))
                def gate(br):
                    for n in range(2):
                        token_major([(("g", l, br, n), 0), (("g", l, br, n), 1)], ("gp", l, br, n), range(2),
                                    *xT[256])

                def branch(br, yT):
                    for n in range(2):
                        token_major([("b", l, br, n)], ("bp", l, br, n), range(2), *yT)

                def scan_sums(c):
                    pe.wait_ge(*e.at("daU", l, c))
                    for h2 in range(2):
                        ps = new("csb", l, c, h2)
                        m = pe.matmul(ps[:, :], ones, E_[:, 4 * h2:4 * h2 + 4, :], start=True, stop=True)
                        m.then_inc(*e.inc("csb", l, c, h2))
                    ps = new("csp", l, c)
                    m = pe.matmul(ps[:, 0:8], upper, small[:, 32 + 8 * c:40 + 8 * c], start=True, stop=True)
                    m = pe.matmul(ps[:, 8:16], ones, small[:, 32 + 8 * c:40 + 8 * c], start=True, stop=True)
                    m.then_inc(*e.inc("csp", l, c))
                    ps = new("cbp", l, c)
                    for g in range(2):
                        m = pe.matmul(ps[:, g * P:(g + 1) * P], cv[:, 4 + g, c * P:(c + 1) * P],
                                      cv[:, 6 + g, c * P:(c + 1) * P], start=True, stop=True)
                    m.then_inc(*e.inc("cbp", l, c))

                def scan_inside(c):
                    pe.wait_ge(*e.at("MT", l, c))
                    ps = new("yd", l, c)
                    for h in range(8):
                        m = pe.matmul(ps[:, h * 64:(h + 1) * 64], E_[:, h, :], xdt[:, h * 64:(h + 1) * 64],
                                      start=True, stop=True)
                    m.then_inc(*e.inc("yd", l, c))

                scan_sums(0)
                pe.wait_ge(*e.at("ws", l))
                ps = new("wst", l)
                for g in range(4):
                    m = pe.transpose(ps[:, g * P:(g + 1) * P], ws[:, g, :], ident)
                m.then_inc(*e.inc("wst", l))
                gate(0)
                for t in range(2):
                    pe.wait_ge(*e.at("gvn", l, t))
                    if t == 0:
                        pe.wait_ge(*e.at("wT", l))
                    ps = new("spp", l, t)
                    for g in range(4):
                        m = pe.matmul(ps[:, g * P:(g + 1) * P], wT[:, g, :], gv[:, t, g * P:(g + 1) * P],
                                      start=True, stop=True)
                    m.then_inc(*e.inc("spp", l, t))
                scan_inside(0)
                pe.wait_ge(*e.at("btok", l))
                pe.wait_ge(*e.at("xdd", l))
                ps = new("stp", l)
                for g in range(2):
                    m = pe.matmul(ps[:, g * 256:(g + 1) * 256], btok[:, g, :],
                                  xdd[:, g * 256:(g + 1) * 256], start=True, stop=True)
                m.then_inc(*e.inc("stp", l))
                turn_y(("a", l), gu, 4, 256, ("ya", l))
                pe.wait_ge(*e.at("yT", ("a", l), 1))
                branch(0, ytT[1])
                turn_y(("cq", l), cq, 3, 256, ("cqn", l))
                turn_y(("ck", l), ckv, 2, 256, ("ckn", l))
                scan_sums(1)
                gate(2)
                scan_inside(1)
                pe.wait_ge(*e.at("st", l))
                ps = new("yo", l)
                for g in range(2):
                    m = pe.matmul(ps[:, g * 256:(g + 1) * 256], cv[:, 6 + g, P:2 * P],
                                  st[:, g * 256:(g + 1) * 256], start=True, stop=True)
                m.then_inc(*e.inc("yo", l))
                pe.wait_ge(*e.at("yT", ("cq", l), 2))
                for n in range(2):
                    token_major([("q", l, n)], ("qp", l, n), range(2), cqTh, cqTl)
                pe.wait_ge(*e.at("yT", ("ck", l), 1))
                ps = {(n, t): new("kvp", l, n, t) for n in range(2) for t in range(2)}
                for k in range(2):
                    wh, wl = split_ready(("kv", l), k)
                    for n, t in ps:
                        m = mm3(ps[n, t][:, :], ckTh[:, k, t * P:(t + 1) * P], ckTl[:, k, t * P:(t + 1) * P],
                                wh[:, 0, n * 512:(n + 1) * 512], wl[:, 0, n * 512:(n + 1) * 512], k == 0, k == 1)
                        if k == 1:
                            also = [("used", ("kv", l), 1)] if n + t == 2 else []
                            m.then_inc(*e.inc("kvp", l, n, t, also=also))
                    if k == 0:
                        m.then_inc(*e.inc("used", ("kv", l), 0))
                turn_y(("c", l), z, 4, 256, ("yc", l))
                pe.wait_ge(*e.at("yT", ("c", l), 3))
                branch(2, ytT[0])
                gate(1)
                for t in range(2):
                    pe.wait_ge(*e.at("qkr", l, t))
                for h in range(HEADS):
                    ps = new("qkt", l, h)
                    for i in range(2):
                        for t in range(2):
                            m = pe.transpose(ps[0:QK, 256 * i + t * P:256 * i + (t + 1) * P],
                                             qk[:, t, 8 * i + h, :], ident)
                    m.then_inc(*e.inc("qkt", l, h))
                for i in range(HEADS + 2):
                    if i < HEADS:
                        h = i
                        pe.wait_ge(*e.at("qkT", l, h))
                        ps = new("sc", l, h)
                        m = pe.matmul(ps[:, 0:P], qkT[0:QK, h, 0:P], qkT[0:QK, h, 256:384], start=True, stop=True)
                        m = pe.matmul(ps[:, 256:512], qkT[0:QK, h, P:256], qkT[0:QK, h, 256:512],
                                      start=True, stop=True)
                        m.then_inc(*e.inc("sc", l, h))
                    if 1 <= i <= HEADS:
                        h = i - 1
                        pe.wait_ge(*e.at("pr", l, h))
                        ps = new("ptp", l, h)
                        for j in range(3):
                            m = pe.transpose(ps[:, j * P:(j + 1) * P], pr[:, h % 2, j * P:(j + 1) * P], ident)
                        m.then_inc(*e.inc("ptp", l, h))
                    if i >= 2:
                        h = i - 2
                        pe.wait_ge(*e.at("pT", l, h))
                        ps = new("op", l, h)
                        v0, v1 = (kv[:, t, h * P + 64:(h + 1) * P] for t in range(2))
                        m = pe.matmul(ps[:, 0:64], pT[:, 0:P], v0, start=True, stop=True)
                        m = pe.matmul(ps[:, 64:128], pT[:, P:2 * P], v0, start=True, stop=False)
                        m = pe.matmul(ps[:, 64:128], pT[:, 2 * P:3 * P], v1, start=False, stop=True)
                        m.then_inc(*e.inc("op", l, h))
                turn_y(("b", l), yb, 4, 256, ("yb", l))
                pe.wait_ge(*e.at("yT", ("b", l), 1))
                branch(1, ytT[1])
                turn_y(("m", l), merged, 8, 256, ("mg", l))
                pe.wait_ge(*e.at("yT", ("m", l), 3))
                for n in range(2):
                    token_major([(("wo", l, n), 0), (("wo", l, n), 1)], ("wop", l, n), range(2), *xT[256], by_tile=n)

            for l in range(DEPTH):
                ffn(("f1", l), 256, 18 * l, ())
                mixers(l)
                ffn(("f2", l), 256, 18 * l + MODS_PER_FFN, ())

            ffn(("g1", 0), 512, None, (0, 1))
            turn_in(("r",), 512, ("xn", ("r",)))
            for h in range(4):
                for part in "qk":
                    feature_major(("r" + part, h), 512, [("r" + part + "p", h, i) for i in range(2)], *xT[512],
                                  norm=("r",) if h == 0 and part == "q" else None)
                if h == 0:
                    broadcast_gate(("r",), dgm, (0, 1))
                for part in "vg":
                    token_major([(("r" + part, h), 0), (("r" + part, h), 1)], ("r" + part + "p", h),
                                range(4), *xT[512])
                pe.wait_ge(*e.at("rqk", h))
                ps = new("rap", h, 0)
                for jt in range(2):
                    for k in range(2):
                        m = pe.matmul(ps[:, 256 * jt:256 * jt + 256], rk[:, k, jt * P:(jt + 1) * P],
                                      rq[:, k, 0:256], start=k == 0, stop=k == 1, skip_group_check=True)
                m.then_inc(*e.inc("rap", h, 0))
                for jt in range(2):
                    ps = new("rap", h, 1 + jt)
                    for k in range(2):
                        m = pe.matmul(ps[:, :], rk[:, k, 256 + jt * P:256 + (jt + 1) * P], rq[:, k, :],
                                      start=k == 0, stop=k == 1)
                    m.then_inc(*e.inc("rap", h, 1 + jt))
                pe.wait_ge(*e.at("ra", h, 2))
                pe.wait_ge(*e.at("rv", h, 3))
                for t in range(4):
                    ps = new("rop", h, t)
                    if t < 2:
                        pairs = [(ra[:, 0, 256 * jt + t * P:256 * jt + (t + 1) * P], jt) for jt in range(2)]
                        pairs += [(ra[:, 1 + jt, t * P:(t + 1) * P], 2 + jt) for jt in range(2)]
                    else:
                        pairs = [(ra[:, 1 + jt, t * P:(t + 1) * P], 2 + jt) for jt in range(2)]
                    for i, (a, j) in enumerate(pairs):
                        m = pe.matmul(ps[:, :], a, rv[:, j, :], start=i == 0, stop=i == len(pairs) - 1)
                    m.then_inc(*e.inc("rop", h, t))
                turn_y(("r", h), rg, 4, 512, ("ry", h))
                pe.wait_ge(*e.at("yT", ("r", h), 3))
                for n in range(2):
                    token_major([("rw", h, n)], ("rwp", h, n), range(4), rYh, rYl, by_tile=int(h == 3 and n == 1))
            ffn(("g2", 0), 512, None, (0, 1))
            ffn(("g1", 1), 512, None, (0, 1))
            turn_in(("n",), 512, ("xn", ("n",)))
            for j in range(4):
                feature_major(("nq", j), 256, [("nqp", j)], *xT[512], norm=("n",) if j == 0 else None)
            for j in range(4):
                feature_major(("nk", j), 512, [("nkp", j, i) for i in range(2)], *xT[512])
            for n in range(2):
                token_major([(("nv", n), 0), (("nv", n), 1)], ("nvp", n), range(4), *xT[512])
            pe.wait_ge(*e.at("nq", 3))
            pe.wait_ge(*e.at("nk", 3, 1))
            pe.wait_ge(*e.at("nv", 1, 3))
            items = [(h, t) for h in range(16) for t in range(2)]
            for i in range(len(items) + 2):
                if i < len(items):
                    h, t = items[i]
                    p0 = 64 * (h % 2)
                    ps = new("nsp", h, t)
                    pe.matmul(ps[:, :], nq[p0:p0 + 64, h // 2, t * P:(t + 1) * P],
                              nk[p0:p0 + 64, h // 2, :], start=True, stop=False, skip_group_check=True)
                    pe.wait_ge(*e.at("nbias", h // 4))
                    m = pe.matmul(ps[:, 0:256], cst[:, C_FLIP:C_FLIP + P], nbias[h // 4 % 2][:, t, h % 4, :],
                                  start=False, stop=True, skip_group_check=True)
                    m.then_inc(*e.inc("nsp", h, t, also=[("nbias_used", h // 4)]))
                if 1 <= i <= len(items):
                    h, t = items[i - 1]
                    pe.wait_ge(*e.at("npr", h, t))
                    ps = new("nptp", h, t)
                    for j in range(4):
                        m = pe.transpose(ps[:, j * P:(j + 1) * P], npr[:, t, j * P:(j + 1) * P], ident)
                    m.then_inc(*e.inc("nptp", h, t))
                if i >= 2:
                    h, t = items[i - 2]
                    pe.wait_ge(*e.at("npT", h, t))
                    ps = new("nop", h, t)
                    for j in range(4):
                        m = pe.matmul(ps[:, 0:64], npT[:, t, j * P:(j + 1) * P], nv[:, j, h * 64:(h + 1) * 64],
                                      start=j == 0, stop=j == 3)
                    m.then_inc(*e.inc("nop", h, t))
            broadcast_gate(("n",), dgm, (0,))
            turn_y(("n",), ny, 8, 256, ("ny",))
            pe.wait_ge(*e.at("yT", ("n",), 3))
            for n in range(2):
                token_major([(("nw", n), 0), (("nw", n), 1)], ("nwp", n), range(2), *xT[256], by_tile=n)
            ffn(("g2", 1), 256, None, (0,))

        NEXT_T = {("mx", 0): 256, ("f1", 1): 256, ("mx", 1): 256, ("g1", 0): 256, ("r",): 512, ("g1", 1): 512,
                  ("n",): 512, ("last",): 256}
        idx = slabs.index

        def ahead(until, key):
            parts = slabs.items[idx[key]][4]
            until(slabs.part_index[key, parts - 1] + NSPLIT - 1)

        def ahead_of_tail(until, key):
            until(slabs.part_index[key, 0] + NSPLIT - 1)

        def down_ahead(until, name, n, d):
            if n and d >= 4:
                ahead_of_tail(until, (name, "down", 1, 4))
            else:
                ahead(until, (name, "down", n, d))

        @block.scalar
        def _(act):
            e = Signals(L, "act")
            split = [0]

            def until(s):
                while split[0] <= min(s, len(slabs.parts) - 1):
                    i = split[0]
                    key, part = slabs.parts[i][0:2]
                    split[0] += 1
                    src, hi, _ = part_views(key, part)
                    act.wait_ge(*arrival(key))
                    if i >= NSPLIT:
                        act.wait_ge(*e.at("used", *slabs.parts[i - NSPLIT][0:2]))
                    nc.scalar.activation(hi, src, ACT.Copy).then_inc(*e.inc("hi", key, part))

            A = nc.scalar.activation

            squared = []

            def squares(name, t, n):
                act.wait_ge(*e.at("X", name, t, n))
                if squared:
                    act.wait_ge(*e.at(*squared[-1]))
                squared.append(("ssa", name, t, n))
                A(junk_a[:, :], stripe(X, n, t), ACT.Square, scale=D ** -0.5,
                  accum_out=small[:, 4 * n + t:4 * n + t + 1]).then_inc(*e.inc("ssa", name, t, n))

            def first_squares(name, T):
                for t in range(1, T // P, 2):
                    squares(name, t, 0)

            def norm(name, T):
                for t in range(T // P + 1):
                    if t % 2 and t < T // P:
                        squares(name, t, 1)
                    if t:
                        act.wait_ge(*e.at("rstd", name, t - 1))
                        A(stripe(xn, 1, t - 1), stripe(X, 1, t - 1), ACT.Copy, scale=small[:, 7 + t:8 + t])\
                            .then_inc(*e.inc("xn", name, t - 1, 1))

            def turned(name, T, gain, bias):
                xTh = xT[T][0]
                act.wait_ge(*e.at("aff", name))
                if not bias:
                    for k in range(KD):
                        act.wait_ge(*e.at("turn", name, k))
                        A(xTh[:, k, :], unit("turn", name, k)[:, 0:256], ACT.Copy, scale=gain(k, 0))\
                            .then_inc(*e.inc("xh", name, k))
                    return
                for k in range(KD + 1):
                    if k < KD:
                        act.wait_ge(*e.at("turn", name, k))
                        for who in range(T // 256):
                            m = A(xn[:, 2 * who:2 * who + 2, k * P:(k + 1) * P],
                                  unit("turn", name, k)[:, 256 * who:256 * who + 256].rearrange("p (t c) -> p t c", c=P),
                                  ACT.Identity, scale=gain(k, who), bias=bias(k, who))
                        m.then_inc(*e.inc("xv", name, k, frees=("turn", name, k)))
                    if k:
                        act.wait_ge(*e.at("xv", name, k - 1))
                        A(xTh[:, k - 1, :].rearrange("p (t c) -> p t c", c=P), xn[:, 0:T // P, (k - 1) * P:k * P],
                          ACT.Copy).then_inc(*e.inc("xh", name, k - 1))

            def turned_y(name, chunks, T, dst, gain=None):
                per = 512 // T
                for u in range((chunks + per - 1) // per):
                    act.wait_ge(*e.at("ty", name, u))
                    if gain is None:
                        m = A(dst[:, u * per:(u + 1) * per, 0:T], unit("ty", name, u)[:, :]
                              .rearrange("p (j t) -> p j t", t=T), ACT.Copy)
                        m.then_inc(*e.inc("yh", name, u))
                    else:
                        for j in range(min(per, chunks - u * per)):
                            c = u * per + j
                            m = A(dst[:, c, 0:T], unit("ty", name, u)[:, j * T:(j + 1) * T], ACT.Copy, scale=gain(c))
                            m.then_inc(*e.inc("yh", name, c))

            def ffn(name, T, gate_whos, nxt, mod0=None):
                for g in range(GROUPS):
                    for i in range(T // 256):
                        ahead(until, (name, "gate", g))
                        act.wait_ge(*e.at("gate", name, g, i))
                        b = (g * (T // 256) + i) % 2
                        if (g * (T // 256) + i) >= 2:
                            g2, i2 = divmod(g * (T // 256) + i - 2, T // 256)
                            act.wait_ge(*e.at("hidden", name, g2, i2))
                        A(sg[:, b, :], unit("gate", name, g, i)[:, :], ACT.Silu).then_inc(*e.inc("sg", name, g, i, frees=("gate", name, g, i)))
                    if name == ("f1", 0):
                        parameters(g)
                    ahead(until, (name, "up", g))
                    for i in range(T // 256):
                        b = (g * (T // 256) + i) % 2
                        o = (g * (T // 256) + i) * 512
                        act.wait_ge(*e.at("ht", name, g, i))
                        A(hh[:, o:o + 512], sg[:, b, :], ACT.Copy).then_inc(*e.inc("hhi", name, g, i))
                    if mod0 is not None and 0 < g <= MODS_PER_FFN:
                        ahead(until, ("mod", mod0 + g - 1, 1))
                for who in gate_whos:
                    for n in range(2):
                        act.wait_ge(*e.at("gbp", name, who, n))
                        A(gb[:, who, n * 512:(n + 1) * 512], unit("gbp", name, who, n)[:, :], ACT.Copy,
                                 scale=0.5).then_inc(*e.inc("gb", name, who, n, frees=("gbp", name, who, n)))
                for n in range(2):
                    for d in range(6):
                        down_ahead(until, name, n, d)
                        if n == 1 and d == 1:
                            first_squares(nxt, NEXT_T[nxt])

            def parameters(g):
                if g == 0:
                    act.wait_ge(*e.at("cols_copied", 2))
                    A(scc[:, :, 0], cols[:, 2, CC:CC + 8], ACT.Silu).then_inc(*e.inc("scc_half", 0))
                    A(scc[:, :, 1], cols[:, 2, CC + 8:CC + 16], ACT.Silu).then_inc(*e.inc("scc"))
                    act.wait_ge(*e.at("scc"))
                    A(sc4[:, :, 0:2], scc[:, :, :], ACT.Copy).then_inc(*e.inc("sc4hi"))
                elif g == 3:
                    act.wait_ge(*e.at("angles"))
                    A(cs16[:, :, :, :], cs16[:, :, :, :], ACT.Sin).then_inc(*e.inc("sincos"))
                elif g == 4:
                    act.wait_ge(*e.at("lgx"))
                    A(lgs[:, 1, :], lgs[:, 1, :], ACT.Exp).then_inc(*e.inc("lge"))
                    act.wait_ge(L.sem("params_landed"), L.all_params())
                    A(dtb[:, 1, :, :], dtb[:, 1, :, :], ACT.Exp).then_inc(*e.inc("alog"))

            until(NSPLIT - 2)

            gain1 = lambda row: (lambda k, who: col(0, row + k))
            gain2 = lambda k, who: aff[:, k, who:who + 1]

            def bias2(l, j):
                return lambda k, who: modc[:, l, (j * 3) * 8 + k, who:who + 1]

            def mixers(l):
                nm = ("mx", l)
                norm(nm, 256)
                turned(nm, 256, gain1(NORMX + 8 * l), None)
                for i in range(4):
                    ahead(until, ("xbc", l, i))
                    act.wait_ge(*e.at("xbc", l, i))
                    if i == 0:
                        act.wait_ge(*e.at("xr0", l))
                    A(xr[:, 2 * i:2 * i + 2, 3:259], unit("xbc", l, i)[:, :].rearrange("p (m t) -> p m t", m=2),
                             ACT.Copy).then_inc(*e.inc("xr", l, i, frees=("xbc", l, i)))
                ahead(until, ("dt", l))
                ahead(until, (("z", l), 0))
                ahead(until, (("z", l), 1))
                for t in range(2):
                    act.wait_ge(*e.at("zp", l, t))
                    A(z[:, t, :], unit("zp", l, t)[:, :], ACT.Silu).then_inc(*e.inc("z", l, t, frees=("zp", l, t)))
                act.wait_ge(*e.at("dtn", l))
                A(small[:, 64:80], small[:, 64:80], ACT.Exp).then_inc(*e.inc("dte", l))
                for ch in range(8):
                    act.wait_ge(*e.at("conv", l))
                    m = A(cv[:, ch, :], cv[:, ch, :], ACT.Silu, bias=col(1, CVB + 8 * l + ch))
                m.then_inc(*e.inc("cv", l))
                for n in range(2):
                    for half in range(2):
                        ahead(until, (("uv", l, n), half))
                    for t in range(2):
                        act.wait_ge(*e.at("uvp", l, n, t))
                        dst = gv if n else gu
                        A(dst[:, t, :], unit("uvp", l, n, t)[:, :], ACT.Gelu).then_inc(*e.inc("uv", l, n, t, frees=("uvp", l, n, t)))
                for half in range(2):
                    ahead(until, (("cq", l), half))
                for t in range(2):
                    act.wait_ge(*e.at("cqp", l, t))
                    A(cq[:, t, :], unit("cqp", l, t)[:, 0:384], ACT.Copy).then_inc(*e.inc("cq", l, t, frees=("cqp", l, t)))
                for half in range(2):
                    ahead(until, (("ckv", l), half))
                for t in range(2):
                    act.wait_ge(*e.at("ckvp", l, t))
                    A(ckv[:, t, :], unit("ckvp", l, t)[:, 0:288], ACT.Copy).then_inc(*e.inc("ckv", l, t, frees=("ckvp", l, t)))
                for t in range(2):
                    act.wait_ge(*e.at("xst", l, t))
                    A(xs[:, t, :], unit("xst", l, t)[:, :], ACT.Copy).then_inc(*e.inc("xs", l, t, frees=("xst", l, t)))
                act.wait_ge(*e.at("bt", l))
                A(btok[:, :, :], unit("bt", l)[:, 0:256].rearrange("p (g n) -> p g n", g=2), ACT.Copy).then_inc(*e.inc("btok", l, frees=("bt", l)))

                def gate(br, n):
                    for half in range(2):
                        ahead(until, (("g", l, br, n), half))
                    for t in range(2):
                        act.wait_ge(*e.at("gp", l, br, n, t))
                        if br != 0:
                            act.wait_ge(*e.at("merged", l, {2: 0, 1: 2}[br], n, t))
                        A(stripe(gates, n, t), unit("gp", l, br, n, t)[:, :], ACT.Sigmoid)\
                            .then_inc(*e.inc("gate_rows", l, br, n, t, frees=("gp", l, br, n, t)))

                def branch(br):
                    for n in range(2):
                        ahead(until, ("b", l, br, n))

                def scan_exps(c):
                    act.wait_ge(*e.at("diff", l, c))
                    A(E_[:, :, :], E_[:, :, :], ACT.Exp).then_inc(*e.inc("expE", l, c))
                    act.wait_ge(*e.at("dec", l, c))
                    A(small[:, 96:112], small[:, 96:112], ACT.Exp).then_inc(*e.inc("expc", l, c))

                gate(0, 0)
                scan_exps(0)
                gate(0, 1)
                act.wait_ge(*e.at("stp", l))
                A(st[:, :], unit("stp", l)[:, :], ACT.Copy).then_inc(*e.inc("st", l, frees=("stp", l)))
                turned_y(("a", l), 4, 256, ytT[1][0])
                branch(0)
                turned_y(("cq", l), 3, 256, cqTh, lambda c: col(0, QN + 3 * l + c))
                turned_y(("ck", l), 2, 256, ckTh, lambda c: col(0, KVN + 2 * l + c))
                gate(2, 0)
                scan_exps(1)
                gate(2, 1)
                for n in range(2):
                    ahead(until, ("q", l, n))
                    for t in range(2):
                        act.wait_ge(*e.at("qp", l, n, t))
                        A(qk[:, t, 4 * n:4 * n + 4, :],
                                 unit("qp", l, n, t)[:, 0:384].rearrange("p (h d) -> p h d", d=QK), ACT.Copy).then_inc(*e.inc("q", l, n, t, frees=("qp", l, n, t)))
                ahead(until, ("kv", l))
                act.wait_ge(*e.at("yd_in", l, 1))
                for n in range(2):
                    for t in range(2):
                        act.wait_ge(*e.at("kvp", l, n, t))
                        A(stripe(kv, n, t), unit("kvp", l, n, t)[:, :], ACT.Copy).then_inc(*e.inc("kv", l, n, t, frees=("kvp", l, n, t)))
                turned_y(("c", l), 4, 256, ytT[0][0], lambda c: col(0, SSN + 4 * l + c))
                branch(2)
                gate(1, 0)
                gate(1, 1)
                for h in range(HEADS):
                    act.wait_ge(*e.at("qkt", l, h))
                    A(qkT[0:QK, h, :], unit("qkt", l, h)[0:QK, :], ACT.Copy).then_inc(*e.inc("qkT", l, h, frees=("qkt", l, h)))
                for i in range(HEADS + 1):
                    if i < HEADS:
                        h = i
                        act.wait_ge(*e.at("nmax", l, h))
                        if h >= 2:
                            act.wait_ge(*e.at("ptp", l, h - 2))
                        o = 112 + 8 * (h % 2)
                        A(pr[:, h % 2, 0:P], unit("sc", l, h)[:, 0:P], ACT.Exp, scale=QK ** -0.5,
                          bias=small[:, o + 2:o + 3], accum_out=small[:, o + 4:o + 5])
                        m = A(pr[:, h % 2, P:384], unit("sc", l, h)[:, 256:512], ACT.Exp, scale=QK ** -0.5,
                              bias=small[:, o + 3:o + 4], accum_out=small[:, o + 5:o + 6])
                        m.then_inc(*e.inc("pr", l, h, frees=("sc", l, h)))
                    if i >= 1:
                        h = i - 1
                        act.wait_ge(*e.at("ptp", l, h))
                        if h >= 1:
                            act.wait_ge(*e.at("op", l, h - 1))
                        A(pT[:, :], unit("ptp", l, h)[:, 0:384], ACT.Copy).then_inc(*e.inc("pT", l, h, frees=("ptp", l, h)))
                turned_y(("b", l), 4, 256, ytT[1][0])
                branch(1)
                turned_y(("m", l), 8, 256, xT[256][0])
                for half in range(2):
                    ahead(until, (("wo", l, 0), half))
                ahead(until, (("wo", l, 1), 0))
                first_squares(("f2", l), 256)
                ahead_of_tail(until, (("wo", l, 1), 1))

            first_squares(("f1", 0), 256)
            for l in range(DEPTH):
                norm(("f1", l), 256)
                turned(("f1", l), 256, gain1(NORM1 + 8 * l), None)
                ffn(("f1", l), 256, (), ("mx", l), 18 * l)
                mixers(l)
                norm(("f2", l), 256)
                turned(("f2", l), 256, gain1(NORM2 + 8 * l), None)
                ffn(("f2", l), 256, (), ("f1", l + 1) if l == 0 else ("g1", 0), 18 * l + MODS_PER_FFN)

            def block_two_ffn(name, l, j, T, whos, nxt):
                if (name, l) == ("g1", 0):
                    squares((name, l), 3, 0)
                norm((name, l), T)
                turned((name, l), T, gain2, bias2(l, j))
                ffn((name, l), T, whos, nxt)

            block_two_ffn("g1", 0, 0, 512, (0, 1), ("r",))
            norm(("r",), 512)
            turned(("r",), 512, gain2, bias2(0, 1))
            for h in range(4):
                for part, dst in (("q", rq), ("k", rk)):
                    ahead(until, ("r" + part, h))
                    for i in range(2):
                        act.wait_ge(*e.at("r" + part + "p", h, i))
                        if h:
                            act.wait_ge(*e.at("rap", h - 1, 2))
                        A(dst[:, i, 256:512], unit("r" + part + "p", h, i)[:, 256:512], ACT.Copy).then_inc(*e.inc("r" + part + "c", h, i))
                for who in range(2 if h == 0 else 0):
                    for n in range(2):
                        act.wait_ge(*e.at("gbp", ("r",), who, n))
                        A(gbm[:, who, n * 512:(n + 1) * 512], unit("gbp", ("r",), who, n)[:, :], ACT.Copy)\
                            .then_inc(*e.inc("gb", ("r",), who, n, frees=("gbp", ("r",), who, n)))
                for half in range(2):
                    ahead(until, (("rv", h), half))
                for t in range(4):
                    act.wait_ge(*e.at("rvp", h, t))
                    if h:
                        act.wait_ge(*e.at("rop", h - 1, 3))
                    A(rv[:, t, :], unit("rvp", h, t)[:, :], ACT.Copy).then_inc(*e.inc("rv", h, t, frees=("rvp", h, t)))
                for half in range(2):
                    ahead(until, (("rg", h), half))
                for t in range(4):
                    act.wait_ge(*e.at("rgp", h, t))
                    if h:
                        act.wait_ge(*e.at("ty", ("r", h - 1), 3))
                    A(rg[:, t, :], unit("rgp", h, t)[:, :], ACT.Silu).then_inc(*e.inc("rg", h, t, frees=("rgp", h, t)))
                dist = rcst[:, R_DIST:R_DIST + 512].rearrange("p (j i) -> p j i", j=2)
                act.wait_ge(*e.at("lg"))
                if h:
                    act.wait_ge(*e.at("ra", h - 1, 2))
                act.wait_ge(*e.at("wlog", h))
                A(WX[:, :, 1, :], WX[:, :, 1, :], ACT.Exp)
                A(WX[:, :, 0, :], dist, ACT.Exp, scale=lgs[:, 2, h:h + 1], bias=lgs[:, 3, h:h + 1])
                m = A(wtmp[:, :, 0, :], dist, ACT.Exp, scale=lgs[:, 4, 4 + h:5 + h], bias=lgs[:, 3, 4 + h:5 + h])
                m.then_inc(*e.inc("wexp", h))
                turned_y(("r", h), 4, 512, rYh, lambda c, h=h: col(1, GN + 4 * h + c))
                for n in range(2):
                    if h == 3 and n == 1:
                        first_squares(("g2", 0), 512)
                        ahead_of_tail(until, ("rw", h, n))
                    else:
                        ahead(until, ("rw", h, n))
                    if h == 0:
                        for t in range(4):
                            act.wait_ge(*e.at("rwp", 0, n, t))
                            A(stripe(Y, n, t), unit("rwp", 0, n, t)[:, :], ACT.Copy).then_inc(*e.inc("Y0", n, t, frees=("rwp", 0, n, t)))
            block_two_ffn("g2", 0, 2, 512, (0, 1), ("g1", 1))
            block_two_ffn("g1", 1, 0, 512, (0, 1), ("n",))
            norm(("n",), 512)
            turned(("n",), 512, gain2, bias2(1, 1))
            for j in range(4):
                ahead(until, ("nq", j))
                act.wait_ge(*e.at("nqp", j))
                A(nq[:, 2 * j:2 * j + 2, :], unit("nqp", j)[:, :].rearrange("p (m t) -> p m t", m=2), ACT.Copy,
                         scale=0.125).then_inc(*e.inc("nq", j, frees=("nqp", j)))
            for j in range(4):
                ahead(until, ("nk", j))
                for i in range(2):
                    act.wait_ge(*e.at("nkp", j, i))
                    A(nk[:, 2 * j + i, :], unit("nkp", j, i)[:, :], ACT.Copy).then_inc(*e.inc("nk", j, i, frees=("nkp", j, i)))
            for n in range(2):
                for half in range(2):
                    ahead(until, (("nv", n), half))
                for t in range(4):
                    act.wait_ge(*e.at("nvp", n, t))
                    A(stripe(nv, n, t), unit("nvp", n, t)[:, :], ACT.Copy).then_inc(*e.inc("nv", n, t, frees=("nvp", n, t)))
            items = [(h, t) for h in range(16) for t in range(2)]
            for i, (h, t) in enumerate(items):
                act.wait_ge(*e.at("nnm", h, t))
                if h:
                    act.wait_ge(*e.at("nptp", h - 1, t))
                o = 128 + 4 * (i % 4)
                m = A(npr[:, t, :], unit("nsp", h, t)[:, :], ACT.Exp, bias=small[:, o + 1:o + 2],
                      accum_out=small[:, o + 2:o + 3])
                m.then_inc(*e.inc("npr", h, t, frees=("nsp", h, t)))
            for n in range(2):
                act.wait_ge(*e.at("gbp", ("n",), 0, n))
                A(gbm[:, 0, n * 512:(n + 1) * 512], unit("gbp", ("n",), 0, n)[:, :], ACT.Copy).then_inc(*e.inc("gb", ("n",), 0, n, frees=("gbp", ("n",), 0, n)))
            turned_y(("n",), 8, 256, xT[256][0])
            for half in range(2):
                ahead(until, (("nw", 0), half))
            ahead(until, (("nw", 1), 0))
            first_squares(("g2", 1), 256)
            ahead_of_tail(until, (("nw", 1), 1))
            block_two_ffn("g2", 1, 2, 256, (0,), ("last",))
            norm(("last",), 256)

        @block.vector
        def _(dve):
            e = Signals(L, "dve")
            chained = [0]

            def link(ins):
                chained[0] += 1
                ins.then_inc(L.sem("dve_chain"), 1)
                dve.wait_ge(L.sem("dve_chain"), chained[0])

            split = [0]

            def until(s):
                while split[0] <= min(s, len(slabs.parts) - 1):
                    key, part = slabs.parts[split[0]][0:2]
                    split[0] += 1
                    src, hi, lo = part_views(key, part)
                    dve.wait_ge(*e.at("hi", key, part))
                    nc.vector.tensor_tensor(lo, src, hi.bitcast(F32), ALU.subtract).then_inc(*e.inc("lo", key, part))

            V = nc.vector
            TT, TS, STT = V.tensor_tensor, V.tensor_scalar, V.scalar_tensor_tensor

            def sumsq(dst, a, junk):
                return V.tensor_tensor_reduce(junk, a, a, 1.0, 0.0, ALU.mult, ALU.add, dst)

            def rstd(name, src, n, width):
                TS(src, src, 1.0 / width, EPS, ALU.mult, ALU.add).then_inc(*e.inc("ms", name))
                dve.wait_ge(*e.at("rstd", name))

            def squares(name, t, n):
                dve.wait_ge(*e.at("X", name, t, n))
                a = stripe(X, n, t)
                link(V.tensor_tensor_reduce(junk_v[:, :], a, a, 1.0 / D, 0.0, ALU.mult, ALU.add,
                                            small[:, 4 * n + t:4 * n + t + 1]))

            def first_squares(name, T):
                for t in range(0, T // P, 2):
                    squares(name, t, 0)

            def norm(name, T, rows=None, tiles=4):
                def mean_square(t):
                    if t % 2:
                        dve.wait_ge(*e.at("ssa", name, t, 1))
                    STT(small[:, t:t + 1], small[:, t:t + 1], EPS, small[:, 4 + t:5 + t], ALU.add, ALU.add)\
                        .then_inc(*e.inc("ms", name, t))

                for t in range(T // P + 1):
                    if t < T // P:
                        if rows and t < tiles:
                            rows(t)
                        if t % 2 == 0:
                            squares(name, t, 1)
                            mean_square(t)
                    if t:
                        if t % 2 == 0:
                            mean_square(t - 1)
                        dve.wait_ge(*e.at("rstd", name, t - 1))
                        TS(stripe(xn, 0, t - 1), stripe(X, 0, t - 1), small[:, 7 + t:8 + t], None, ALU.mult)\
                            .then_inc(*e.inc("xn", name, t - 1, 0))

            def turned(name, T, gain, bias):
                xTh, xTl = xT[T]
                for k in range(KD):
                    dve.wait_ge(*e.at("xh", name, k))
                    if bias:
                        tc = lambda x: x[:, k, :].rearrange("p (t c) -> p t c", c=P)
                        TT(tc(xTl), xn[:, 0:T // P, k * P:(k + 1) * P], tc(xTh).bitcast(F32), ALU.subtract)\
                            .then_inc(*e.inc("xT", name, k))
                    else:
                        STT(xTl[:, k, :], unit("turn", name, k)[:, 0:256], gain(k, 0), xTh[:, k, :].bitcast(F32),
                            ALU.mult, ALU.subtract).then_inc(*e.inc("xT", name, k, frees=("turn", name, k)))

            def turned_y(name, chunks, T, dsth, dstl, gain=None):
                per = 512 // T
                for u in range((chunks + per - 1) // per):
                    dve.wait_ge(*e.at("ty", name, u))
                    ps = unit("ty", name, u)
                    if gain is None:
                        dve.wait_ge(*e.at("yh", name, u))
                        m = TT(dstl[:, u * per:(u + 1) * per, 0:T], ps[:, :].rearrange("p (j t) -> p j t", t=T),
                               dsth[:, u * per:(u + 1) * per, 0:T].bitcast(F32), ALU.subtract)
                        m.then_inc(*e.inc("yT", name, u, frees=("ty", name, u)))
                    else:
                        n = min(per, chunks - u * per)
                        dve.wait_ge(*e.at("yh", name, u * per + n - 1))
                        for j in range(n):
                            c = u * per + j
                            m = STT(dstl[:, c, 0:T], ps[:, j * T:(j + 1) * T], gain(c),
                                    dsth[:, c, 0:T].bitcast(F32), ALU.mult, ALU.subtract)
                            m.then_inc(*e.inc("yT", name, c, frees=("ty", name, u) if j == n - 1 else None))

            def mod_row(i):
                dve.wait_ge(*e.at("modp", i))
                if i:
                    dve.wait_ge(*e.at("modtp", i - 1))
                V.tensor_copy(modrow[:, :], unit("modp", i)[0:4, :]).then_inc(*e.inc("modrow", i, frees=("modp", i)))

            def mod_cols(i):
                l, g = divmod(i, 18)
                dve.wait_ge(*e.at("modtp", i))
                ps = unit("modtp", i)[:, 0:16].rearrange("p (c w) -> p c w", w=4)
                V.tensor_copy(modt[:, :, :], ps).then_inc(*e.inc("modt", i, frees=("modtp", i)))
                dve.wait_ge(*e.at("modt", i))
                link(TT(modt[:, :, 0:2], modt[:, :, 0:2], modt[:, :, 2:4], ALU.add))
                b = cols[:, 2 + l, BM + 4 * g:BM + 4 * g + 4].unsqueeze(2).to_broadcast([P, 4, 2])
                TT(modc[:, l, 4 * g:4 * g + 4, :], modt[:, :, 0:2], b, ALU.add).then_inc(*e.inc("modc", i))

            def affine(name, l, j):
                g = cols[:, 0, NORMG + 24 * l + 8 * j:NORMG + 24 * l + 8 * j + 8].unsqueeze(2)\
                    .to_broadcast([P, 8, 2])
                m = STT(aff[:, :, :], modc[:, l, (j * 3 + 1) * 8:(j * 3 + 2) * 8, :], 1.0, g, ALU.add, ALU.mult)
                m.then_inc(*e.inc("aff", name))
                dve.wait_ge(*e.at("aff", name))

            def diagonals(name, l, j, dgt, whos):
                for who in whos:
                    if who:
                        dve.wait_ge(*e.at("gbp", name, who - 1, 1))
                    gcol = modc[:, l, (j * 3 + 2) * 8:(j * 3 + 3) * 8, who:who + 1].to_broadcast([P, 8, P])
                    TT(dgt[:, :, :], ident.unsqueeze(1).to_broadcast([P, 8, P]), gcol, ALU.mult).then_inc(*e.inc("diag", name, who))

            def ffn(name, T, mod0, l=0, j=0, whos=(), nxt=None):
                per = T // 256
                for g in range(GROUPS):
                    ahead(until, (name, "gate", g))
                    if name == ("f1", 0):
                        parameters(g)
                    ahead(until, (name, "up", g))
                    for i in range(per):
                        b = (g * per + i) % 2
                        o = (g * per + i) * 512
                        dve.wait_ge(*e.at("sg", name, g, i))
                        dve.wait_ge(*e.at("up", name, g, i))
                        TT(sg[:, b, :], sg[:, b, :], unit("up", name, g, i)[:, :], ALU.mult).then_inc(*e.inc("ht", name, g, i, frees=("up", name, g, i)))
                    for i in range(per):
                        b = (g * per + i) % 2
                        o = (g * per + i) * 512
                        dve.wait_ge(*e.at("ht", name, g, i))
                        dve.wait_ge(*e.at("hhi", name, g, i))
                        TT(hl[:, o:o + 512], sg[:, b, :], hh[:, o:o + 512].bitcast(F32), ALU.subtract).then_inc(*e.inc("hidden", name, g, i))
                    if mod0 is not None:
                        if 1 < g <= MODS_PER_FFN + 1:
                            mod_cols(mod0 + g - 2)
                        if 0 < g <= MODS_PER_FFN:
                            ahead(until, ("mod", mod0 + g - 1, 1))
                            mod_row(mod0 + g - 1)
                if whos:
                    dve.wait_ge(*e.at("up", name, GROUPS - 1, per - 1))
                    diagonals(name, l, j, dg, whos)
                def rows(t, n=1):
                    dve.wait_ge(*e.at("down", name, n, t))
                    ps = unit("down", name, n, t)
                    if not whos:
                        STT(stripe(X, n, t), ps[:, :], 0.5, stripe(X, n, t), ALU.mult, ALU.add)\
                            .then_inc(*e.inc("X", nxt, t, n, frees=("down", name, n, t)))
                    else:
                        dve.wait_ge(*e.at("gb", name, t // 2, 1))
                        TT(sg[:, t % 2, :], ps[:, :], stripe(gb, n, t // 2), ALU.mult)\
                            .then_inc(*e.inc("sgg", name, n, t, frees=("down", name, n, t)))
                        dve.wait_ge(*e.at("sgg", name, n, t))
                        TT(stripe(X, n, t), sg[:, t % 2, :], stripe(X, n, t), ALU.add)\
                            .then_inc(*e.inc("X", nxt, t, n))

                for n in range(2):
                    for d in range(6):
                        down_ahead(until, name, n, d)
                        if n == 1 and d == 1:
                            first_squares(nxt, NEXT_T[nxt])
                    if n == 0:
                        for t in tiles_of(T):
                            rows(t, 0)
                return rows

            def columns(i):
                dve.wait_ge(*e.at("cols", i))
                also = [("aff", (n, l)) for n in ("f1", "mx", "f2") for l in range(DEPTH)] if i == 0 else []
                V.tensor_copy(cols[:, i, 0:ROWS[i]], unit("cols", i)[:, 0:ROWS[i]])\
                    .then_inc(*e.inc("cols_copied", i, also=also, frees=("cols", i)))

            def angles(t):
                a = cs16[:, t, 0, :]
                r = small[:, 144:160]
                link(TS(a, cst[:, C_FREQ:C_FREQ + 16], bsum[:, 4 + t:5 + t], None, ALU.mult))
                link(TS(r, a, 1.0 / TWO_PI, None, ALU.mult))
                link(TS(r, r, 12582912.0, None, ALU.add))
                link(TS(r, r, -12582912.0, None, ALU.add))
                for c in (TP1, TP2, TP3):
                    link(STT(a, r, -c, a, ALU.mult, ALU.add))
                link(TS(cs16[:, t, 1, :], a, -1.0, None, ALU.mult))
                link(TT(cs16[:, t, 1, :], cs16[:, t, 1, :], a, ALU.min))
                link(TS(cs16[:, t, 1, :], cs16[:, t, 1, :], TWO_PI / 4, None, ALU.add))
                TS(a, a, 3.1415925, -3.1415925, ALU.min, ALU.max).then_inc(*e.inc("angles"))

            def log1p(x, s, y, q):
                link(TS(s, x, 2.0, None, ALU.add))
                link(V.reciprocal(s, s))
                link(TT(s, s, x, ALU.mult))
                link(TT(y, s, s, ALU.mult))
                link(TS(q, y, 1.0 / 17, None, ALU.mult))
                for k in (15, 13, 11, 9, 7, 5, 3):
                    link(STT(q, q, 1.0 / k, y, ALU.add, ALU.mult))
                link(STT(q, q, 1.0, s, ALU.add, ALU.mult))
                return q

            def parameters(g):
                if g == 0:
                    for i in range(1, 4):
                        columns(i)
                elif g == 1:
                    dve.wait_ge(*e.at("sc4hi"))
                    TT(sc4[:, :, 2:4], scc[:, :, :], sc4[:, :, 0:2].bitcast(F32), ALU.subtract).then_inc(*e.inc("sc4"))
                    dve.wait_ge(L.sem("params_landed"), L.all_params())
                    link(V.tensor_copy(bsum[:, 4:6], bsum[:, 0:2].bitcast(I32)))
                    angles(0)
                elif g == 2:
                    angles(1)
                elif g == 3:
                    d = lgs[:, 0, :]
                    link(TS(lgs[:, 1, :], d, -1.0, None, ALU.mult))
                    TT(lgs[:, 1, :], lgs[:, 1, :], d, ALU.min).then_inc(*e.inc("lgx"))
                elif g == 5:
                    d = lgs[:, 0, :]
                    dve.wait_ge(*e.at("lge"))
                    q = log1p(lgs[:, 1, :], lgs[:, 5, :], lgs[:, 6, :], lgs[:, 7, :])
                    link(TS(d, d, 0.0, None, ALU.min))
                    link(STT(lgs[:, 2, :], q, -2.0, d, ALU.mult, ALU.add))
                    link(TS(lgs[:, 3, :], lgs[:, 2, :], 256.0, None, ALU.mult))
                    TS(lgs[:, 4, :], lgs[:, 2, :], -1.0, None, ALU.mult).then_inc(*e.inc("lg"))
                    dve.wait_ge(*e.at("lg"))
                    dve.wait_ge(*e.at("alog"))
                    link(TS(dtb[:, 1, :, :], dtb[:, 1, :, :], -1.0, None, ALU.mult))

            gain1 = lambda row: (lambda k, who: col(0, row + k))
            gain2 = lambda k, who: aff[:, k, who:who + 1]

            def bias2(l, j):
                return lambda k, who: modc[:, l, (j * 3) * 8 + k, who:who + 1]

            def heads(a, n, width):
                return a.unsqueeze(2).to_broadcast([P, n, width])

            def mixers(l, rows):
                nm = ("mx", l)
                norm(nm, 256, rows)
                turned(nm, 256, gain1(NORMX + 8 * l), None)
                for i in range(4):
                    ahead(until, ("xbc", l, i))
                ahead(until, ("dt", l))
                dtv, dte = small[:, 16:32], small[:, 64:80]
                for t in range(2):
                    dve.wait_ge(*e.at("dtp", l, t))
                    m = TT(small[:, 16 + 8 * t:24 + 8 * t], unit("dtp", l, t)[:, 0:8], dtb[:, 0, l, :], ALU.add)
                    m.then_inc(*e.inc("dtr", l, t, frees=("dtp", l, t)))
                    dve.wait_ge(*e.at("dtr", l, t))
                link(TS(dte, dtv, -1.0, None, ALU.mult))
                TT(dte, dte, dtv, ALU.min).then_inc(*e.inc("dtn", l))
                for i in range(4):
                    dve.wait_ge(*e.at("xr", l, i))
                for tap in range(4):
                    for ch in range(8):
                        wc = col(1, CVW + 32 * l + 8 * tap + ch)
                        src = xr[:, ch, tap:tap + 256]
                        if tap == 0:
                            m = TS(cv[:, ch, :], src, wc, None, ALU.mult)
                        else:
                            m = STT(cv[:, ch, :], src, wc, cv[:, ch, :], ALU.mult, ALU.add)
                    if tap < 3:
                        link(m)
                    else:
                        m.then_inc(*e.inc("conv", l))
                    ahead(until, (("z", l), tap % 2))
                dve.wait_ge(*e.at("dte", l))
                q = log1p(dte, small[:, 160:176], small[:, 176:192], small[:, 192:208])
                link(TS(dtv, dtv, 0.0, None, ALU.max))
                link(STT(dtv, q, 2.0, dtv, ALU.mult, ALU.add))
                for t in range(2):
                    link(TT(small[:, 32 + 8 * t:40 + 8 * t], small[:, 16 + 8 * t:24 + 8 * t], dtb[:, 1, l, :], ALU.mult))
                h64 = lambda a: a.rearrange("p (h d) -> p h d", d=64)

                def gate(br, n, half):
                    ahead(until, (("g", l, br, n), half))

                def branch(br):
                    for n in range(2):
                        ahead(until, ("b", l, br, n))
                        for t in range(2):
                            dve.wait_ge(*e.at("bp", l, br, n, t))
                            dve.wait_ge(*e.at("gate_rows", l, br, n, t))
                            ps = unit("bp", l, br, n, t)
                            if br == 0:
                                TT(stripe(merged, n, t), ps[:, :], stripe(gates, n, t), ALU.mult)\
                                    .then_inc(*e.inc("merged", l, br, n, t, frees=("bp", l, br, n, t)))
                            else:
                                m = TT(tmp[:, t, :], ps[:, :], stripe(gates, n, t), ALU.mult)
                                m.then_inc(*e.inc("mtmp", l, br, n, t, frees=("bp", l, br, n, t)))
                                dve.wait_ge(*e.at("mtmp", l, br, n, t))
                                TT(stripe(merged, n, t), tmp[:, t, :], stripe(merged, n, t), ALU.add)\
                                    .then_inc(*e.inc("merged", l, br, n, t, also=[("mg", l, t)] if br == 1 and n == 1 else []))

                def scan_decays(c):
                    TT(E_[:, :, :], upper.unsqueeze(1).to_broadcast([P, 8, P]),
                       heads(small[:, 32 + 8 * c:40 + 8 * c], 8, P), ALU.mult).then_inc(*e.inc("daU", l, c))

                def scan_differences(c):
                    dve.wait_ge(*e.at("xs", l, c))
                    if c:
                        dve.wait_ge(*e.at("stp", l))
                    link(TT(h64(xdt[:, :]), h64(xs[:, c, :]), heads(small[:, 16 + 8 * c:24 + 8 * c], 8, 64), ALU.mult))
                    dve.wait_ge(*e.at("csp", l, c))
                    csc = small[:, 80:96]
                    V.tensor_copy(csc, unit("csp", l, c)[:, 0:16]).then_inc(*e.inc("csc", l, c, frees=("csp", l, c)))
                    dve.wait_ge(*e.at("csc", l, c))
                    V.tensor_copy(small[:, 96:104], csc[:, 0:8])
                    TT(small[:, 104:112], csc[:, 8:16], csc[:, 0:8], ALU.subtract).then_inc(*e.inc("dec", l, c))
                    for h2 in range(2):
                        dve.wait_ge(*e.at("csb", l, c, h2))
                    for h2 in range(2):
                        for h in range(4):
                            m = TS(E_[:, 4 * h2 + h, :], unit("csb", l, c, h2)[:, h * P:(h + 1) * P],
                                   csc[:, 4 * h2 + h:4 * h2 + h + 1], 0.0, ALU.subtract, ALU.min)
                        m.then_inc(*e.inc("diff_half", l, c, h2, also=[("diff", l, c)], frees=("csb", l, c, h2)))
                    dve.wait_ge(*e.at("cbp", l, c))
                    TT(cbm[:, :, :], unit("cbp", l, c)[:, 0:256].rearrange("p (g t) -> p g t", g=2),
                       upper.unsqueeze(1).to_broadcast([P, 2, P]), ALU.mult).then_inc(*e.inc("cbm", l, c, frees=("cbp", l, c)))

                def scan_weights(c):
                    dve.wait_ge(*e.at("expE", l, c))
                    dve.wait_ge(*e.at("cbm", l, c))
                    for g in range(2):
                        m = TT(E_[:, 4 * g:4 * g + 4, :], E_[:, 4 * g:4 * g + 4, :],
                               cbm[:, g:g + 1, :].to_broadcast([P, 4, P]), ALU.mult)
                    m.then_inc(*e.inc("MT", l, c))
                    dve.wait_ge(*e.at("expc", l, c))
                    if c == 0:
                        TT(h64(xdd[:, :]), h64(xdt[:, :]), heads(small[:, 104:112], 8, 64), ALU.mult).then_inc(*e.inc("xdd", l))

                def scan_rows(c):
                    link(TT(h64(tmp[:, 0, :]), h64(xs[:, c, :]), heads(dtb[:, 2, l, :], 8, 64), ALU.mult))
                    dve.wait_ge(*e.at("yd", l, c))
                    m = TT(tmp[:, 0, :], unit("yd", l, c)[:, :], tmp[:, 0, :], ALU.add)
                    m.then_inc(*e.inc("yd_in", l, c, frees=("yd", l, c)))
                    dve.wait_ge(*e.at("yd_in", l, c))
                    if c:
                        dve.wait_ge(*e.at("yo", l))
                        m = TT(h64(tmp[:, 1, :]), h64(unit("yo", l)[:, :]), heads(small[:, 96:104], 8, 64), ALU.mult)
                        m.then_inc(*e.inc("yo_in", l, frees=("yo", l)))
                        dve.wait_ge(*e.at("yo_in", l))
                        link(TT(tmp[:, 0, :], tmp[:, 0, :], tmp[:, 1, :], ALU.add))
                    dve.wait_ge(*e.at("z", l, c))
                    link(TT(z[:, c, :], z[:, c, :], tmp[:, 0, :], ALU.mult))

                def scan_norm(c):
                    for g in range(2):
                        link(sumsq(small[:, 216 + g:217 + g], z[:, c, g * 256:(g + 1) * 256], tmp[:, 1, 0:256]))
                    rstd(("yc", l, c), small[:, 216:218], 2, 256)
                    for g in range(2):
                        m = TS(z[:, c, g * 256:(g + 1) * 256], z[:, c, g * 256:(g + 1) * 256],
                               small[:, 218 + g:219 + g], None, ALU.mult)
                    m.then_inc(*e.inc("yc", l, c))

                scan_decays(0)
                for n in range(2):
                    for half in range(2):
                        ahead(until, (("uv", l, n), half))
                for half in range(2):
                    ahead(until, (("cq", l), half))
                for half in range(2):
                    ahead(until, (("ckv", l), half))
                for t in range(2):
                    dve.wait_ge(*e.at("uv", l, 1, t))
                    link(sumsq(small[:, 48 + t:49 + t], gv[:, t, :], junk512))
                rstd(("gv", l), small[:, 48:50], 2, 512)
                dve.wait_ge(L.sem("vgain_landed"), 16 * (l + 1))
                for t in range(2):
                    STT(gv[:, t, :], gv[:, t, :], small[:, 50 + t:51 + t], vgain[:, :], ALU.mult, ALU.mult).then_inc(*e.inc("gvn", l, t))
                gate(0, 0, 0)
                scan_differences(0)
                gate(0, 0, 1)
                dve.wait_ge(*e.at("wst", l))
                TT(wT[:, :, :], unit("wst", l)[:, :].rearrange("p (g t) -> p g t", g=4),
                   upper.unsqueeze(1).to_broadcast([P, 4, P]), ALU.mult).then_inc(*e.inc("wT", l, frees=("wst", l)))
                gate(0, 1, 0)
                scan_weights(0)
                for name, a, n, s in (("cq", cq, 384, 208), ("ck", ckv, 256, 212)):
                    for t in range(2):
                        dve.wait_ge(*e.at({"cq": "cq", "ck": "ckv"}[name], l, t))
                        link(sumsq(small[:, s + t:s + t + 1], a[:, t, 0:n], junk512[:, 0:n]))
                    rstd((name, l), small[:, s:s + 2], 2, n)
                    for t in range(2):
                        TS(a[:, t, 0:n], a[:, t, 0:n], small[:, s + 2 + t:s + 3 + t], None, ALU.mult).then_inc(*e.inc(name + "n", l, t))
                gate(0, 1, 1)
                for t in range(2):
                    dve.wait_ge(*e.at("spp", l, t))
                    dve.wait_ge(*e.at("uv", l, 0, t))
                    ps = unit("spp", l, t)
                    for g in range(4):
                        s = slice(g * P, (g + 1) * P)
                        m = STT(gu[:, t, s], ps[:, s], col(1, BS + 4 * l + g), gu[:, t, s], ALU.add, ALU.mult)
                    m.then_inc(*e.inc("ya", l, t, frees=("spp", l, t)))
                turned_y(("a", l), 4, 256, *ytT[1])
                scan_rows(0)
                scan_decays(1)
                branch(0)
                turned_y(("cq", l), 3, 256, cqTh, cqTl, lambda c: col(0, QN + 3 * l + c))
                turned_y(("ck", l), 2, 256, ckTh, ckTl, lambda c: col(0, KVN + 2 * l + c))
                gate(2, 0, 0)
                scan_differences(1)
                gate(2, 0, 1)
                scan_norm(0)
                gate(2, 1, 0)
                scan_weights(1)
                gate(2, 1, 1)
                scan_rows(1)
                ahead(until, ("q", l, 0))
                scan_norm(1)
                ahead(until, ("q", l, 1))
                ahead(until, ("kv", l))
                turned_y(("c", l), 4, 256, *ytT[0], gain=lambda c: col(0, SSN + 4 * l + c))
                branch(2)
                for n in range(2):
                    for t in range(2):
                        dve.wait_ge(*e.at("q", l, n, t))
                        dve.wait_ge(*e.at("kv", l, n, t))
                for t in range(2):
                    kk = kv[:, t, :].rearrange("p (h d) -> p h d", d=P)
                    V.tensor_copy(qk[:, t, 8:16, 0:64], kk[:, :, 0:64])
                    link(V.tensor_copy(qk[:, t, 8:16, 64:96],
                                         ckv[:, t, 256:288].unsqueeze(1).to_broadcast([P, 8, 32])))
                for t in range(2):
                    a = qk[:, t, :, :]
                    gate(1, 0, t)
                    link(TT(sq[:, :, :], a, a, ALU.mult))
                    link(V.tensor_reduce(small[:, 224:240], sq[:, :, :], AX, ALU.add))
                    rstd(("qk", l, t), small[:, 224:240], 16, QK)
                    link(TT(a, a, heads(small[:, 240:256], 16, QK), ALU.mult))
                    for i in range(2):
                        m = TT(qk[:, t, 8 * i:8 * i + 8, :], qk[:, t, 8 * i:8 * i + 8, :],
                               qkg[:, l, i:i + 1, :].to_broadcast([P, 8, QK]), ALU.mult)
                    link(m)
                    gate(1, 1, t)
                    x1, x2 = a[:, :, 64:80], a[:, :, 80:96]
                    sn, cn = (cs16[:, t, i:i + 1, :].to_broadcast([P, 16, 16]) for i in range(2))
                    dve.wait_ge(*e.at("sincos"))
                    q4 = [sq[:, :, 16 * i:16 * i + 16] for i in range(4)]
                    TT(q4[0], x1, cn, ALU.mult)
                    TT(q4[1], x2, sn, ALU.mult)
                    TT(q4[2], x2, cn, ALU.mult)
                    link(TT(q4[3], x1, sn, ALU.mult))
                    TT(x1, q4[0], q4[1], ALU.subtract)
                    TT(x2, q4[2], q4[3], ALU.add).then_inc(*e.inc("qkr", l, t))
                    dve.wait_ge(*e.at("qkr", l, t))
                for i in range(HEADS + 2):
                    if i < HEADS:
                        h = i
                        o = 112 + 8 * (h % 2)
                        dve.wait_ge(*e.at("sc", l, h))
                        ps = unit("sc", l, h)
                        dv = ps[:, :].rearrange("p (a b) -> p a b", b=P)[:, 0:4:3, :]
                        link(TT(dv, dv, cst[:, C_CAUSAL:C_CAUSAL + P].unsqueeze(1).to_broadcast([P, 2, P]), ALU.add))
                        V.tensor_reduce(small[:, o:o + 1], ps[:, 0:P], AX, ALU.max)
                        link(V.tensor_reduce(small[:, o + 1:o + 2], ps[:, 256:512], AX, ALU.max))
                        TS(small[:, o + 2:o + 4], small[:, o:o + 2], -QK ** -0.5, None, ALU.mult).then_inc(*e.inc("nmax", l, h))
                    if i >= 2:
                        h = i - 2
                        o = 112 + 8 * (h % 2)
                        dve.wait_ge(*e.at("op", l, h))
                        for t in range(2):
                            m = TS(yb[:, t, h * 64:(h + 1) * 64], unit("op", l, h)[:, 64 * t:64 * t + 64],
                                   small[:, o + 6 + t:o + 7 + t], None, ALU.mult)
                        m.then_inc(*e.inc("yb_head", l, h, also=[("yb", l, 0), ("yb", l, 1)], frees=("op", l, h)))
                    if 1 <= i <= HEADS:
                        h = i - 1
                        o = 112 + 8 * (h % 2)
                        dve.wait_ge(*e.at("pr", l, h))
                        link(V.reciprocal(small[:, o + 6:o + 8], small[:, o + 4:o + 6]))
                turned_y(("b", l), 4, 256, *ytT[1])
                branch(1)
                turned_y(("m", l), 8, 256, *xT[256])
                def rows(t, n=1):
                    dve.wait_ge(*e.at("wop", l, n, t))
                    TT(stripe(X, n, t), unit("wop", l, n, t)[:, :], stripe(X, n, t), ALU.add)\
                        .then_inc(*e.inc("X", ("f2", l), t, n, frees=("wop", l, n, t)))

                for half in range(2):
                    ahead(until, (("wo", l, 0), half))
                for t in range(2):
                    rows(t, 0)
                ahead(until, (("wo", l, 1), 0))
                first_squares(("f2", l), 256)
                ahead_of_tail(until, (("wo", l, 1), 1))
                return rows

            junk512 = tmp[:, 1, :]
            until(NSPLIT - 2)
            dve.wait_ge(L.sem("x_landed"), 16)
            V.memset(small[:, 0:8], 0.0).then_inc(*e.inc("X", ("f1", 0), 0, 0, also=[
                ("X", ("f1", 0), t, n) for t in range(2) for n in range(2)]))
            dve.wait_ge(*e.at("X", ("f1", 0), 0, 0))
            first_squares(("f1", 0), 256)
            rows = None
            for l in range(DEPTH):
                norm(("f1", l), 256, rows)
                if l == 0:
                    columns(0)
                    dve.wait_ge(*e.at("cols_copied", 0))
                turned(("f1", l), 256, gain1(NORM1 + 8 * l), None)
                rows = ffn(("f1", l), 256, 18 * l, nxt=("mx", l))
                rows = mixers(l, rows)
                norm(("f2", l), 256, rows)
                turned(("f2", l), 256, gain1(NORM2 + 8 * l), None)
                rows = ffn(("f2", l), 256, 18 * l + MODS_PER_FFN, nxt=("f1", l + 1) if l == 0 else ("g1", 0))

            def block_two_ffn(name, l, j, T, whos, nxt, rows):
                nm = (name, l)
                if nm == ("g1", 0):
                    V.memset(small[:, 2:4], 0.0).then_inc(*e.inc("ctx_ready", also=[
                        ("X", nm, t, n) for t in (2, 3) for n in range(2)]))
                    dve.wait_ge(*e.at("ctx_ready"))
                    squares(nm, 2, 0)
                affine(nm, l, j)
                norm(nm, T, rows, 2 if nm == ("g1", 0) else 4)
                turned(nm, T, gain2, bias2(l, j))
                return ffn(nm, T, None, l, j, whos, nxt)

            rows = block_two_ffn("g1", 0, 0, 512, (0, 1), ("r",), rows)
            affine(("r",), 0, 1)
            norm(("r",), 512, rows)
            turned(("r",), 512, gain2, bias2(0, 1))
            dist = rcst[:, R_DIST:R_DIST + 512].rearrange("p (j i) -> p j i", j=2)
            cosT, sinT = rcst[:, R_COS:R_COS + 256], rcst[:, R_SIN:R_SIN + 256]
            dve.wait_ge(L.sem("rcst_landed"), 16)
            for h in range(4):
                for part, dst in (("q", rq), ("k", rk)):
                    ahead(until, ("r" + part, h))
                    p0, p1 = (unit("r" + part + "p", h, i)[:, 0:256] for i in range(2))
                    for i in range(2):
                        dve.wait_ge(*e.at("r" + part + "c", h, i))
                    if h:
                        dve.wait_ge(*e.at("rap", h - 1, 2))
                    r0, r1 = rt[:, 0, 0:256], rt[:, 0, 256:512]
                    TT(dst[:, 0, 0:256], p0, cosT, ALU.mult)
                    TT(r0, p1, sinT, ALU.mult)
                    TT(dst[:, 1, 0:256], p1, cosT, ALU.mult)
                    link(TT(r1, p0, sinT, ALU.mult))
                    TT(dst[:, 0, 0:256], dst[:, 0, 0:256], r0, ALU.subtract)
                    m = TT(dst[:, 1, 0:256], dst[:, 1, 0:256], r1, ALU.add)
                    m.then_inc(*e.inc("rope", h, part, also=[("rqk", h)], frees=("r" + part + "p", h, 0)))
                    L.freed[("r" + part + "p", h, 1)] = L.events[("rope", h, part)]
                    dve.wait_ge(*e.at("rope", h, part))
                if h == 0:
                    diagonals(("r",), 0, 1, dgm, (0, 1))
                for part in "vg":
                    for half in range(2):
                        ahead(until, (("r" + part, h), half))
                if h:
                    dve.wait_ge(*e.at("ra", h - 1, 2))
                V.tensor_scalar(WX[:, :, 1, :], dist, 0.0, lgs[:, 2, h:h + 1], ALU.max, ALU.mult)
                link(V.tensor_scalar(wtmp[:, :, 1, :], dist, 0.0, lgs[:, 4, 4 + h:5 + h], ALU.min, ALU.mult))
                TT(WX[:, :, 1, :], WX[:, :, 1, :], wtmp[:, :, 1, :], ALU.add).then_inc(*e.inc("wlog", h))
                dve.wait_ge(*e.at("wexp", h))
                link(TT(WX[:, :, 0, :], WX[:, :, 0, :], wtmp[:, :, 0, :], ALU.add))
                if h:
                    dve.wait_ge(*e.at("rop", h - 1, 3))
                for u in range(3):
                    dve.wait_ge(*e.at("rap", h, u))
                    ps = unit("rap", h, u)[:, :].rearrange("p (a i) -> p a i", a=2)
                    wv = WX[:, :, 1, :] if u == 0 else WX[:, u - 1, :, :]
                    STT(ra[:, u, :].rearrange("p (a i) -> p a i", a=2), ps, 1.0 / 16, wv, ALU.mult, ALU.mult).then_inc(*e.inc("ra", h, u, frees=("rap", h, u)))
                for t in range(4):
                    o = 144 + 16 * (t % 2)
                    dve.wait_ge(*e.at("rop", h, t))
                    ps = unit("rop", h, t)
                    link(V.bn_stats(small[:, o:o + 6], ps[:, :]))
                    link(V.bn_aggr(small[:, o + 6:o + 8], small[:, o:o + 6]))
                    rstd(("ro", h, t), small[:, o + 7:o + 8], 1, 1)
                    m = TS(rt[:, t % 2, :], ps[:, :], small[:, o + 6:o + 7], small[:, o + 8:o + 9],
                           ALU.subtract, ALU.mult)
                    m.then_inc(*e.inc("rn", h, t, frees=("rop", h, t)))
                    dve.wait_ge(*e.at("rn", h, t))
                    dve.wait_ge(*e.at("rg", h, t))
                    TT(rg[:, t, :], rg[:, t, :], rt[:, t % 2, :], ALU.mult).then_inc(*e.inc("ry", h, t))
                turned_y(("r", h), 4, 512, rYh, rYl, lambda c, h=h: col(1, GN + 4 * h + c))

                def rows(t, n=1, h=h):
                    dve.wait_ge(*e.at("rwp", h, n, t))
                    dve.wait_ge(*(e.at("Y0", n, t) if h == 1 else e.at("Y", h - 1, n, t)))
                    TT(stripe(Y, n, t), unit("rwp", h, n, t)[:, :], stripe(Y, n, t), ALU.add)\
                        .then_inc(*e.inc("Y", h, n, t, frees=("rwp", h, n, t)))
                    if h == 3:
                        dve.wait_ge(*e.at("Y", h, n, t))
                        dve.wait_ge(*e.at("gb", ("r",), t // 2, 1))
                        link(TT(stripe(Y, n, t), stripe(Y, n, t), stripe(gbm, n, t // 2), ALU.mult))
                        TT(stripe(X, n, t), stripe(X, n, t), stripe(Y, n, t), ALU.add)\
                            .then_inc(*e.inc("X", ("g2", 0), t, n))

                for n in range(2):
                    if h == 3 and n == 1:
                        ahead_of_tail(until, ("rw", h, n))
                        first_squares(("g2", 0), 512)
                    else:
                        ahead(until, ("rw", h, n))
                        for t in range(4 if h else 0):
                            rows(t, n)
            rows = block_two_ffn("g2", 0, 2, 512, (0, 1), ("g1", 1), rows)
            rows = block_two_ffn("g1", 1, 0, 512, (0, 1), ("n",), rows)
            affine(("n",), 1, 1)
            norm(("n",), 512, rows)
            turned(("n",), 512, gain2, bias2(1, 1))
            for j in range(4):
                ahead(until, ("nq", j))
            for j in range(4):
                ahead(until, ("nk", j))
            for n in range(2):
                for half in range(2):
                    ahead(until, (("nv", n), half))
            diagonals(("n",), 1, 1, dgm, (0,))
            items = [(h, t) for h in range(16) for t in range(2)]
            for i in range(len(items) + 2):
                if i < len(items):
                    h, t = items[i]
                    o = 128 + 4 * (i % 4)
                    dve.wait_ge(*e.at("nsp", h, t))
                    ps = unit("nsp", h, t)
                    link(V.tensor_reduce(small[:, o:o + 1], ps[:, :], AX, ALU.max))
                    TS(small[:, o + 1:o + 2], small[:, o:o + 1], -1.0, None, ALU.mult).then_inc(*e.inc("nnm", h, t))
                if i >= 2:
                    h, t = items[i - 2]
                    o = 128 + 4 * ((i - 2) % 4)
                    dve.wait_ge(*e.at("nop", h, t))
                    TS(ny[:, t, h * 64:(h + 1) * 64], unit("nop", h, t)[:, 0:64], small[:, o + 3:o + 4], None,
                              ALU.mult).then_inc(*e.inc("ny_head", h, t, also=[("ny", t)], frees=("nop", h, t)))
                if 1 <= i <= len(items):
                    h, t = items[i - 1]
                    o = 128 + 4 * ((i - 1) % 4)
                    dve.wait_ge(*e.at("npr", h, t))
                    link(V.reciprocal(small[:, o + 3:o + 4], small[:, o + 2:o + 3]))
                    dve.wait_ge(*e.at("nptp", h, t))
                    if h:
                        dve.wait_ge(*e.at("nop", h - 1, t))
                    V.tensor_copy(npT[:, t, :], unit("nptp", h, t)[:, :]).then_inc(*e.inc("npT", h, t, frees=("nptp", h, t)))
            turned_y(("n",), 8, 256, *xT[256])

            def rows(t, n=1):
                dve.wait_ge(*e.at("nwp", n, t))
                dve.wait_ge(*e.at("gb", ("n",), 0, n))
                if n or t:
                    dve.wait_ge(*e.at("X", ("g2", 1), (t + 1) % 2, n if t else 0))
                TT(nt[:, :], unit("nwp", n, t)[:, :], stripe(gbm, n, 0), ALU.mult).then_inc(*e.inc("nt", n, t, frees=("nwp", n, t)))
                dve.wait_ge(*e.at("nt", n, t))
                TT(stripe(X, n, t), stripe(X, n, t), nt[:, :], ALU.add).then_inc(*e.inc("X", ("g2", 1), t, n))

            for half in range(2):
                ahead(until, (("nw", 0), half))
            for t in range(2):
                rows(t, 0)
            ahead(until, (("nw", 1), 0))
            first_squares(("g2", 1), 256)
            ahead_of_tail(until, (("nw", 1), 1))
            rows = block_two_ffn("g2", 1, 2, 256, (0,), ("last",), rows)
            norm(("last",), 256, rows)
            dve.wait_ge(L.sem("fg_landed"), 16)
            for t in range(2):
                for n in range(2):
                    dve.wait_ge(*e.at("xn", ("last",), t, n))
                TT(fo[:, t, :], xn[:, t, :], fg[:, :], ALU.mult).then_inc(*e.inc("out_row", t))

        @block.gpsimd
        def _(pool):
            e = Signals(L, "pool")
            minus_half = bsum[:, 8:9]

            def rstd(name, dst, src, n):
                pool.wait_ge(*e.at("ms", name))
                nc.gpsimd.tensor_tensor(dst, src, minus_half.to_broadcast([P, n]), ALU.pow).then_inc(*e.inc("rstd", name))

            def norm(name, T):
                for t in range(T // P):
                    pool.wait_ge(*e.at("ms", name, t))
                    nc.gpsimd.tensor_tensor(small[:, 8 + t:9 + t], small[:, t:t + 1], minus_half, ALU.pow)\
                        .then_inc(*e.inc("rstd", name, t))

            nc.gpsimd.memset(minus_half, -0.5).then_inc(L.sem("minus_half"), 1)
            pool.wait_ge(L.sem("minus_half"), 1)
            norm(("f1", 0), 256)
            for l in range(DEPTH):
                if l:
                    norm(("f1", l), 256)
                norm(("mx", l), 256)
                pool.wait_ge(*e.at("turn", ("mx", l), KD - 1))
                nc.gpsimd.memset(xr[:, :, 0:3], 0.0).then_inc(*e.inc("xr0", l))
                if l:
                    pool.wait_ge(*e.at("gvn", l - 1, 1))
                pool.dma_start(vgain[:, :], wide_row(w["gm_v_norm"][l], 512)).then_inc(L.sem("vgain_landed"), 16)
                pool.dma_start(ws[:, :, :], w["gm_w_s"][l].rearrange("g t s -> t g s"))\
                    .then_inc(L.sem("ws_landed"), 16)
                L.events[("ws", l)] = ("ws_landed", 16 * (l + 1))
                rstd(("gv", l), small[:, 50:52], small[:, 48:50], 2)
                rstd(("cq", l), small[:, 210:212], small[:, 208:210], 2)
                rstd(("ck", l), small[:, 214:216], small[:, 212:214], 2)
                for c in range(2):
                    rstd(("yc", l, c), small[:, 218:220], small[:, 216:218], 2)
                for t in range(2):
                    rstd(("qk", l, t), small[:, 240:256], small[:, 224:240], 16)
                norm(("f2", l), 256)
            norm(("g1", 0), 512)
            norm(("r",), 512)
            pool.dma_start(rcst[:, :], consts["rcst"]).then_inc(L.sem("rcst_landed"), 16)
            for h in range(4):
                for t in range(4):
                    o = 144 + 16 * (t % 2)
                    rstd(("ro", h, t), small[:, o + 8:o + 9], small[:, o + 7:o + 8], 1)
            norm(("g2", 0), 512)
            norm(("g1", 1), 512)
            norm(("n",), 512)
            rpb = w["nat_rpb_2"]
            for q4 in range(4):
                if q4 >= 2:
                    pool.wait_ge(*e.at("nbias_used", q4 - 2))
                else:
                    pool.wait_ge(*e.at("xT", ("n",), KD - 1))
                b = nbias[q4 % 2]
                for t in range(2):
                    for r in range(2):
                        for h in range(4):
                            off = rpb.offset + (4 * q4 + h) * 465 + (7 - 2 * t - r) * 31 + 15 - 63
                            pool.dma_start(b[64 * r:64 * r + 64, t, h, :].rearrange("p (a c) -> p a c", a=4),
                                           bass.AP(rpb.tensor, off, [[1, 64], [31, 4], [1, 64]]))\
                                .then_inc(L.sem(f"bias{q4 % 2}_landed"), 16)
                pool.wait_ge(L.sem(f"bias{q4 % 2}_landed"), 256 * (q4 // 2 + 1))
                mask = cst[:, C_NAT:C_NAT + 64].unsqueeze(1).to_broadcast([P, 32, 64])
                bv = b[:, :, :, :].rearrange("p t h (a c) -> p (t h a) c", c=64)
                nc.gpsimd.tensor_tensor(bv, bv, mask, ALU.add).then_inc(*e.inc("nbias", q4))
            norm(("g2", 1), 256)
            pool.dma_start(fg[:, :], wide_row(w["final_norm_g_2"], D)).then_inc(L.sem("fg_landed"), 16)
            norm(("last",), 256)
    return L


_INS = ["x", "positions", "ffn1_norm", "ffn1_w_in", "ffn1_w_out", "mix_norm", "w_in", "gm_v_norm", "gm_w_s", "gm_b_s",
        "mla_q_norm", "mla_kv_norm", "mla_w_uq", "mla_w_ukv", "mla_q_gain", "mla_k_gain", "ssd_conv_w",
        "ssd_conv_b", "ssd_dt_bias", "ssd_a_log", "ssd_d", "ssd_norm", "w_branch", "w_out", "ffn2_norm", "ffn2_w_in",
        "ffn2_w_out", "c_2", "ctx_2", "c_ctx_2", "w_mod_2", "b_mod_2", "norm_g_2", "ffn_w_in_2", "ffn_w_out_2",
        "ret_w_in_2", "ret_w_out_2", "ret_gn_g_2", "ret_decay_f_2", "ret_decay_b_2", "nat_w_qkv_2", "nat_w_o_2",
        "nat_rpb_2", "final_norm_g_2"]


def constants():
    import numpy as np
    i = np.arange(P)
    cst = np.zeros((P, C_END), np.float32)
    cst[:, C_IDENT:C_IDENT + P] = np.eye(P)
    cst[:, C_U:C_U + P] = i[:, None] <= i[None, :]
    cst[:, C_CAUSAL:C_CAUSAL + P] = np.where(i[None, :] <= i[:, None], 0.0, NEG)
    cst[:, C_ONES:C_ONES + P] = 1.0
    c = 63 - i % 64
    cst[:, C_FLIP:C_FLIP + P] = (i[None, :] == 64 * (i[:, None] // 64) + c[:, None])
    first = np.clip(c - 8, 0, 48)
    k = np.arange(64)
    inside = (k[None, :] >= first[:, None]) & (k[None, :] < first[:, None] + 16)
    cst[:, C_NAT:C_NAT + 64] = np.where(inside, 0.0, NEG)
    theta = np.float32(10000.0)
    cst[:, C_FREQ:C_FREQ + 16] = 1.0 / theta ** (np.arange(0, 32, 2, dtype=np.float32) / np.float32(32))
    rcst = np.zeros((P, R_END), np.float32)
    inv = theta ** (-np.arange(0, 256, 2, dtype=np.float32) / np.float32(256))
    ang = (np.arange(256, dtype=np.float32)[None, :] * inv[:, None]).astype(np.float32)
    rcst[:, R_COS:R_COS + 256] = np.cos(ang)
    rcst[:, R_SIN:R_SIN + 256] = np.sin(ang)
    for jt in range(2):
        o = R_DIST + 256 * jt
        rcst[:, o:o + 256] = np.arange(256)[None, :] - (i[:, None] + P * jt)
    return {"cst": cst, "rcst": rcst}


def kernel(**inputs):
    import numpy as _np
    import concourse.bacc as _bacc
    from concourse import mybir as _mybir
    from concourse.bass_utils import run_bass_kernel_spmd as _run

    tables = constants()
    arrays = {f"in_{name}_dram": _np.ascontiguousarray(inputs[name]) for name in _INS}
    arrays.update({f"const_{name}_dram": a for name, a in tables.items()})

    def written(known):
        nc = _bacc.Bacc("TRN2", target_bir_lowering=False, num_devices=1)

        def dram(name):
            a = arrays[name]
            return nc.dram_tensor(name, a.shape, _mybir.dt.from_np(a.dtype), kind="ExternalInput").ap()

        w = {name: dram(f"in_{name}_dram") for name in _INS}
        consts = {name: dram(f"const_{name}_dram") for name in tables}
        out = nc.dram_tensor("out_dram", (1, SEQ, D), F32, kind="ExternalOutput").ap()
        return nc, build(nc, w, consts, out, known)

    _, ledger = written(None)
    nc, _ = written(ledger)
    r = _run(nc, [arrays], core_ids=[0])
    return r.results[0]["out_dram"]
```
